# Optimizing a Trainium2 kernel written in Bass

```python
import jax, jax.numpy as jnp
from jax import lax
import numpy as np

D_MODEL = 1024
BATCH = 1
SEQ = 1024
DEPTH = 1
DEC_BATCH = 8
DEC_SEQ = 8
PAST_LEN = 8192
PAGE_SIZE = 128

D_MIX = D_MODEL
D_RG = D_MIX // 2
D_SG = D_MIX - D_RG
RG_HEADS = 8
RG_HEAD_DIM = D_RG // RG_HEADS
SG_HEADS = 8
SG_HEAD_DIM = D_SG // SG_HEADS
CHUNK = 128
CONV_W = 4
LRU_C = 8.0
D_FF = 4 * D_MODEL
D_IN = 2 * D_RG + 2 * D_SG
EPS = 1e-6

kernel_name = 'hymba_rglru_gmlp_decoder_step'

def rms_norm(x, g):
    xf = x.astype(jnp.float32)
    y = xf * lax.rsqrt(jnp.mean(xf * xf, axis=-1, keepdims=True) + EPS)
    return (y * g.astype(jnp.float32)).astype(x.dtype)

def layer_norm(x, g, b):
    xf = x.astype(jnp.float32)
    mu = jnp.mean(xf, axis=-1, keepdims=True)
    var = jnp.mean(jnp.square(xf - mu), axis=-1, keepdims=True)
    y = (xf - mu) * lax.rsqrt(var + EPS)
    return (y * g.astype(jnp.float32) + b.astype(jnp.float32)).astype(x.dtype)

def causal_conv(xb, buf, w, b):
    t_len = xb.shape[1]
    xp = jnp.concatenate([buf.astype(xb.dtype), xb], axis=1)
    out = b
    for k in range(CONV_W):
        out = out + xp[:, k:k + t_len] * w[k]
    return out, xp[:, -(CONV_W - 1):]

def block_diag(x, w, b):
    bsz, t_len, _ = x.shape
    xh = x.reshape(bsz, t_len, RG_HEADS, RG_HEAD_DIM)
    y = jnp.einsum('bthi,hij->bthj', xh, w) + b
    return y.reshape(bsz, t_len, D_RG)

def rg_lru(x, h0, w_ra, b_ra, w_ri, b_ri, lru_l, pos0):
    t_len = x.shape[1]
    r = jax.nn.sigmoid(block_diag(x, w_ra, b_ra).astype(jnp.float32))
    i = jax.nn.sigmoid(block_diag(x, w_ri, b_ri).astype(jnp.float32))
    log_a = LRU_C * r * jax.nn.log_sigmoid(lru_l.astype(jnp.float32))
    a = jnp.exp(log_a)
    mult = jnp.sqrt(-jnp.expm1(2.0 * log_a))
    reset = (pos0 + jnp.arange(t_len)) == 0
    mult = jnp.where(reset[None, :, None], 1.0, mult)
    bterm = mult * i * x.astype(jnp.float32)
    bterm = bterm.at[:, 0].add(a[:, 0] * h0.astype(jnp.float32))

    def combine(lhs, rhs):
        a1, b1 = lhs
        a2, b2 = rhs
        return a1 * a2, a2 * b1 + b2

    _, h = lax.associative_scan(combine, (a, bterm), axis=1)
    return h.astype(x.dtype), h[:, -1].astype(x.dtype)

def spatial_gate(u, v, w_s, b_s):
    bsz, t_len, _ = v.shape
    n_chunk = -(-t_len // CHUNK)
    pad = n_chunk * CHUNK - t_len
    vp = jnp.pad(v, ((0, 0), (0, pad), (0, 0))).reshape(bsz, n_chunk, CHUNK, SG_HEADS, SG_HEAD_DIM)
    mask = jnp.tril(jnp.ones((CHUNK, CHUNK), dtype=bool))
    ws = jnp.where(mask[None], w_s, 0)
    mixed = jnp.einsum('hts,bcshd->bcthd', ws, vp) + b_s.T[None, None, :, :, None]
    mixed = mixed.reshape(bsz, n_chunk * CHUNK, D_SG)[:, :t_len]
    return u * mixed

def trunk(x, c, conv_state, lru_state, pos0,
          w_ada, b_ada, g_mix, g_ffn, w_in, conv_w, conv_b, w_ra, b_ra, w_ri, b_ri, lru_l,
          ln_v_g, ln_v_b, w_s, b_s, g_rg, g_sg, w_out, w_ff1, w_ff2, g_final):
    t_len = x.shape[1]
    v_start = ((t_len - 1) // CHUNK) * CHUNK
    convs, lrus, vrows = [], [], []
    for l in range(DEPTH):
        ada = jax.nn.silu(c) @ w_ada[l] + b_ada[l]
        sh_m, sc_m, gt_m, sh_f, sc_f, gt_f = jnp.split(ada[:, None, :], 6, axis=-1)
        hm = rms_norm(x, g_mix[l]) * (1.0 + sc_m) + sh_m
        proj = hm @ w_in[l]
        xr, yg, u, v = jnp.split(proj, [D_RG, 2 * D_RG, 2 * D_RG + D_SG], axis=-1)
        xc, new_buf = causal_conv(xr, conv_state[l], conv_w[l], conv_b[l])
        hr, h_last = rg_lru(xc, lru_state[l], w_ra[l], b_ra[l], w_ri[l], b_ri[l], lru_l[l], pos0)
        rg_out = hr * jax.nn.gelu(yg)
        sg_out = spatial_gate(u, layer_norm(v, ln_v_g[l], ln_v_b[l]), w_s[l], b_s[l])
        merged = jnp.concatenate([rms_norm(rg_out, g_rg[l]), rms_norm(sg_out, g_sg[l])], axis=-1)
        x = x + gt_m * (merged @ w_out[l])
        hf = rms_norm(x, g_ffn[l]) * (1.0 + sc_f) + sh_f
        x = x + gt_f * (jnp.square(jax.nn.relu(hf @ w_ff1[l])) @ w_ff2[l])
        convs.append(new_buf)
        lrus.append(h_last)
        vrows.append(v[:, v_start:])
    y = rms_norm(x, g_final)
    return y, jnp.stack(convs), jnp.stack(lrus), jnp.stack(vrows)

def setup_inputs(seed: int = 0) -> dict:
    key = jax.random.key(seed)
    ks = jax.random.split(key, 32)
    f32 = jnp.float32

    def nrm(k, shape, scale):
        return jax.random.normal(k, shape, f32) * scale

    p_lru = jax.random.uniform(ks[12], (DEPTH, D_RG), f32, 0.9, 0.999)
    return {
        'x_prompt': nrm(ks[0], (BATCH, SEQ, D_MODEL), 1.0),
        'x_sample': nrm(ks[1], (DEC_BATCH, DEC_SEQ, D_MODEL), 1.0),
        'c_prompt': nrm(ks[2], (BATCH, D_MODEL), 1.0),
        'c_sample': nrm(ks[3], (DEC_BATCH, D_MODEL), 1.0),
        'state_conv': nrm(ks[4], (DEPTH, DEC_BATCH, CONV_W - 1, D_RG), 1.0),
        'state_rglru': nrm(ks[5], (DEPTH, DEC_BATCH, D_RG), 0.5),
        'w_ada': nrm(ks[6], (DEPTH, D_MODEL, 6 * D_MODEL), 0.5 * D_MODEL ** -0.5),
        'b_ada': nrm(ks[7], (DEPTH, 6 * D_MODEL), 0.1),
        'g_mix': 1.0 + nrm(ks[8], (DEPTH, D_MODEL), 0.1),
        'g_ffn': 1.0 + nrm(ks[9], (DEPTH, D_MODEL), 0.1),
        'w_in': nrm(ks[10], (DEPTH, D_MODEL, D_IN), D_MODEL ** -0.5),
        'conv_w': nrm(ks[11], (DEPTH, CONV_W, D_RG), CONV_W ** -0.5),
        'conv_b': nrm(ks[13], (DEPTH, D_RG), 0.02),
        'w_ra': nrm(ks[14], (DEPTH, RG_HEADS, RG_HEAD_DIM, RG_HEAD_DIM), RG_HEAD_DIM ** -0.5),
        'b_ra': nrm(ks[15], (DEPTH, RG_HEADS, RG_HEAD_DIM), 0.02),
        'w_ri': nrm(ks[16], (DEPTH, RG_HEADS, RG_HEAD_DIM, RG_HEAD_DIM), RG_HEAD_DIM ** -0.5),
        'b_ri': nrm(ks[17], (DEPTH, RG_HEADS, RG_HEAD_DIM), 0.02),
        'lru_l': jnp.log(p_lru) - jnp.log1p(-p_lru),
        'ln_v_g': 1.0 + nrm(ks[18], (DEPTH, D_SG), 0.1),
        'ln_v_b': nrm(ks[19], (DEPTH, D_SG), 0.02),
        'w_s': nrm(ks[20], (DEPTH, SG_HEADS, CHUNK, CHUNK), 0.5 * CHUNK ** -0.5),
        'b_s': 1.0 + nrm(ks[21], (DEPTH, SG_HEADS, CHUNK), 0.1),
        'g_rg': 1.0 + nrm(ks[22], (DEPTH, D_RG), 0.1),
        'g_sg': 1.0 + nrm(ks[23], (DEPTH, D_SG), 0.1),
        'w_out': nrm(ks[24], (DEPTH, D_MIX, D_MODEL), D_MIX ** -0.5),
        'w_ff1': nrm(ks[25], (DEPTH, D_MODEL, D_FF), D_MODEL ** -0.5),
        'w_ff2': nrm(ks[26], (DEPTH, D_FF, D_MODEL), D_FF ** -0.5),
        'g_final': 1.0 + nrm(ks[27], (D_MODEL,), 0.1),
    }

def reference(x_prompt, x_sample, c_prompt, c_sample, state_conv, state_rglru,
              w_ada, b_ada, g_mix, g_ffn, w_in, conv_w, conv_b, w_ra, b_ra, w_ri, b_ri, lru_l,
              ln_v_g, ln_v_b, w_s, b_s, g_rg, g_sg, w_out, w_ff1, w_ff2, g_final):
    conv0 = jnp.zeros((DEPTH, x_prompt.shape[0], CONV_W - 1, D_RG), x_prompt.dtype)
    lru0 = jnp.zeros((DEPTH, x_prompt.shape[0], D_RG), x_prompt.dtype)
    y_prompt, conv_p, lru_p, vrows_p = trunk(
        x_prompt, c_prompt, conv0, lru0, 0,
        w_ada, b_ada, g_mix, g_ffn, w_in, conv_w, conv_b, w_ra, b_ra, w_ri, b_ri, lru_l,
        ln_v_g, ln_v_b, w_s, b_s, g_rg, g_sg, w_out, w_ff1, w_ff2, g_final)
    y_sample, conv_s, lru_s, vrows_s = trunk(
        x_sample, c_sample, state_conv, state_rglru, PAST_LEN,
        w_ada, b_ada, g_mix, g_ffn, w_in, conv_w, conv_b, w_ra, b_ra, w_ri, b_ri, lru_l,
        ln_v_g, ln_v_b, w_s, b_s, g_rg, g_sg, w_out, w_ff1, w_ff2, g_final)
    return (y_prompt, y_sample, conv_p, lru_p, vrows_p, conv_s, lru_s, vrows_s)


_drawn_inputs = setup_inputs


def setup_inputs(seed=0):
    import zlib

    import numpy as np

    out = dict(_drawn_inputs(seed))
    spreads = {}
    factors = {'b_ra': 8.0, 'b_ri': 8.0, 'ln_v_g': 7.918, 'ln_v_b': 8.0}
    for name, (base, spread) in spreads.items():
        noise = np.random.default_rng([zlib.crc32(name.encode()), seed]).standard_normal(out[name].shape)
        drawn = base * np.exp(spread * noise) if base else spread * noise
        out[name] = __import__('jax').numpy.asarray(drawn.astype(out[name].dtype))
    for name, factor in factors.items():
        out[name] = (out[name] * factor).astype(out[name].dtype)
    return out
```

```python
from contextlib import ExitStack

import concourse.bass as bass
from concourse import mybir

F32 = mybir.dt.float32
F32R = mybir.dt.float32r
ALU = mybir.AluOpType
ACT = mybir.ActivationFunctionType

P = 128
D = 1024
T_PROMPT = 1024
NB, TB = 8, 8
T_SAMPLE = NB * TB
T = T_PROMPT + T_SAMPLE
KD = D // P
D_RG = D_SG = D // 2
JB = D_RG // P
D_FF = 4 * D
D_IN = 2 * D_RG + 2 * D_SG
CONV_W = 4
HALO = CONV_W - 1
HEADS, HD = 8, 64
CHUNK = 128
EPS = 1e-6
LRU_C = 8.0
NT = (T + P - 1) // P
NC = 1 + NB
N_ADA = 6 * KD
ADA_EARLY = 2 * KD

GROUPS = [(0, 384), (384, 384), (768, 320)]
TILES_OF = [[0, 1, 2], [3, 4, 5], [6, 7, 8]]
PROMPT_G2 = T_PROMPT - GROUPS[2][0]

SEG = HALO + TB
ROW_W = HALO + T_PROMPT + NB * SEG
SCAN_W = ROW_W - HALO
WIDE = 1120
SCAN_GROUPS = [(0, 384), (384, 384), (768, SCAN_W - 768)]

R_STATE, R_H0, R_CW, R_CB, R_BRA, R_BRI, R_LRU, R_LNG, R_LNB, R_GRG, R_GSG, R512 = 0, 24, 32, 36, 37, 38, 39, 40, 41, 42, 43, 44
R_GMIX, R_GFFN, R_C, R1024 = 0, 1, 2, 2 + NC
TAILS = HALO + NB * HALO + 1 + NB

U_V, U_RG, U_U, U_OUT_A, U_OUT_B = 0, 4, 12, 16, 24
U_FF = 32
FF_BLOCKS = D_FF // 256

N_ROW_LOADS = 16
LAM_STEPS = 18
HF_AT = [0, 0, 2, 5, 8, 10, 12, 14, 16]
NORM_ITEMS = 3 * KD + 1


def plan_banks():
    turns, use = [0] * 8, {}

    def take(name, bank):
        use[name] = (bank, turns[bank])
        turns[bank] += 1

    take("rows512", 7)
    take("rows1024", 6)
    take("ws0", 7)
    take("ws1", 6)
    take("wsmall", 7)
    take("rowsum", 6)
    for t in range(NT):
        for h in range(2):
            take(("x", t, h), (2 * t + h) % 6)
    take("ada1", 6)
    for g, b in enumerate((7, 6, 7)):
        take(("bcx", g), b)
    for j in range(JB):
        for g in range(3):
            take(("v", j, g), 3 * (j % 2) + g)
    take("ada2", 6)
    for j in range(JB):
        for name, s in (("xr", 0), ("yg", 1)):
            for g in range(3):
                take((name, j, g), 3 * s + g)
        if j == JB - 1:
            for jj in range(JB):
                for g in range(3):
                    take(("mix", jj, g), 3 * (jj % 2) + g)
        for name, s in (("gr", 0), ("gi", 1)):
            for g in range(3):
                take((name, j, g), 3 * s + g)
    for t in range(NT):
        take(("vt", t), 7)
    for j in range(JB):
        for g in range(3):
            take(("u", j, g), 3 * (j % 2) + g)
    take("ss_rg", 7)
    take(("bcrg", 0), 6)
    take(("bcrg", 1), 7)
    take(("bcrg", 2), 6)
    for g in range(3):
        take(("ss_sg", g), 7)
        take(("bcsg", g), 6)
    take("tails", 7)
    for o in range(KD):
        for g in range(2):
            take(("out", o, g), 3 * (o % 2) + g)
    for o in range(KD):
        take(("out", o, 2), 3 * (o % 2) + 2)
    for g in range(3):
        take(("ss_x1", g), 7)
        take(("bcx1", g), 6)
    assert len(set(turns[:6])) == 1
    ff = turns[0]
    for b in range(6):
        turns[b] += 5 * FF_BLOCKS
    for g in range(3):
        take(("ss_y", g), 7)
    for t in range(NT):
        for h in range(2):
            take(("y", t, h), (2 * t + h) % 6)
    return use, ff


USE, FF_TURN = plan_banks()


def ff1_turn(b):
    return FF_TURN if isinstance(b, int) and b == 0 else 5 * b + (FF_TURN - 4)


def ff2_turn(b):
    last = isinstance(b, int) and b == FF_BLOCKS - 1
    return 5 * b + (FF_TURN + 1 if last else FF_TURN + 2)


def ff1_half(b):
    return U_FF // 2 if isinstance(b, int) and b == 0 else 2 * b + (U_FF // 2 - 1)


def ff2_half(b):
    last = isinstance(b, int) and b == FF_BLOCKS - 1
    return 2 * b + (U_FF // 2 + 1 if last else U_FF // 2 + 2)


def build(nc, a, out):
    with ExitStack() as ctx:
        sem = lambda name: ctx.enter_context(nc.semaphore(name))
        psum = [ctx.enter_context(nc.psum_tensor(f"bank{b}", [P, 512], F32)) for b in range(8)]

        base = (nc.sbuf_base + 31) // 32 * 32

        def at(name, shape, offset, dt=F32):
            return nc.alloc_sbuf_tensor_at(name, [P, *shape], dt, offset=offset)

        off_x = base
        off_act = off_x + KD * T * 4
        off_w = off_act + 2 * KD * T * 4
        off_v = off_w + 6 * 4096
        off_rg = off_v + JB * NT * P * 4
        off_t = off_rg + JB * T * 4
        off_c = off_t + 5 * WIDE * 4
        tmp = lambda n: off_t + n * WIDE * 4

        xT = at("xT", [KD, T], off_x)
        act_hi = at("act_hi", [KD, T], off_act, F32R)
        act_lo = at("act_lo", [KD, T], off_act + KD * T * 4, F32R)
        w_raw = at("w_raw", [2, 1024], off_w)
        w_hi = at("w_hi", [2, 1024], off_w + 2 * 4096, F32R)
        w_lo = at("w_lo", [2, 1024], off_w + 4 * 4096, F32R)
        V = at("V", [JB, NT * P], off_v)
        RG = at("RG", [JB, T], off_rg)
        row = at("row", [WIDE], tmp(0))
        xc = at("xc", [WIDE], tmp(1))
        rr = at("rr", [WIDE], tmp(2))
        ig = at("ig", [WIDE], tmp(3))
        aa = at("aa", [WIDE], tmp(4))
        sq_rg = at("sq_rg", [2, WIDE], tmp(0))
        ss_rg = at("ss_rg", [T], tmp(2))
        ss_sg = at("ss_sg", [T], tmp(3))
        sq_g = at("sq_g", [2, 384], tmp(4))
        xin = at("xin", [NT, D], off_v)
        ada_w = at("ada_w", [KD, ADA_EARLY * P], off_act)
        smp0 = at("smp0", [KD, T_SAMPLE], tmp(0) + 2048)
        ws_raw = at("ws_raw", [HEADS, CHUNK], tmp(1))
        own = at("own", [NB], tmp(1) + 4096)
        rows1024 = at("rows1024", [D], tmp(2))
        eye8 = at("eye8", [NB, TB], tmp(2) + 4096)
        rows512 = at("rows512", [D_RG], tmp(3))
        bada_rows = at("bada_rows", [P], tmp(3) + 2048)
        ada_e = at("ada_e", [ADA_EARLY, NC], tmp(3) + 2560)
        gain_m = at("gain_m", [KD, NC], tmp(3) + 3136)
        ones64 = at("ones64", [HD], tmp(3) + 3424)
        tmp0 = at("tmp0", [2, 384], tmp(4))
        h_hi = at("h_hi", [4, T], off_v, F32R)
        h_lo = at("h_lo", [4, T], off_v + 4 * T * 4, F32R)
        relu = at("relu", [2, 384], tmp(0))
        sqr = at("sqr", [2, 384], tmp(1))
        ss_x = at("ss_x", [T], tmp(2))
        yout = at("yout", [NT, D], off_act)

        pos = [off_c]

        def const(name, shape, dt=F32):
            n = 4
            for s in shape:
                n *= s
            t = at(name, shape, pos[0], dt)
            pos[0] += (n + 31) // 32 * 32
            return t

        off_ws = pos[0]
        wsT = const("wsT", [HEADS, CHUNK])
        off_w64 = pos[0]
        ws64 = const("ws64", [HEADS, NB, TB])
        off_bs = pos[0]
        mix_b = const("mix_b", [JB, CHUNK])
        off_gate = pos[0]
        gate_w = const("gate_w", [2, JB, P])
        ident = const("ident", [P])
        ada_late = const("ada_late", [N_ADA - ADA_EARLY, NC])
        gain_f = const("gain_f", [KD, NC])
        ada_ring = const("ada_ring", [2, KD, P])
        r5 = const("r5", [JB, R512])
        r10 = const("r10", [KD, R1024])
        bada = const("bada", [N_ADA])
        silu = const("silu", [KD, NC])
        tails = const("tails", [JB, TAILS])
        bn = const("bn", [NT, 6])
        mv = const("mv", [NT, 2])
        v_std = const("v_std", [NT])
        ssq = const("ssq", [NT])
        std = const("std", [NT])
        rstd = const("rstd", [NT])
        ones = const("ones", [1])
        eps = const("eps", [1])
        lam = const("lam", [8, JB])
        decay = const("decay", [JB])
        decay_n = const("decay_n", [JB])
        assert pos[0] <= nc.sbuf_usable_end, (pos[0], nc.sbuf_usable_end)
        tmp1 = at("tmp1", [2, 384], off_ws)
        smp1 = at("smp1", [KD, T_SAMPLE], off_w64)
        smp_acc = at("smp_acc", [KD, T_SAMPLE], off_bs)
        g_fin = at("g_fin", [D], off_gate)
        smp_t = at("smp_t", [T_SAMPLE], off_ws + 3072)
        tails_out = at("tails_out", [D_RG], off_w64)

        full = [sem(f"bank{b}_full") for b in range(8)]
        free = [sem(f"bank{b}_free") for b in range(8)]
        raw_in = [sem(f"raw_in{s}") for s in range(2)]
        hi_done = [sem(f"hi_done{s}") for s in range(2)]
        lo_done = [sem(f"lo_done{s}") for s in range(2)]
        ada_in = [sem(f"ada_in{s}") for s in range(2)]
        ada_used = sem("ada_used")
        x_in = [sem(f"x_in{t}") for t in range(NT)]
        ada_w_in = [sem(f"ada_w_in{k}") for k in range(KD)]
        rows_in = sem("rows_in")
        ws_in = sem("ws_in")
        bs_in = sem("bs_in")
        gates_in = sem("gates_in")
        gfin_in = sem("gfin_in")
        stored = sem("stored")
        tails_stored = sem("tails_stored")
        vrows_out = sem("vrows_out")
        pool_set = sem("pool_set")
        x_sq = sem("x_sq")
        norm_tmp = sem("norm_tmp")
        norm_hi = sem("norm_hi")
        act_ready = sem("act_ready")
        smp_step = sem("smp_step")
        eye_ready = sem("eye_ready")
        silu_sig = sem("silu_sig")
        silu_ready = sem("silu_ready")
        lam_exp = sem("lam_exp")
        lam_step = sem("lam_step")
        ada_ready = sem("ada_ready")
        mixb_ready = sem("mixb_ready")
        std_done = sem("std_done")
        rstd_done = sem("rstd_done")
        halo_done = sem("halo_done")
        tap_done = sem("tap_done")
        row_read = sem("row_read")
        ix_done = sem("ix_done")
        decay_done = sem("decay_done")
        act_chain = sem("act_chain")
        q_done = sem("q_done")
        root_done = sem("root_done")
        term_done = sem("term_done")
        scan_done = sem("scan_done")
        rg_done = sem("rg_done")
        h_tail = sem("h_tail")
        v_stat = sem("v_stat")
        v_std_done = sem("v_std_done")
        v_norm = sem("v_norm")
        mix_done = sem("mix_done")
        rgsq = sem("rgsq")
        rgsum = sem("rgsum")
        sgsq = sem("sgsq")
        sgsum = sem("sgsum")
        rg_norm = sem("rg_norm")
        mrg_hi = sem("mrg_hi")
        mrg_ready = sem("mrg_ready")
        sg_norm = sem("sg_norm")
        msg_hi = sem("msg_hi")
        msg_ready = sem("msg_ready")
        x1_smp = sem("x1_smp")
        x1sq = sem("x1sq")
        x1sum = sem("x1sum")
        relu_done = sem("relu_done")
        hhi_done = sem("hhi_done")
        h_ready = sem("h_ready")
        smp_zero = sem("smp_zero")
        y_smp = sem("y_smp")
        ysq = sem("ysq")
        ysum = sem("ysum")

        def cols(t, g):
            c, n = GROUPS[g]
            return t[:, c:c + n] if len(t.shape) == 2 else t[:, :, c:c + n]

        def blk(t, k, g, n=None):
            c, m = GROUPS[g]
            return t[:, k, c:c + (m if n is None else n)]

        def smp(t, start, n):
            at0 = min(start, seg0)
            return t[:, at0:at0 + NB * SEG].rearrange("p (b x) -> p b x", x=SEG)[:, :, start - at0:start - at0 + n]

        def by_sample(t):
            return t.rearrange("p (b t) -> p b t", t=TB)

        f32 = lambda view: view.bitcast(F32)
        row_tok = HALO
        seg0 = HALO + T_PROMPT
        tile_rows = lambda t: min(P, T - t * P)

        def claim(pe, name):
            bank, turn = USE[name]
            if turn > 0:
                pe.wait_ge(free[bank], turn)
            return psum[bank]

        def when_full(eng, name):
            bank, turn = USE[name]
            eng.wait_ge(full[bank], turn + 1)
            return psum[bank]

        def when_read(eng, name):
            bank, turn = USE[name]
            eng.wait_ge(free[bank], turn + 1)

        full_of = lambda name: full[USE[name][0]]
        free_of = lambda name: free[USE[name][0]]

        x_p = a["x_prompt"].rearrange("a t d -> (a t) d")
        x_s = a["x_sample"].rearrange("b t d -> (b t) d")
        w_in_v = a["w_in"][0].rearrange("(k p) n -> p k n", p=P)
        w_out_v = a["w_out"][0].rearrange("(k p) n -> p k n", p=P)
        w_ff1_v = a["w_ff1"][0].rearrange("(k p) n -> p k n", p=P)
        w_ff2_v = a["w_ff2"][0].rearrange("(k p) n -> p k n", p=P)
        w_ada_v = a["w_ada"][0].rearrange("(k p) n -> p k n", p=P)

        unit_cols = [2 * D_RG + D_SG + P * j for j in range(JB)]
        for j in range(JB):
            unit_cols += [P * j, D_RG + P * j]
        unit_cols += [2 * D_RG + P * j for j in range(JB)]

        block = ctx.enter_context(nc.Block())

        @block.sync
        def _(sp):
            for t in range(NT):
                src = x_p[P * t:P * t + P] if t < NT - 1 else x_s
                sp.dma_start(xin[0:tile_rows(t), t, :], src).then_inc(x_in[t], 16)

            def unit(s, half, src, shape_k):
                if not (isinstance(half, int) and half == 0):
                    sp.wait_ge(lo_done[s], half)
                sp.dma_start(w_raw[:, s, :].rearrange("p (k n) -> p k n", k=shape_k), src).then_inc(raw_in[s], 16)

            def in_unit(n):
                unit(n % 2, n // 2, w_in_v[:, :, unit_cols[n]:unit_cols[n] + P], KD)

            def ada_unit(m):
                if m >= 2:
                    sp.wait_ge(ada_used, m - 1)
                c = (ADA_EARLY + m) * P
                sp.dma_start(ada_ring[:, m % 2], w_ada_v[:, :, c:c + P]).then_inc(ada_in[m % 2], 16)

            n_late = N_ADA - ADA_EARLY
            in_unit(0)
            in_unit(1)
            ada_unit(0)
            ada_unit(1)
            in_unit(2)
            in_unit(3)
            for n in range(U_OUT_A - 4):
                for m in range(3 * n + 2, min(3 * n + 5, n_late)):
                    ada_unit(m)
                in_unit(n + 4)
            when_read(sp, ("gi", JB - 1, 2))
            sp.dma_start(g_fin[:], a["g_final"].partition_broadcast(P)).then_inc(gfin_in, 16)
            for n in range(U_OUT_A, U_FF):
                o = (n - U_OUT_A) % KD
                unit(n % 2, n // 2, w_out_v[:, :, P * o:P * o + P], KD)

            def ff1_units(b):
                for c in range(2):
                    unit(c, ff1_half(b), w_ff1_v[:, :, bass.ds(256 * b + P * c, P)], KD)

            def ff2_units(b):
                for h in range(2):
                    unit(h, ff2_half(b), w_ff2_v[:, bass.ds(2 * b, 2), 512 * h:512 * h + 512], 2)

            ff1_units(0)
            with sp.Fori(0, FF_BLOCKS - 1) as b:
                ff1_units(b + 1)
                ff2_units(b)
            ff2_units(FF_BLOCKS - 1)
            yp, ys = out[0].rearrange("a t d -> (a t) d"), out[1].rearrange("b t d -> (b t) d")
            for t in range(NT):
                when_read(sp, ("y", t, 1))
                dst = yp[P * t:P * t + P] if t < NT - 1 else ys
                sp.dma_start(dst, yout[0:tile_rows(t), t, :]).then_inc(stored, 16)
            sp.wait_ge(stored, 16 * NT)
            sp.wait_ge(tails_stored, 64)

        @block.gpsimd
        def _(pool):
            g = nc.gpsimd
            g.memset(gate_w[:], 0.0).then_inc(pool_set, 1)
            g.memset(ident[:], 0.0).then_inc(pool_set, 1)
            g.memset(ones[:], 1.0).then_inc(pool_set, 1)
            g.memset(ones64[:], 1.0).then_inc(pool_set, 1)
            g.memset(eps[:], EPS).then_inc(pool_set, 1)
            g.memset(own[0:64], 1.0).then_inc(pool_set, 1)
            pool.wait_ge(pool_set, 6)
            g.affine_select(out=ident[:], in_=ident[:], compare_op=ALU.not_equal, fill=1.0, base=0,
                            pattern=[[-1, P]], channel_multiplier=1).then_inc(pool_set, 1)
            g.affine_select(out=own[0:64], in_=own[0:64], compare_op=ALU.is_ge, fill=0.0, base=0,
                            pattern=[[-TB, NB]], channel_multiplier=1).then_inc(pool_set, 1)
            pool.wait_ge(pool_set, 8)
            g.affine_select(out=own[0:64], in_=own[0:64], compare_op=ALU.is_ge, fill=0.0, base=TB - 1,
                            pattern=[[TB, NB]], channel_multiplier=-1).then_inc(pool_set, 1)
            pool.wait_ge(ws_in, 16)
            g.affine_select(out=ws_raw[:], in_=ws_raw[:], compare_op=ALU.is_ge, fill=0.0, base=0,
                            pattern=[[0, HEADS], [-1, CHUNK]], channel_multiplier=1).then_inc(pool_set, 1)

            for j in range(JB):
                if j == 0:
                    pool.wait_ge(act_ready, NORM_ITEMS)
                    when_read(pool, "rows512")
                else:
                    pool.wait_ge(term_done, j)
                g.memset(row[:, 0:HALO], 0.0).then_inc(halo_done, 1)
                g.tensor_copy(smp(row, seg0, HALO),
                              r5[:, j, R_STATE:R_STATE + NB * HALO].rearrange("p (b x) -> p b x", x=HALO)
                              ).then_inc(halo_done, 1)
                when_read(pool, ("xr", j, 2))
                g.tensor_copy(tails[:, j, 0:HALO], row[:, T_PROMPT:T_PROMPT + HALO])
                g.tensor_copy(tails[:, j, HALO:HALO + NB * HALO].rearrange("p (b x) -> p b x", x=HALO),
                              smp(row, seg0 + TB, HALO)).then_inc(row_read, 1)
                when_read(pool, ("gi", j, 2))
                g.tensor_tensor(ig[:, 0:SCAN_W], ig[:, 0:SCAN_W], xc[:, 0:SCAN_W], ALU.mult).then_inc(ix_done, 1)
                if j == 2:
                    when_read(pool, ("vt", NT - 1))
                    pool.dma_start(out[4][0, 0].rearrange("t (j d) -> t j d", j=JB), V[:, :, P * 7:P * 8]).then_inc(vrows_out, 16)
                    pool.dma_start(out[7][0].rearrange("b t (j d) -> (b t) j d", j=JB), V[0:64, :, P * 8:P * 9]
                                   ).then_inc(vrows_out, 16)
                pool.wait_ge(scan_done, 3 * j + 3)
                c = HALO + NB * HALO
                g.tensor_copy(tails[:, j, c:c + 1], rr[:, T_PROMPT - 1:T_PROMPT])
                g.tensor_copy(tails[:, j, c + 1:c + 1 + NB],
                              smp(rr, seg0 + TB - 1, 1).rearrange("p b x -> p (b x)")).then_inc(h_tail, 1)
            pool.wait_ge(vrows_out, 32)
            when_read(pool, ("mix", JB - 1, 2))
            g.memset(smp_acc[:], 0.0).then_inc(smp_zero, 1)
            pool.wait_ge(h_tail, JB)
            for j in range(1, JB):
                pool.wait_ge(rgsq, j + 1)
                if j > 1:
                    pool.wait_ge(rgsum, j - 1)
                g.tensor_tensor(ss_rg[:], sq_rg[:, 0, 0:T] if j == 1 else ss_rg[:],
                                sq_rg[:, j % 2, 0:T], ALU.add).then_inc(rgsum, 1)
            for gi in range(3):
                for j in range(JB):
                    pool.wait_ge(mrg_hi, JB * gi + j + 1)
                    g.tensor_tensor(blk(act_lo, j, gi), blk(RG, j, gi), f32(blk(act_hi, j, gi)),
                                    ALU.subtract).then_inc(mrg_ready, 1)
            when_read(pool, "tails")
            n1, n2 = HALO, HALO + NB * HALO
            pool.dma_start(out[2][0, 0], tails_out[0:n1, :]).then_inc(tails_stored, 16)
            pool.dma_start(out[5][0].rearrange("b t d -> (b t) d"), tails_out[n1:n2, :]).then_inc(tails_stored, 16)
            pool.dma_start(out[3][0], tails_out[n2:n2 + 1, :]).then_inc(tails_stored, 16)
            pool.dma_start(out[6][0], tails_out[n2 + 1:n2 + 1 + NB, :]).then_inc(tails_stored, 16)

            def hidden_lo(b, pair):
                for c in range(2):
                    for gi in range(3):
                        item = 3 * c + gi
                        n = GROUPS[gi][1]
                        bank = 3 * c + gi
                        pool.wait_ge(free[bank], ff1_turn(b) + 1)
                        pool.wait_ge(hhi_done, 6 * b + item + 1)
                        s = 2 * pair + c
                        g.tensor_tensor(blk(h_lo, s, gi), sqr[:, item % 2, 0:n], f32(blk(h_hi, s, gi)),
                                        ALU.subtract).then_inc(h_ready, 1)

            hidden_lo(0, 0)
            with pool.Fori(0, (FF_BLOCKS - 2) // 2) as m:
                hidden_lo(2 * m + 1, 1)
                hidden_lo(2 * m + 2, 0)
            hidden_lo(FF_BLOCKS - 1, 1)

        SCALE_NO = {"x": 1, "rg": 2, ("sg", 0): 3, ("sg", 1): 4, ("sg", 2): 5,
                    ("x1", 0): 6, ("x1", 1): 7, ("x1", 2): 8, ("y", 0): 9, ("y", 1): 10, ("y", 2): 11}

        def by_rows(tiles):
            whole = [t for t in tiles if tile_rows(t) == P]
            parts = [(P, whole[0], whole[-1] + 1)]
            if NT - 1 in tiles:
                parts.append((tile_rows(NT - 1), NT - 1, NT))
            return parts

        @block.tensor
        def _(pe):
            mm = nc.tensor.matmul

            def turn(dst, src, rows=P):
                return nc.tensor.transpose(dst, src, ident[0:rows, 0:rows])

            pe.wait_ge(pool_set, 7)
            pe.wait_ge(rows_in, 16 * N_ROW_LOADS)
            bank = claim(pe, "rows512")
            for j in range(JB):
                last = turn(bank[:, R512 * j:R512 * j + R512], rows512[0:R512, P * j:P * j + P], R512)
            last.then_inc(full_of("rows512"), 1)
            bank = claim(pe, "rows1024")
            for k in range(KD):
                turn(bank[:, R1024 * k:R1024 * k + R1024], rows1024[0:R1024, P * k:P * k + P], R1024)
            turn(bank[:, P:P + N_ADA], bada_rows[0:N_ADA, :], N_ADA).then_inc(full_of("rows1024"), 1)

            pe.wait_ge(pool_set, 10)
            for half in range(2):
                bank = claim(pe, f"ws{half}")
                for h in range(4):
                    last = turn(bank[:, CHUNK * h:CHUNK * h + CHUNK], ws_raw[:, 4 * half + h, :])
                last.then_inc(full_of(f"ws{half}"), 1)
            when_read(pe, "ws0")
            when_read(pe, "ws1")
            pe.wait_ge(eye_ready, 1)
            bank = claim(pe, "wsmall")
            mm(bank[0:64, 0:64], eye8[0:TB].rearrange("p b s -> p (b s)"), wsT[0:TB, :, 0:TB],
               start=True, stop=True).then_inc(full_of("wsmall"), 1)
            bank = claim(pe, "rowsum")
            for h in range(HEADS):
                e = h % 2
                last = mm(bank[HD * e:HD * e + HD, CHUNK * (h // 2):CHUNK * (h // 2) + CHUNK], ones64[:, :],
                          wsT[:, h, :], start=True, stop=True)
            last.then_inc(full_of("rowsum"), 1)

            for t in range(NT):
                pe.wait_ge(x_in[t], 16)
                r = tile_rows(t)
                for h in range(2):
                    bank = claim(pe, ("x", t, h))
                    for i in range(4):
                        k = 4 * h + i
                        last = turn(bank[:, r * i:r * i + r], xin[0:r, t, P * k:P * k + P], r)
                    last.then_inc(full_of(("x", t, h)), 1)

            pe.wait_ge(silu_ready, 1)
            bank = claim(pe, "ada1")
            for k in range(KD):
                pe.wait_ge(ada_w_in[k], 16)
                for m in range(ADA_EARLY):
                    last = mm(bank[:, NC * m:NC * m + NC], ada_w[:, k, P * m:P * m + P], silu[:, k, :],
                              start=(k == 0 and m == 0), stop=(k == KD - 1), skip_group_check=True)
            last.then_inc(full_of("ada1"), 1)

            def spread_scale(name, scale, tiles):
                pe.wait_ge(rstd_done, SCALE_NO[scale])
                bank = claim(pe, name)
                for i, t in enumerate(tiles):
                    r = tile_rows(t)
                    last = turn(bank[:, P * i:P * i + r], rstd[0:r, t:t + 1].to_broadcast([r, P]), r)
                last.then_inc(full_of(name), 1)

            def sum_squares(name, squares, tiles):
                bank = claim(pe, name)
                for t in tiles:
                    r = tile_rows(t)
                    last = mm(bank[0:r, t:t + 1], squares[:, P * t:P * t + r], ones[:, :], start=True, stop=True)
                last.then_inc(full_of(name), 1)

            for g in range(3):
                spread_scale(("bcx", g), "x", TILES_OF[g])

            def split_product(bank, n, w, rhs, k, first, final):
                mm(bank[:, 0:n], w(w_hi), rhs(act_hi if rhs_act[0] else h_hi), start=first, stop=False)
                mm(bank[:, 0:n], w(w_hi), rhs(act_lo if rhs_act[0] else h_lo), start=False, stop=False)
                return mm(bank[:, 0:n], w(w_lo), rhs(act_hi if rhs_act[0] else h_hi), start=False, stop=final)

            rhs_act = [True]

            def project(bank, s, g, wait_k=None):
                c, n = GROUPS[g]
                for k in range(KD):
                    if wait_k:
                        wait_k(k)
                    last = split_product(bank, n, lambda t: t[:, s, P * k:P * k + P],
                                         lambda t: t[:, k, c:c + n], k, k == 0, k == KD - 1)
                return last

            late = [0]

            def ada_product():
                m = late[0]
                if m == N_ADA - ADA_EARLY:
                    return
                late[0] += 1
                bank = claim(pe, "ada2") if m == 0 else psum[USE["ada2"][0]]
                pe.wait_ge(ada_in[m % 2], 16 * (m // 2 + 1))
                for k in range(KD):
                    last = mm(bank[:, NC * m:NC * m + NC], ada_ring[:, m % 2, k, :], silu[:, k, :],
                              start=(m == 0 and k == 0), stop=(k == KD - 1), skip_group_check=True)
                last.then_inc(full_of("ada2") if m == N_ADA - ADA_EARLY - 1 else ada_used, 1)

            def v_by_token(t):
                bank = claim(pe, ("vt", t))
                r = tile_rows(t)
                for j in range(JB):
                    last = turn(bank[0:r, P * j:P * j + P], V[:, j, P * t:P * t + r])
                last.then_inc(full_of(("vt", t)), 1)

            def in_tile(name, j, n, after=()):
                pe.wait_ge(lo_done[n % 2], n // 2 + 1)
                for g in range(3):
                    wait_k = None
                    if n == 0:
                        wait_k = lambda k: pe.wait_ge(act_ready, KD * g + k + 1 + (g == 2))
                    bank = claim(pe, (name, j, g))
                    project(bank, n % 2, g, wait_k).then_inc(full_of((name, j, g)), 1)
                    for f in after[g:g + 1]:
                        f()

            for j in range(JB):
                in_tile("v", j, U_V + j, [ada_product] * 3)
            for j in range(JB):
                def after_group(g, yg, j=j):
                    ada_product()
                    if j < 3 and not yg and g == 2:
                        v_by_token(3 * j)
                    if j < 3 and yg and g > 0:
                        v_by_token(3 * j + g)
                if j == 0:
                    for jj in range(2, JB):
                        for g in range(3):
                            when_read(pe, ("v", jj, g))
                in_tile("xr", j, U_RG + 2 * j, [lambda g=g: after_group(g, False) for g in range(3)])
                in_tile("yg", j, U_RG + 2 * j + 1, [lambda g=g: after_group(g, True) for g in range(3)])
                if j == JB - 1:
                    pe.wait_ge(v_norm, NT + 2)
                    for jj in range(JB):
                        for g in range(2):
                            bank = claim(pe, ("mix", jj, g))
                            for c in range(4):
                                for e in range(2):
                                    col = P * (4 * g + c) + HD * e
                                    last = mm(bank[HD * e:HD * e + HD, P * c:P * c + P], V[:, jj, col:col + HD],
                                              wsT[:, 2 * jj + e, :], start=True, stop=True)
                            last.then_inc(full_of(("mix", jj, g)), 1)
                        bank = claim(pe, ("mix", jj, 2))
                        for e in range(2):
                            col = P * (NT - 1) + HD * e
                            last = mm(bank[HD * e:HD * e + HD, 0:T_SAMPLE], V[0:T_SAMPLE, jj, col:col + HD],
                                      ws64[0:T_SAMPLE, 2 * jj + e].rearrange("p b t -> p (b t)"),
                                      start=True, stop=True)
                        last.then_inc(full_of(("mix", jj, 2)), 1)
                if j == 0:
                    pe.wait_ge(gates_in, 64)
                pe.wait_ge(tap_done, 4 * j + 4)
                for i, name in enumerate(("gr", "gi")):
                    for g, (c, n) in enumerate(SCAN_GROUPS):
                        bank = claim(pe, (name, j, g))
                        mm(bank[:, 0:n], gate_w[:, i, j, :], xc[:, c:c + n],
                           start=True, stop=True).then_inc(full_of((name, j, g)), 1)

            for j in range(JB - 1):
                in_tile("u", j, U_U + j)
            pe.wait_ge(rgsum, JB - 1)
            sum_squares("ss_rg", ss_rg, range(NT))

            def sum_sg(g):
                pe.wait_ge(sgsum, 3 * (JB - 2) + g + 1)
                sum_squares(("ss_sg", g), ss_sg, TILES_OF[g])

            def after_u0():
                spread_scale(("bcrg", 0), "rg", TILES_OF[0])
                spread_scale(("bcrg", 1), "rg", TILES_OF[1])

            def after_u1():
                sum_sg(0)
                spread_scale(("bcrg", 2), "rg", TILES_OF[2])

            in_tile("u", JB - 1, U_U + JB - 1, [after_u0, after_u1])
            spread_scale(("bcsg", 0), ("sg", 0), TILES_OF[0])
            sum_sg(1)

            def out_group(n, o, g):
                def wait_k(k):
                    if k < JB:
                        pe.wait_ge(mrg_ready, JB * g + k + 1)
                    else:
                        pe.wait_ge(msg_ready, JB * g + k - JB + 1)
                pe.wait_ge(lo_done[n % 2], n // 2 + 1)
                bank = claim(pe, ("out", o, g))
                project(bank, n % 2, g, wait_k if o == 0 else None).then_inc(full_of(("out", o, g)), 1)

            for o in range(KD):
                out_group(U_OUT_A + o, o, 0)
                if o == 0:
                    spread_scale(("bcsg", 1), ("sg", 1), TILES_OF[1])
                    sum_sg(2)
                out_group(U_OUT_A + o, o, 1)
                if o == 0:
                    spread_scale(("bcsg", 2), ("sg", 2), TILES_OF[2])
                    pe.wait_ge(h_tail, JB)
                    bank = claim(pe, "tails")
                    for j in range(JB):
                        last = turn(bank[0:TAILS, P * j:P * j + P], tails[:, j, :])
                    last.then_inc(full_of("tails"), 1)
            for o in range(KD):
                out_group(U_OUT_B + o, o, 2)
                if o == 0:
                    pe.wait_ge(x1sum, 2 * (KD - 1))
                    sum_squares(("ss_x1", 0), ss_x, TILES_OF[0])
                if o == 1:
                    spread_scale(("bcx1", 0), ("x1", 0), TILES_OF[0])
                    sum_squares(("ss_x1", 1), ss_x, TILES_OF[1])
                if o == 4:
                    spread_scale(("bcx1", 1), ("x1", 1), TILES_OF[1])

            def hidden(b, first=False):
                rhs_act[0] = True
                for c in range(2):
                    pe.wait_ge(lo_done[c], ff1_half(b) + 1)
                    for g in range(3):
                        wait_k = None
                        if first and c == 0:
                            wait_k = lambda k: pe.wait_ge(act_ready, NORM_ITEMS + KD * g + k + 1 + (g == 2))
                        pe.wait_ge(free[3 * c + g], ff1_turn(b))
                        project(psum[3 * c + g], c, g, wait_k).then_inc(full[3 * c + g], 1)
                        if first and c == 0 and g == 0:
                            pe.wait_ge(x1sum, 3 * (KD - 1))
                            sum_squares(("ss_x1", 2), ss_x, TILES_OF[2])
                        if first and c == 0 and g == 1:
                            spread_scale(("bcx1", 2), ("x1", 2), TILES_OF[2])

            def back(b, pair):
                rhs_act[0] = False
                for h in range(2):
                    pe.wait_ge(lo_done[h], ff2_half(b) + 1)
                    for i in range(4):
                        o = 4 * h + i
                        for g, (c, n) in enumerate(GROUPS):
                            bank = 3 * (o % 2) + g
                            if o == 0:
                                pe.wait_ge(h_ready, 6 * b + 3 + g + 1)
                            pe.wait_ge(free[bank], ff2_turn(b) + o // 2)
                            for k in range(2):
                                last = split_product(psum[bank], n, lambda t: t[:, h, 512 * k + P * i:512 * k + P * i + P],
                                                     lambda t: t[:, 2 * pair + k, c:c + n], k, k == 0, k == 1)
                            last.then_inc(full[bank], 1)

            hidden(0, first=True)
            with pe.Fori(0, (FF_BLOCKS - 2) // 2) as m:
                hidden(2 * m + 1)
                back(2 * m, 0)
                hidden(2 * m + 2)
                back(2 * m + 1, 1)
            hidden(FF_BLOCKS - 1)
            back(FF_BLOCKS - 2, 0)
            back(FF_BLOCKS - 1, 1)

            for g in range(3):
                pe.wait_ge(ysum, 3 * (KD - 2) + g + 1)
                sum_squares(("ss_y", g), ss_x, TILES_OF[g])
            for t in range(NT):
                r = tile_rows(t)
                for h in range(2):
                    bank = claim(pe, ("y", t, h))
                    for i in range(4):
                        last = turn(bank[0:r, P * i:P * i + P], xT[:, 4 * h + i, P * t:P * t + r])
                    last.then_inc(full_of(("y", t, h)), 1)

        @block.scalar
        def _(act):
            s = nc.scalar

            loads = [
                (rows1024[R_GMIX:R_GMIX + 1, :], a["g_mix"]), (rows1024[R_GFFN:R_GFFN + 1, :], a["g_ffn"]),
                (rows1024[R_C:R_C + 1, :], a["c_prompt"]), (rows1024[R_C + 1:R_C + NC, :], a["c_sample"]),
                (bada_rows[0:N_ADA, :], a["b_ada"][0].rearrange("(m p) -> m p", p=P)),
                (rows512[R_STATE:R_STATE + NB * HALO, :], a["state_conv"][0].rearrange("b t d -> (b t) d")),
                (rows512[R_H0:R_H0 + NB, :], a["state_rglru"][0]),
                (rows512[R_CW:R_CW + CONV_W, :], a["conv_w"][0]),
                (rows512[R_CB:R_CB + 1, :], a["conv_b"]),
                (rows512[R_BRA:R_BRA + 1, :], a["b_ra"].rearrange("l h d -> l (h d)")),
                (rows512[R_BRI:R_BRI + 1, :], a["b_ri"].rearrange("l h d -> l (h d)")),
                (rows512[R_LRU:R_LRU + 1, :], a["lru_l"]), (rows512[R_LNG:R_LNG + 1, :], a["ln_v_g"]),
                (rows512[R_LNB:R_LNB + 1, :], a["ln_v_b"]), (rows512[R_GRG:R_GRG + 1, :], a["g_rg"]),
                (rows512[R_GSG:R_GSG + 1, :], a["g_sg"]),
            ]
            assert len(loads) == N_ROW_LOADS
            for dst, src in loads:
                act.dma_start(dst, src).then_inc(rows_in, 16)
            act.dma_start(ws_raw[:], a["w_s"][0].rearrange("h t s -> t h s")).then_inc(ws_in, 16)
            for k in range(KD):
                act.dma_start(ada_w[:, k, :], w_ada_v[:, k, 0:ADA_EARLY * P]).then_inc(ada_w_in[k], 16)
            act.wait_ge(pool_set, 1)
            for i, name in enumerate(("w_ra", "w_ri")):
                for e in range(2):
                    act.dma_start(gate_w[HD * e:HD * e + HD, i, :, HD * e:HD * e + HD],
                                  a[name][0].rearrange("(j e) i o -> e i j o", e=2)[e]).then_inc(gates_in, 16)
            for h in range(HEADS):
                e = h % 2
                act.dma_start(mix_b[HD * e:HD * e + HD, h // 2, :],
                              a["b_s"][0, h:h + 1, :].to_broadcast([HD, CHUNK])).then_inc(bs_in, 16)

            for t in range(NT):
                r = tile_rows(t)
                act.wait_ge(x_in[t], 16)
                if t > 0:
                    act.wait_ge(x_sq, t)
                s.activation(w_lo[0:r, 1, :], xin[0:r, t, :], ACT.Square, accum_out=ssq[0:r, t:t + 1]).then_inc(x_sq, 1)
                bank = when_full(act, ("x", t, 1))
                s.activation(xT[:, 4:8, P * t:P * t + r], bank[:, 0:4 * r].rearrange("p (k c) -> p k c", k=4),
                             ACT.Copy).then_inc(free_of(("x", t, 1)), 1)
                if t == 2:
                    when_read(act, "rows1024")
                    s.activation(silu[:], r10[:, :, R_C:R_C + NC], ACT.Sigmoid).then_inc(silu_sig, 1)
                if t == 3:
                    act.wait_ge(lam_step, 1)
                    s.activation(lam[:, 1, :], lam[:, 0, :], ACT.Exp, scale=-1.0).then_inc(lam_exp, 1)

            def root(name, scale, tiles, d):
                bank = when_full(act, name)
                if SCALE_NO[scale] > 1:
                    act.wait_ge(rstd_done, SCALE_NO[scale] - 1)
                parts = by_rows(tiles)
                for i, (r, t0, t1) in enumerate(parts):
                    ins = s.activation(std[0:r, t0:t1], bank[0:r, t0:t1], ACT.Sqrt, bias=eps[0:r, :], scale=1.0 / d)
                ins.then_inc(free_of(name), 1)

            def split_hi(slot, half, src_read):
                act.wait_ge(raw_in[slot], 16 * (half + 1))
                if src_read is not None:
                    act.wait_ge(*src_read)
                s.activation(w_hi[:, slot, :], w_raw[:, slot, :], ACT.Copy).then_inc(hi_done[slot], 1)

            def full_at(name):
                bank, turn = USE[name]
                return full[bank], turn + 1

            act.wait_ge(x_sq, NT)
            act.wait_ge(pool_set, 5)
            for r, t0, t1 in by_rows(range(NT)):
                ins = s.activation(std[0:r, t0:t1], ssq[0:r, t0:t1], ACT.Sqrt, bias=eps[0:r, :], scale=1.0 / D)
            ins.then_inc(std_done, 1)
            split_hi(0, 0, None)
            split_hi(1, 0, None)

            def norm_hi_items(base, n0, n1, shift, smp_buf, tmp_buf):
                for i in range(n0, n1):
                    act.wait_ge(norm_tmp, base + i + 1)
                    if i == 2 * KD:
                        s.activation(act_hi[:, :, T_PROMPT:T], smp_buf[:, :, :], ACT.Copy).then_inc(norm_hi, 1)
                        continue
                    g, k = (i // KD, i % KD) if i < 2 * KD else (2, i - 2 * KD - 1)
                    n = GROUPS[g][1] if g < 2 else PROMPT_G2
                    s.activation(blk(act_hi, k, g, n), tmp_buf[:, i % 2, 0:n], ACT.Identity,
                                 bias=shift[:, k, 0:1]).then_inc(norm_hi, 1)

            norm_hi_items(0, 0, NORM_ITEMS, ada_e[:, 0:KD], smp0, tmp0)

            for j in range(JB):
                for g in range(3):
                    bank = when_full(act, ("v", j, g))
                    if j == 0 and g == 0:
                        act.wait_ge(act_ready, NORM_ITEMS)
                    s.activation(blk(V, j, g), bank[:, 0:GROUPS[g][1]], ACT.Copy).then_inc(free_of(("v", j, g)), 1)
                n = U_V + j + 2
                split_hi(n % 2, n // 2, full_at(("v", j, 2)))

            def v_copy(t):
                bank = when_full(act, ("vt", t))
                r = tile_rows(t)
                s.activation(V[0:r, :, P * t:P * t + P], bank[0:r, :].rearrange("p (j d) -> p j d", j=JB),
                             ACT.Copy).then_inc(free_of(("vt", t)), 1)

            for j in range(JB):
                if j > 0:
                    act.wait_ge(term_done, j)
                for g in range(2):
                    bank = when_full(act, ("xr", j, g))
                    c, n = GROUPS[g]
                    s.activation(row[:, row_tok + c:row_tok + c + n], bank[:, 0:n], ACT.Copy
                                 ).then_inc(free_of(("xr", j, g)), 1)
                bank = when_full(act, ("xr", j, 2))
                c = row_tok + GROUPS[2][0]
                s.activation(row[:, c:c + PROMPT_G2], bank[:, 0:PROMPT_G2], ACT.Copy)
                s.activation(smp(row, seg0 + HALO, TB), by_sample(bank[:, PROMPT_G2:PROMPT_G2 + T_SAMPLE]), ACT.Copy
                             ).then_inc(free_of(("xr", j, 2)), 1)
                n = U_RG + 2 * j + 2
                split_hi(n % 2, n // 2, full_at(("xr", j, 2)))
                when_read(act, ("xr", j, 2))
                act.wait_ge(halo_done, 2 * j + 2)
                if j > 0:
                    act.wait_ge(ix_done, j)
                s.activation(xc[:, 0:SCAN_W], row[:, 0:SCAN_W], ACT.Identity, bias=r5[:, j, R_CB:R_CB + 1],
                             scale=r5[:, j, R_CW:R_CW + 1]).then_inc(tap_done, 1)
                if j < 3:
                    v_copy(3 * j)
                for g in range(3):
                    bank = when_full(act, ("yg", j, g))
                    s.activation(blk(RG, j, g), bank[:, 0:GROUPS[g][1]], ACT.Gelu_apprx_tanh
                                 ).then_inc(free_of(("yg", j, g)), 1)
                    if j < 3 and g > 0:
                        v_copy(3 * j + g)
                n = U_RG + 2 * j + 3
                split_hi(n % 2, n // 2, full_at(("yg", j, 2)))
                if j > 0:
                    act.wait_ge(rg_done, j)
                    act.wait_ge(h_tail, j)
                for name, dst, bias in (("gr", rr, R_BRA), ("gi", ig, R_BRI)):
                    for g, (c, n) in enumerate(SCAN_GROUPS):
                        bank = when_full(act, (name, j, g))
                        s.activation(dst[:, c:c + n], bank[:, 0:n], ACT.Sigmoid, bias=r5[:, j, bias:bias + 1]
                                     ).then_inc(free_of((name, j, g)), 1)
                when_read(act, ("gr", j, 2))
                act.wait_ge(lam_step, LAM_STEPS)
                s.activation(aa[:, 0:SCAN_W], rr[:, 0:SCAN_W], ACT.Exp, scale=decay[:, j:j + 1]).then_inc(decay_done, 1)
                act.wait_ge(decay_done, j + 1)
                s.activation(rr[:, 0:SCAN_W], rr[:, 0:SCAN_W], ACT.Tanh, scale=decay_n[:, j:j + 1]).then_inc(act_chain, 1)
                act.wait_ge(row_read, j + 1)
                act.wait_ge(tap_done, 4 * j + 4)
                s.activation(row[:, 0:SCAN_W], aa[:, 0:SCAN_W], ACT.Square).then_inc(act_chain, 1)
                act.wait_ge(q_done, j + 1)
                s.activation(row[:, 0:SCAN_W], row[:, 0:SCAN_W], ACT.Sqrt).then_inc(root_done, 1)
                if j == 2:
                    act.wait_ge(v_stat, 2 * NT)
                    for r, t0, t1 in by_rows(range(NT)):
                        s.activation(v_std[0:r, t0:t1], mv[0:r, t0:t1, 1], ACT.Sqrt, bias=eps[0:r, :]
                                     ).then_inc(v_std_done, 1)

            def rg_square(j):
                if j >= 2:
                    act.wait_ge(rgsum, 1)
                s.activation(sq_rg[:, j % 2, 0:T], RG[:, j, :], ACT.Square).then_inc(rgsq, 1)

            def sg_square(j, g):
                i = 3 * j + g
                when_read(act, ("u", j, g))
                if i >= 5:
                    act.wait_ge(sgsum, i - 4)
                n = GROUPS[g][1]
                s.activation(cols(ss_sg, g) if j == 0 else sq_g[:, i % 2, 0:n], blk(V, j, g), ACT.Square
                             ).then_inc(sgsq, 1)

            def branch_hi(g):
                act.wait_ge(*full_at(("u", JB - 1, g)))
                for j in range(JB):
                    act.wait_ge(rg_norm, JB * g + j + 1)
                    s.activation(blk(act_hi, j, g), blk(RG, j, g), ACT.Copy).then_inc(mrg_hi, 1)

            def gate_hi(g):
                for j in range(JB):
                    act.wait_ge(sg_norm, JB * g + j + 1)
                    s.activation(blk(act_hi, JB + j, g), blk(V, j, g), ACT.Copy).then_inc(msg_hi, 1)

            act.wait_ge(rg_done, JB)
            act.wait_ge(h_tail, JB)
            rg_square(0)
            rg_square(1)
            for j in range(JB - 1):
                for g in range(3):
                    sg_square(j, g)
                if j == 0:
                    rg_square(2)
                    rg_square(3)
                n = U_U + j + 2
                split_hi(n % 2, n // 2, full_at(("u", j, 2)))
            root("ss_rg", "rg", range(NT), D_RG)
            sg_square(3, 0)
            branch_hi(0)
            sg_square(3, 1)
            root(("ss_sg", 0), ("sg", 0), TILES_OF[0], D_SG)
            branch_hi(1)
            sg_square(3, 2)
            branch_hi(2)
            n = U_OUT_A + 1
            split_hi(n % 2, n // 2, full_at(("u", 3, 2)))
            gate_hi(0)
            root(("ss_sg", 1), ("sg", 1), TILES_OF[1], D_SG)
            gate_hi(1)
            root(("ss_sg", 2), ("sg", 2), TILES_OF[2], D_SG)
            gate_hi(2)
            bank = when_full(act, "tails")
            s.activation(tails_out[0:TAILS, :], bank[0:TAILS, :], ACT.Copy).then_inc(free_of("tails"), 1)

            def x1_square(o, g):
                i = 2 * o + g
                if g < 2:
                    when_read(act, ("out", o, g))
                    if i >= 4:
                        act.wait_ge(x1sum, i - 3)
                    slot = i % 2
                else:
                    act.wait_ge(x1_smp, o + 1)
                    act.wait_ge(x1sum, max(2 * (KD - 1), 2 * (KD - 1) + o - 2))
                    slot = o % 2
                n = GROUPS[g][1]
                s.activation(cols(ss_x, g) if o == 0 else sq_g[:, slot, 0:n], blk(xT, o, g), ACT.Square
                             ).then_inc(x1sq, 1)

            hf = lambda n0, n1: norm_hi_items(NORM_ITEMS, n0, n1, ada_late[:, KD:2 * KD], smp1, tmp1)
            for o in range(KD):
                x1_square(o, 0)
                x1_square(o, 1)
                n = U_OUT_A + o + 2
                split_hi(n % 2, n // 2, full_at(("out", o, 1)))
            for o in range(KD):
                x1_square(o, 2)
                n = U_OUT_B + o + 2
                split_hi(n % 2, n // 2, full_at(("out", o, 2)))
                if o == 0:
                    root(("ss_x1", 0), ("x1", 0), TILES_OF[0], D)
                if o == 1:
                    root(("ss_x1", 1), ("x1", 1), TILES_OF[1], D)
                hf(HF_AT[o], HF_AT[o + 1])
            root(("ss_x1", 2), ("x1", 2), TILES_OF[2], D)
            hf(2 * KD, NORM_ITEMS)

            def hidden_hi(b, pair, next_unit=None, first=False):
                for c in range(2):
                    for g in range(3):
                        i = 3 * c + g
                        n = GROUPS[g][1]
                        bank = 3 * c + g
                        act.wait_ge(full[bank], ff1_turn(b) + 1)
                        if not (first and i < 2):
                            act.wait_ge(h_ready, 6 * b + i - 1)
                        s.activation(relu[:, i % 2, 0:n], psum[bank][:, 0:n], ACT.Relu).then_inc(relu_done, 1)
                        act.wait_ge(relu_done, 6 * b + i + 1)
                        s.activation(blk(h_hi, 2 * pair + c, g), relu[:, i % 2, 0:n], ACT.Square).then_inc(hhi_done, 1)
                    if next_unit is not None:
                        split_hi(c, next_unit, (full[3 * c + 2], ff1_turn(b) + 1))

            def back_hi(b, next_unit):
                for h in range(2):
                    if next_unit is not None:
                        split_hi(h, next_unit, (full[5], ff2_turn(b) + 2 * h + 2))

            hidden_hi(0, 0, ff1_half(1), first=True)
            with act.Fori(0, (FF_BLOCKS - 2) // 2) as m:
                hidden_hi(2 * m + 1, 1, ff2_half(2 * m))
                back_hi(2 * m, ff1_half(2 * m + 2))
                hidden_hi(2 * m + 2, 0, ff2_half(2 * m + 1))
                back_hi(2 * m + 1, ff1_half(2 * m + 3))
            hidden_hi(FF_BLOCKS - 1, 1, ff2_half(FF_BLOCKS - 2))
            back_hi(FF_BLOCKS - 2, ff2_half(FF_BLOCKS - 1))

            for o in range(KD):
                for g in range(3):
                    i = 3 * o + g
                    if g < 2:
                        act.wait_ge(free[3 * (o % 2) + g], ff2_turn(FF_BLOCKS - 1) + o // 2 + 1)
                    else:
                        act.wait_ge(y_smp, 2 * o + 2)
                    if i >= 5:
                        act.wait_ge(ysum, i - 4)
                    n = GROUPS[g][1]
                    s.activation(cols(ss_x, g) if o == 0 else sq_g[:, i % 2, 0:n], blk(xT, o, g), ACT.Square
                                 ).then_inc(ysq, 1)
            for g in range(3):
                root(("ss_y", g), ("y", g), TILES_OF[g], D)

        @block.vector
        def _(dve):
            v = nc.vector

            bank = when_full(dve, "rows512")
            v.tensor_copy(r5[:], bank[:, 0:JB * R512].rearrange("p (j r) -> p j r", j=JB)
                          ).then_inc(free_of("rows512"), 1)
            bank = when_full(dve, "rows1024")
            v.tensor_copy(bada[:], bank[:, P:P + N_ADA])
            v.tensor_copy(r10[:], bank[:, 0:KD * R1024].rearrange("p (k r) -> p k r", k=KD)
                          ).then_inc(free_of("rows1024"), 1)
            dve.wait_ge(pool_set, 9)
            v.tensor_copy(eye8[0:TB], ident[0:TB, 0:TB].unsqueeze(1).to_broadcast([TB, NB, TB])).then_inc(eye_ready, 1)
            for half in range(2):
                bank = when_full(dve, f"ws{half}")
                v.tensor_copy(wsT[:, 4 * half:4 * half + 4], bank[:].rearrange("p (h t) -> p h t", h=4)
                              ).then_inc(free_of(f"ws{half}"), 1)
            when_read(dve, "rows512")
            raw_l = r5[:, :, R_LRU]
            v.scalar_tensor_tensor(lam[:, 0, :], raw_l, -1.0, raw_l, ALU.mult, ALU.max).then_inc(lam_step, 1)
            bank = when_full(dve, "wsmall")
            small = bank[0:64, 0:64].rearrange("p (h t) -> p h t", h=HEADS).unsqueeze(2).to_broadcast([64, HEADS, NB, TB])
            mask = own[0:64].unsqueeze(1).unsqueeze(3).to_broadcast([64, HEADS, NB, TB])
            v.tensor_tensor(ws64[0:64], small, mask, ALU.mult).then_inc(free_of("wsmall"), 1)
            bank = when_full(dve, "rowsum")
            dve.wait_ge(bs_in, 16 * HEADS)
            for j in range(JB):
                ins = v.scalar_tensor_tensor(mix_b[:, j, :], bank[:, CHUNK * j:CHUNK * j + CHUNK],
                                             r5[:, j, R_LNB:R_LNB + 1], mix_b[:, j, :], ALU.mult, ALU.add)
            ins.then_inc(free_of("rowsum"), 1)

            for t in range(NT):
                r = tile_rows(t)
                bank = when_full(dve, ("x", t, 0))
                v.tensor_copy(xT[:, 0:4, P * t:P * t + r], bank[:, 0:4 * r].rearrange("p (k c) -> p k c", k=4)
                              ).then_inc(free_of(("x", t, 0)), 1)
                if t == 3:
                    dve.wait_ge(silu_sig, 1)
                    v.tensor_tensor(silu[:], silu[:], r10[:, :, R_C:R_C + NC], ALU.mult).then_inc(silu_ready, 1)

            steps = [1]

            def step(ins):
                steps[0] += 1
                ins.then_inc(lam_step, 1)
                dve.wait_ge(lam_step, steps[0])

            u, num, s1, s2, ser, low = (lam[:, i, :] for i in (1, 2, 3, 4, 5, 6))
            dve.wait_ge(lam_exp, 1)
            step(v.tensor_scalar(num, u, 2.0, None, ALU.add))
            step(v.reciprocal(num, num))
            step(v.tensor_tensor(s1, u, num, ALU.mult))
            step(v.tensor_tensor(s2, s1, s1, ALU.mult))
            step(v.tensor_scalar(ser, s2, 1.0 / 17.0, None, ALU.mult))
            for d in (15, 13, 11, 9, 7, 5, 3):
                step(v.scalar_tensor_tensor(ser, ser, 1.0 / d, s2, ALU.add, ALU.mult))
            step(v.scalar_tensor_tensor(ser, ser, 1.0, s1, ALU.add, ALU.mult))
            step(v.tensor_scalar(low, raw_l, 0.0, None, ALU.min))
            step(v.scalar_tensor_tensor(low, ser, -2.0, low, ALU.mult, ALU.add))
            step(v.tensor_scalar(decay[:], low, LRU_C, None, ALU.mult))
            step(v.tensor_scalar(decay_n[:], low, -LRU_C, None, ALU.mult))
            assert steps[0] == LAM_STEPS

            def inverse(scale, tiles):
                for i, (r, t0, t1) in enumerate(by_rows(tiles)):
                    ins = v.reciprocal(rstd[0:r, t0:t1], std[0:r, t0:t1])
                ins.then_inc(rstd_done, 1)

            dve.wait_ge(std_done, 1)
            inverse("x", range(NT))

            bank = when_full(dve, "ada1")
            v.tensor_tensor(ada_e[:], bank[:, 0:ADA_EARLY * NC].rearrange("p (m c) -> p m c", c=NC),
                            bada[:, 0:ADA_EARLY].unsqueeze(2).to_broadcast([P, ADA_EARLY, NC]), ALU.add
                            ).then_inc(free_of("ada1"), 1)
            when_read(dve, "ada1")
            v.scalar_tensor_tensor(gain_m[:], ada_e[:, KD:2 * KD], 1.0,
                                   r10[:, :, R_GMIX:R_GMIX + 1].to_broadcast([P, KD, NC]), ALU.add, ALU.mult
                                   ).then_inc(ada_ready, 1)
            dve.wait_ge(ada_ready, 1)

            def split_lo(slot, half):
                dve.wait_ge(hi_done[slot], half + 1)
                v.tensor_tensor(w_lo[:, slot, :], w_raw[:, slot, :], f32(w_hi[:, slot, :]), ALU.subtract
                                ).then_inc(lo_done[slot], 1)

            def release(name, done, count):
                dve.wait_ge(done, count)
                dve.sem_inc(free_of(name), 1)

            pending = [None]

            def norm_items(no, n0, n1, spread, gain, shift, smp_buf, tmp_buf):
                base = NORM_ITEMS * no

                def lower(i):
                    dve.wait_ge(norm_hi, base + i + 1)
                    if i == 2 * KD:
                        v.tensor_tensor(act_lo[:, :, T_PROMPT:T], smp_buf[:, :, :], f32(act_hi[:, :, T_PROMPT:T]),
                                        ALU.subtract).then_inc(act_ready, 1)
                        return
                    g, k = (i // KD, i % KD) if i < 2 * KD else (2, i - 2 * KD - 1)
                    n = GROUPS[g][1] if g < 2 else PROMPT_G2
                    v.scalar_tensor_tensor(blk(act_lo, k, g, n), tmp_buf[:, i % 2, 0:n], shift[:, k, 0:1],
                                           f32(blk(act_hi, k, g, n)), ALU.add, ALU.subtract).then_inc(act_ready, 1)

                for i in range(n0, n1):
                    if i in (0, KD, 2 * KD) and no == 1:
                        when_read(dve, ("ss_x1", i // KD))
                        inverse(("x1", i // KD), TILES_OF[i // KD])
                    if i == 2 * KD:
                        bank = when_full(dve, (spread, 2))
                        if no == 1:
                            dve.wait_ge(tails_stored, 64)
                        sc = bank[:, PROMPT_G2:PROMPT_G2 + T_SAMPLE]
                        v.tensor_tensor(smp_buf[:], xT[:, :, T_PROMPT:T],
                                        sc.unsqueeze(1).to_broadcast([P, KD, T_SAMPLE]), ALU.mult
                                        ).then_inc(smp_step, 1)
                        for q, (m, op) in enumerate(((gain, ALU.mult), (shift, ALU.add))):
                            dve.wait_ge(smp_step, 2 * no + q + 1)
                            view = smp_buf[:].rearrange("p k (b t) -> p k b t", t=TB)
                            ins = v.tensor_tensor(view, view, m[:, :, 1:NC].unsqueeze(3).to_broadcast([P, KD, NB, TB]), op)
                            ins.then_inc(smp_step if q == 0 else norm_tmp, 1)
                    else:
                        g, k = (i // KD, i % KD) if i < 2 * KD else (2, i - 2 * KD - 1)
                        n = GROUPS[g][1] if g < 2 else PROMPT_G2
                        bank = when_full(dve, (spread, g))
                        if i >= 2:
                            dve.wait_ge(act_ready, base + i - 1)
                        v.scalar_tensor_tensor(tmp_buf[:, i % 2, 0:n], blk(xT, k, g, n), gain[:, k, 0:1],
                                               bank[:, 0:n], ALU.mult, ALU.mult).then_inc(norm_tmp, 1)
                    if pending[0] is not None:
                        lower(pending[0])
                    pending[0] = i
                    if i in (KD - 1, 2 * KD - 1, NORM_ITEMS - 1):
                        lower(i)
                        pending[0] = None
                        g = {KD - 1: 0, 2 * KD - 1: 1, NORM_ITEMS - 1: 2}[i]
                        release((spread, g), act_ready, base + i + 1)
                if pending[0] is not None:
                    lower(pending[0])
                    pending[0] = None

            split_lo(0, 0)
            split_lo(1, 0)
            norm_items(0, 0, NORM_ITEMS, "bcx", gain_m[:], ada_e[:, 0:KD], smp0, tmp0)
            for j in range(JB):
                n = U_V + j + 2
                split_lo(n % 2, n // 2)

            def v_stats(t):
                when_read(dve, ("vt", t))
                r = tile_rows(t)
                v.bn_stats(bn[0:r, t, :], V[0:r, :, P * t:P * t + P]).then_inc(v_stat, 1)
                dve.wait_ge(v_stat, 2 * t + 1)
                v.bn_aggr(mv[0:r, t, :], bn[0:r, t, :]).then_inc(v_stat, 1)

            for j in range(JB):
                n = U_RG + 2 * j + 2
                split_lo(n % 2, n // 2)
                for k in range(1, CONV_W):
                    dve.wait_ge(tap_done, 4 * j + k)
                    v.scalar_tensor_tensor(xc[:, 0:SCAN_W], row[:, k:k + SCAN_W], r5[:, j, R_CW + k:R_CW + k + 1],
                                           xc[:, 0:SCAN_W], ALU.mult, ALU.add).then_inc(tap_done, 1)
                if j < 3:
                    for i in range(3):
                        v_stats(3 * j + i)
                else:
                    dve.wait_ge(v_std_done, 2)
                    for r, t0, t1 in by_rows(range(NT)):
                        v.reciprocal(v_std[0:r, t0:t1], v_std[0:r, t0:t1]).then_inc(v_norm, 1)
                    dve.wait_ge(v_norm, 2)
                    dve.wait_ge(vrows_out, 32)
                    for t in range(NT):
                        r = tile_rows(t)
                        v.tensor_scalar(V[0:r, :, P * t:P * t + P], V[0:r, :, P * t:P * t + P], mv[0:r, t, 0:1],
                                        v_std[0:r, t:t + 1], ALU.subtract, ALU.mult).then_inc(v_norm, 1)
                    n_late = N_ADA - ADA_EARLY
                    bank = when_full(dve, "ada2")
                    v.tensor_tensor(ada_late[:], bank[:, 0:n_late * NC].rearrange("p (m c) -> p m c", c=NC),
                                    bada[:, ADA_EARLY:N_ADA].unsqueeze(2).to_broadcast([P, n_late, NC]), ALU.add
                                    ).then_inc(free_of("ada2"), 1)
                    when_read(dve, "ada2")
                    v.scalar_tensor_tensor(gain_f[:], ada_late[:, 2 * KD:3 * KD], 1.0,
                                           r10[:, :, R_GFFN:R_GFFN + 1].to_broadcast([P, KD, NC]), ALU.add, ALU.mult
                                           ).then_inc(ada_ready, 1)
                n = U_RG + 2 * j + 3
                split_lo(n % 2, n // 2)
                if j == JB - 1:
                    for jj in range(JB):
                        gain = r5[:, jj, R_LNG:R_LNG + 1]
                        for g in range(2):
                            bank = when_full(dve, ("mix", jj, g))
                            v.scalar_tensor_tensor(
                                V[:, jj, 512 * g:512 * g + 512].rearrange("p (c t) -> p c t", t=CHUNK),
                                bank[:].rearrange("p (c t) -> p c t", t=CHUNK), gain,
                                mix_b[:, jj, :].unsqueeze(1).to_broadcast([P, 4, CHUNK]), ALU.mult, ALU.add
                            ).then_inc(free_of(("mix", jj, g)), 1)
                        bank = when_full(dve, ("mix", jj, 2))
                        v.scalar_tensor_tensor(
                            by_sample(V[:, jj, T_PROMPT:T]), by_sample(bank[:, 0:T_SAMPLE]), gain,
                            mix_b[:, jj, 0:TB].unsqueeze(1).to_broadcast([P, NB, TB]), ALU.mult, ALU.add
                        ).then_inc(free_of(("mix", jj, 2)), 1)
                dve.wait_ge(act_chain, 2 * j + 2)
                v.scalar_tensor_tensor(row[:, 0:SCAN_W], row[:, 0:SCAN_W], 1.0, rr[:, 0:SCAN_W],
                                       ALU.add, ALU.mult).then_inc(q_done, 1)
                dve.wait_ge(root_done, j + 1)
                dve.wait_ge(ix_done, j + 1)
                v.tensor_tensor(ig[:, 1:SCAN_W], row[:, 1:SCAN_W], ig[:, 1:SCAN_W], ALU.mult).then_inc(term_done, 1)
                v.memset(smp(aa, seg0 - 1, 1), 0.0).then_inc(scan_done, 1)
                dve.wait_ge(term_done, j + 1)
                v.tensor_copy(smp(ig, seg0 - 1, 1), r5[:, j, R_H0:R_H0 + NB].unsqueeze(2)).then_inc(scan_done, 1)
                dve.wait_ge(scan_done, 3 * j + 2)
                v.tensor_tensor_scan(rr[:, 0:SCAN_W], aa[:, 0:SCAN_W], ig[:, 0:SCAN_W], 0.0, ALU.mult, ALU.add
                                     ).then_inc(scan_done, 1)
                dve.wait_ge(scan_done, 3 * j + 3)
                when_read(dve, ("yg", j, 2))
                v.tensor_tensor(RG[:, j, 0:T_PROMPT], RG[:, j, 0:T_PROMPT], rr[:, 0:T_PROMPT], ALU.mult)
                v.tensor_tensor(by_sample(RG[:, j, T_PROMPT:T]), by_sample(RG[:, j, T_PROMPT:T]), smp(rr, seg0, TB),
                                ALU.mult).then_inc(rg_done, 1)

            def gate(j, g):
                bank = when_full(dve, ("u", j, g))
                v.tensor_tensor(blk(V, j, g), bank[:, 0:GROUPS[g][1]], blk(V, j, g), ALU.mult
                                ).then_inc(free_of(("u", j, g)), 1)

            def add_sg(i):
                g = i % 3
                dve.wait_ge(sgsq, i + 1)
                if i < 3:
                    return
                if i >= 6:
                    dve.wait_ge(sgsum, i - 5)
                v.tensor_tensor(cols(ss_sg, g), cols(ss_sg, g), sq_g[:, i % 2, 0:GROUPS[g][1]], ALU.add
                                ).then_inc(sgsum, 1)

            for j in range(JB - 1):
                for g in range(3):
                    gate(j, g)
                    if 3 * j + g > 0:
                        add_sg(3 * j + g - 1)
                n = U_U + j + 2
                split_lo(n % 2, n // 2)
            add_sg(3 * (JB - 1) - 1)
            when_read(dve, "ss_rg")
            inverse("rg", range(NT))

            def norm_rg(g):
                bank = when_full(dve, ("bcrg", g))
                for j in range(JB):
                    v.scalar_tensor_tensor(blk(RG, j, g), blk(RG, j, g), r5[:, j, R_GRG:R_GRG + 1],
                                           bank[:, 0:GROUPS[g][1]], ALU.mult, ALU.mult).then_inc(rg_norm, 1)
                release(("bcrg", g), rg_norm, JB * (g + 1))

            def norm_sg(g):
                when_read(dve, ("ss_sg", g))

                def lower(j):
                    dve.wait_ge(msg_hi, JB * g + j + 1)
                    v.tensor_tensor(blk(act_lo, JB + j, g), blk(V, j, g), f32(blk(act_hi, JB + j, g)), ALU.subtract
                                    ).then_inc(msg_ready, 1)

                bank = when_full(dve, ("bcsg", g))
                for j in range(JB):
                    v.scalar_tensor_tensor(blk(V, j, g), blk(V, j, g), r5[:, j, R_GSG:R_GSG + 1],
                                           bank[:, 0:GROUPS[g][1]], ALU.mult, ALU.mult).then_inc(sg_norm, 1)
                    if j > 0:
                        lower(j - 1)
                lower(JB - 1)
                release(("bcsg", g), sg_norm, JB * (g + 1))

            for g in range(3):
                gate(JB - 1, g)
                add_sg(3 * (JB - 1) + g)
                norm_rg(g)
                if g == 1:
                    when_read(dve, ("ss_sg", 0))
                    inverse(("sg", 0), TILES_OF[0])
            n = U_OUT_A + 1
            split_lo(n % 2, n // 2)
            for g in range(3):
                if g > 0:
                    when_read(dve, ("ss_sg", g))
                    inverse(("sg", g), TILES_OF[g])
                norm_sg(g)

            def add_out(o, g):
                gt = ada_late[:, o, :]
                bank = when_full(dve, ("out", o, g))
                n = GROUPS[g][1] if g < 2 else PROMPT_G2
                ins = v.scalar_tensor_tensor(blk(xT, o, g, n), bank[:, 0:n], gt[:, 0:1], blk(xT, o, g, n),
                                             ALU.mult, ALU.add)
                if g < 2:
                    ins.then_inc(free_of(("out", o, g)), 1)
                    return
                if o > 0:
                    dve.wait_ge(x1_smp, o)
                v.tensor_tensor(by_sample(smp_t[:]), by_sample(bank[:, PROMPT_G2:PROMPT_G2 + T_SAMPLE]),
                                gt[:, 1:NC].unsqueeze(2).to_broadcast([P, NB, TB]), ALU.mult
                                ).then_inc(free_of(("out", o, 2)), 1)
                when_read(dve, ("out", o, 2))
                v.tensor_tensor(xT[:, o, T_PROMPT:T], xT[:, o, T_PROMPT:T], smp_t[:], ALU.add).then_inc(x1_smp, 1)

            def add_x1(o, g):
                if o == 0:
                    return
                if g < 2:
                    i = 2 * o + g
                    dve.wait_ge(x1sq, i + 1)
                    if o >= 2:
                        dve.wait_ge(x1sum, i - 3)
                    slot = i % 2
                else:
                    dve.wait_ge(x1sq, 2 * KD + o + 1)
                    if o >= 2:
                        dve.wait_ge(x1sum, 2 * (KD - 1) + o - 1)
                    slot = o % 2
                v.tensor_tensor(cols(ss_x, g), cols(ss_x, g), sq_g[:, slot, 0:GROUPS[g][1]], ALU.add).then_inc(x1sum, 1)

            hf = lambda n0, n1: norm_items(1, n0, n1, "bcx1", gain_f[:], ada_late[:, KD:2 * KD], smp1, tmp1)
            for o in range(KD):
                add_out(o, 0)
                if o > 0:
                    add_x1(o - 1, 1)
                add_out(o, 1)
                add_x1(o, 0)
                n = U_OUT_A + o + 2
                split_lo(n % 2, n // 2)
            add_x1(KD - 1, 1)
            for o in range(KD):
                add_out(o, 2)
                n = U_OUT_B + o + 2
                split_lo(n % 2, n // 2)
                add_x1(o, 2)
                hf(HF_AT[o], HF_AT[o + 1])
            hf(2 * KD, NORM_ITEMS)

            def hidden_square(b, next_unit=None, first=False):
                for c in range(2):
                    for g in range(3):
                        i = 3 * c + g
                        n = GROUPS[g][1]
                        bank = 3 * c + g
                        dve.wait_ge(relu_done, 6 * b + i + 1)
                        if not (first and i < 2):
                            dve.wait_ge(h_ready, 6 * b + i - 1)
                        v.scalar_tensor_tensor(sqr[:, i % 2, 0:n], psum[bank][:, 0:n], 0.0, relu[:, i % 2, 0:n],
                                               ALU.max, ALU.mult).then_inc(free[bank], 1)
                    if next_unit is not None:
                        split_lo(c, next_unit)

            def add_back(b, o, g):
                bank = 3 * (o % 2) + g
                dve.wait_ge(full[bank], ff2_turn(b) + o // 2 + 1)
                n = GROUPS[g][1] if g < 2 else PROMPT_G2
                ins = v.scalar_tensor_tensor(blk(xT, o, g, n), psum[bank][:, 0:n], ada_late[:, 3 * KD + o, 0:1],
                                             blk(xT, o, g, n), ALU.mult, ALU.add)
                if g == 2:
                    ins = v.tensor_tensor(smp_acc[:, o, :], smp_acc[:, o, :],
                                          psum[bank][:, PROMPT_G2:PROMPT_G2 + T_SAMPLE], ALU.add)
                ins.then_inc(free[bank], 1)

            def back_add(b, next_unit):
                for h in range(2):
                    for i in range(4):
                        for g in range(3):
                            add_back(b, 4 * h + i, g)
                    split_lo(h, next_unit)

            dve.wait_ge(smp_zero, 1)
            hidden_square(0, ff1_half(1), first=True)
            with dve.Fori(0, (FF_BLOCKS - 2) // 2) as m:
                hidden_square(2 * m + 1, ff2_half(2 * m))
                back_add(2 * m, ff1_half(2 * m + 2))
                hidden_square(2 * m + 2, ff2_half(2 * m + 1))
                back_add(2 * m + 1, ff1_half(2 * m + 3))
            hidden_square(FF_BLOCKS - 1, ff2_half(FF_BLOCKS - 2))
            back_add(FF_BLOCKS - 2, ff2_half(FF_BLOCKS - 1))

            def add_y(i):
                g = i % 3
                dve.wait_ge(ysq, i + 1)
                if i < 3:
                    return
                if i >= 6:
                    dve.wait_ge(ysum, i - 5)
                v.tensor_tensor(cols(ss_x, g), cols(ss_x, g), sq_g[:, i % 2, 0:GROUPS[g][1]], ALU.add
                                ).then_inc(ysum, 1)

            last_b = FF_BLOCKS - 1
            for o in range(KD):
                for g in range(3):
                    add_back(last_b, o, g)
                    if g == 2:
                        dve.wait_ge(free[3 * (o % 2) + 2], ff2_turn(last_b) + o // 2 + 1)
                        if o > 0:
                            dve.wait_ge(y_smp, 2 * o)
                        v.tensor_tensor(by_sample(smp_t[:]), by_sample(smp_acc[:, o, :]),
                                        ada_late[:, 3 * KD + o, 1:NC].unsqueeze(2).to_broadcast([P, NB, TB]),
                                        ALU.mult).then_inc(y_smp, 1)
                        dve.wait_ge(y_smp, 2 * o + 1)
                        v.tensor_tensor(xT[:, o, T_PROMPT:T], xT[:, o, T_PROMPT:T], smp_t[:], ALU.add
                                        ).then_inc(y_smp, 1)
                    if 3 * o + g > 0:
                        add_y(3 * o + g - 1)
            add_y(3 * KD - 1)
            for g in range(3):
                when_read(dve, ("ss_y", g))
                inverse(("y", g), TILES_OF[g])
            dve.wait_ge(rstd_done, SCALE_NO["y", 2])
            dve.wait_ge(gfin_in, 16)
            for t in range(NT):
                r = tile_rows(t)
                for h in range(2):
                    bank = when_full(dve, ("y", t, h))
                    v.scalar_tensor_tensor(yout[0:r, t, 512 * h:512 * h + 512], bank[0:r, :], rstd[0:r, t:t + 1],
                                           g_fin[0:r, 512 * h:512 * h + 512], ALU.mult, ALU.mult
                                           ).then_inc(free_of(("y", t, h)), 1)


_INS = ['x_prompt', 'x_sample', 'c_prompt', 'c_sample', 'state_conv', 'state_rglru', 'w_ada', 'b_ada', 'g_mix',
        'g_ffn', 'w_in', 'conv_w', 'conv_b', 'w_ra', 'b_ra', 'w_ri', 'b_ri', 'lru_l', 'ln_v_g', 'ln_v_b', 'w_s',
        'b_s', 'g_rg', 'g_sg', 'w_out', 'w_ff1', 'w_ff2', 'g_final']
_OUTS = [(1, T_PROMPT, D), (NB, TB, D), (1, 1, HALO, D_RG), (1, 1, D_RG), (1, 1, CHUNK, D_SG),
         (1, NB, HALO, D_RG), (1, NB, D_RG), (1, NB, TB, D_SG)]


def kernel(**inputs):
    import numpy as _np
    import concourse.bacc as _bacc
    from concourse import mybir as _mybir
    from concourse.bass_utils import run_bass_kernel_spmd as _run

    nc = _bacc.Bacc("TRN2", target_bir_lowering=False, num_devices=1)
    arrays, args = {}, {}
    for name in _INS:
        x = _np.ascontiguousarray(inputs[name])
        arrays[f"in_{name}"] = x
        args[name] = nc.dram_tensor(f"in_{name}", x.shape, _mybir.dt.from_np(x.dtype), kind="ExternalInput").ap()
    outs = [nc.dram_tensor(f"out_{i}", shape, _mybir.dt.float32, kind="ExternalOutput").ap()
            for i, shape in enumerate(_OUTS)]
    build(nc, args, outs)
    r = _run(nc, [arrays], core_ids=[0])
    return tuple(r.results[0][f"out_{i}"] for i in range(len(_OUTS)))
```

```python
from contextlib import ExitStack

import concourse.bass as bass
from concourse import mybir

F32 = mybir.dt.float32
F32R = mybir.dt.float32r
ALU = mybir.AluOpType
ACT = mybir.ActivationFunctionType

P = 128
D = 1024
T_PROMPT = 1024
NB, TB = 8, 8
T_SAMPLE = NB * TB
T = T_PROMPT + T_SAMPLE
KD = D // P
D_RG = D_SG = D // 2
JB = D_RG // P
D_FF = 4 * D
D_IN = 2 * D_RG + 2 * D_SG
CONV_W = 4
HALO = CONV_W - 1
HEADS, HD = 8, 64
CHUNK = 128
EPS = 1e-6
LRU_C = 8.0
NT = (T + P - 1) // P
NC = 1 + NB
N_ADA = 6 * KD
ADA_EARLY = 2 * KD

GROUPS = [(0, 384), (384, 384), (768, 320)]
TILES_OF = [[0, 1, 2], [3, 4, 5], [6, 7, 8]]
PROMPT_G2 = T_PROMPT - GROUPS[2][0]

SEG = HALO + TB
ROW_W = HALO + T_PROMPT + NB * SEG
SCAN_W = ROW_W - HALO
WIDE = 1120
SCAN_GROUPS = [(0, 384), (384, 384), (768, SCAN_W - 768)]

R_STATE, R_H0, R_CW, R_CB, R_BRA, R_BRI, R_LRU, R_LNG, R_LNB, R_GRG, R_GSG, R512 = 0, 24, 32, 36, 37, 38, 39, 40, 41, 42, 43, 44
R_GMIX, R_GFFN, R_C, R1024 = 0, 1, 2, 2 + NC
TAILS = HALO + NB * HALO + 1 + NB

PIECE = 512
E_PIECES, L_PIECES = ADA_EARLY * P // PIECE, (N_ADA - ADA_EARLY) * P // PIECE
E_UNITS, L_UNITS = E_PIECES * KD // 2, L_PIECES * KD
UNIT_SLOTS = [*range(4, 18), *range(20, 24), *range(26, 30), *range(32, 36), *range(38, 44)]
LAST_TURN = UNIT_SLOTS[-1] + 1
assert len(UNIT_SLOTS) * 2 == L_UNITS
PIECE_OF = {UNIT_SLOTS[i]: i * 2 // KD for i in range(len(UNIT_SLOTS))}
FIRST_SLOT = [UNIT_SLOTS[KD // 2 * p] for p in range(L_PIECES)]
LAST_SLOT = [UNIT_SLOTS[KD // 2 * (p + 1) - 1] for p in range(L_PIECES)]
ROWS_SLOT, WS_SLOTS, SMALL_SLOT, ROWSUM_SLOT = 6, (7, 8), 9, 10

U_V, U_RG, U_U, U_OUT_A, U_OUT_B = 0, 4, 12, 16, 24
U_FF = 32
FF_BLOCKS = D_FF // 256

N_EARLY_LOADS = 5
N_ROW_LOADS = 11
LAM_STEPS = 18
HF_AT = [0, 0, 2, 5, 8, 10, 12, 14, 16]
HM_ITEMS = 3 * KD
NORM_ITEMS = 3 * KD + 1


def plan_banks():
    turns, use = [0] * 8, {}

    def take(name, bank):
        use[name] = (bank, turns[bank])
        turns[bank] += 1

    take("rows1024", 6)
    for t in range(NT):
        for h in range(2):
            take(("x", t, h), (2 * t + h) % 6)
    for g, b in enumerate((7, 0, 1)):
        take(("bcx", g), b)
    for p in range(E_PIECES):
        take(("ap_early", p), 2 + p)
    take("ada1", 6)

    def slot(i):
        if i in FIRST_SLOT:
            p = FIRST_SLOT.index(i)
            if p > 0:
                take(("turned", p - 1), 7)
            take(("ap", p), 6)
        if i == LAST_TURN:
            take(("turned", L_PIECES - 1), 7)
        if i == ROWS_SLOT:
            take("rows512", 7)
        if i in WS_SLOTS:
            take(f"ws{WS_SLOTS.index(i)}", 7)
        if i == SMALL_SLOT:
            take("wsmall", 7)
        if i == ROWSUM_SLOT:
            take("rowsum", 7)

    n_slot = 0
    for j in range(JB):
        for g in range(3):
            take(("v", j, g), 3 * (j % 2) + g)
            slot(n_slot)
            n_slot += 1
    for j in range(JB):
        for name, s in (("xr", 0), ("yg", 1)):
            for g in range(3):
                take((name, j, g), 3 * s + g)
                slot(n_slot)
                n_slot += 1
                if j < 3 and (g > 0 if name == "yg" else g == 2):
                    take(("vt", 3 * j + (g if name == "yg" else 0)), 7)
        if j == JB - 1:
            for jj in range(JB):
                for g in range(3):
                    take(("mix", jj, g), 3 * (jj % 2) + g)
        for name, s in (("gr", 0), ("gi", 1)):
            for g in range(3):
                take((name, j, g), 3 * s + g)
    for i in range(n_slot, n_slot + 3 * (JB - 1)):
        slot(i)
    for j in range(JB):
        for g in range(3):
            take(("u", j, g), 3 * (j % 2) + g)
    take("ss_rg", 7)
    take(("bcrg", 0), 6)
    take(("bcrg", 1), 7)
    take(("bcrg", 2), 6)
    for g in range(3):
        take(("ss_sg", g), 7)
        take(("bcsg", g), 6)
    take("tails", 7)
    for o in range(KD):
        for g in range(2):
            take(("out", o, g), 3 * (o % 2) + g)
    for o in range(KD):
        take(("out", o, 2), 3 * (o % 2) + 2)
    for g in range(3):
        take(("ss_x1", g), 7)
        take(("bcx1", g), 6)
    assert len(set(turns[:6])) == 1
    ff = turns[0]
    for b in range(6):
        turns[b] += 5 * FF_BLOCKS
    for g in range(3):
        take(("ss_y", g), 7)
    for t in range(NT):
        for h in range(2):
            take(("y", t, h), (2 * t + h) % 6)
    return use, ff


USE, FF_TURN = plan_banks()


def ff1_turn(b):
    return FF_TURN if isinstance(b, int) and b == 0 else 5 * b + (FF_TURN - 4)


def ff2_turn(b):
    last = isinstance(b, int) and b == FF_BLOCKS - 1
    return 5 * b + (FF_TURN + 1 if last else FF_TURN + 2)


def ff1_half(b):
    return U_FF // 2 if isinstance(b, int) and b == 0 else 2 * b + (U_FF // 2 - 1)


def ff2_half(b):
    last = isinstance(b, int) and b == FF_BLOCKS - 1
    return 2 * b + (U_FF // 2 + 1 if last else U_FF // 2 + 2)


def build(nc, a, out):
    with ExitStack() as ctx:
        sem = lambda name: ctx.enter_context(nc.semaphore(name))
        psum = [ctx.enter_context(nc.psum_tensor(f"bank{b}", [P, 512], F32)) for b in range(8)]

        base = (nc.sbuf_base + 31) // 32 * 32

        def at(name, shape, offset, dt=F32):
            return nc.alloc_sbuf_tensor_at(name, [P, *shape], dt, offset=offset)

        off_x = base
        off_act = off_x + KD * T * 4
        off_w = off_act + 2 * KD * T * 4
        off_v = off_w + 6 * 4096
        off_rg = off_v + JB * NT * P * 4
        off_t = off_rg + JB * T * 4
        off_c = off_t + 5 * WIDE * 4
        tmp = lambda n: off_t + n * WIDE * 4

        xT = at("xT", [KD, T], off_x)
        act_hi = at("act_hi", [KD, T], off_act, F32R)
        act_lo = at("act_lo", [KD, T], off_act + KD * T * 4, F32R)
        w_raw = at("w_raw", [2, 1024], off_w)
        w_hi = at("w_hi", [2, 1024], off_w + 2 * 4096, F32R)
        w_lo = at("w_lo", [2, 1024], off_w + 4 * 4096, F32R)
        V = at("V", [JB, NT * P], off_v)
        RG = at("RG", [JB, T], off_rg)
        row = at("row", [WIDE], tmp(0))
        xc = at("xc", [WIDE], tmp(1))
        rr = at("rr", [WIDE], tmp(2))
        ig = at("ig", [WIDE], tmp(3))
        aa = at("aa", [WIDE], tmp(4))
        sq_rg = at("sq_rg", [2, WIDE], tmp(0))
        ss_rg = at("ss_rg", [T], tmp(2))
        ss_sg = at("ss_sg", [T], tmp(3))
        sq_g = at("sq_g", [2, 384], tmp(4))
        xin = at("xin", [NT, D], off_v)
        ada_w = at("ada_w", [E_UNITS, 2 * PIECE], off_act)
        ada_w_lo = at("ada_w_lo", [E_UNITS, 2 * PIECE], off_act, F32R)
        xn = at("xn", [KD, T], off_v)
        ws_raw = at("ws_raw", [HEADS, CHUNK], tmp(1))
        own = at("own", [NB], tmp(1) + 4096)
        rows1024 = at("rows1024", [D], tmp(2))
        eye8 = at("eye8", [NB, TB], tmp(2) + 4096)
        rows512 = at("rows512", [D_RG], tmp(3))
        bada_rows = at("bada_rows", [P], tmp(3) + 2048)
        ada_e = at("ada_e", [ADA_EARLY, NC], tmp(3) + 2560)
        gain_m = at("gain_m", [KD, NC], tmp(3) + 3136)
        ones64 = at("ones64", [HD], tmp(3) + 3424)
        h_hi = at("h_hi", [4, T], off_v, F32R)
        h_lo = at("h_lo", [4, T], off_v + 4 * T * 4, F32R)
        relu = at("relu", [2, 384], tmp(0))
        sqr = at("sqr", [2, 384], tmp(1))
        ss_x = at("ss_x", [T], tmp(2))
        yout = at("yout", [NT, D], off_act)

        pos = [off_c]

        def const(name, shape, dt=F32):
            n = 4
            for s in shape:
                n *= s
            t = at(name, shape, pos[0], dt)
            pos[0] += (n + 31) // 32 * 32
            return t

        off_ws = pos[0]
        wsT = const("wsT", [HEADS, CHUNK])
        off_w64 = pos[0]
        ws64 = const("ws64", [HEADS, NB, TB])
        off_bs = pos[0]
        mix_b = const("mix_b", [JB, CHUNK])
        off_gate = pos[0]
        gate_w = const("gate_w", [2, JB, P])
        ident = const("ident", [P])
        ada_late = const("ada_late", [N_ADA - ADA_EARLY, NC])
        silu = at("silu", [KD, NC], pos[0] - (N_ADA - ADA_EARLY) * NC * 4)
        gain_f = const("gain_f", [KD, NC])
        off_ring = pos[0]
        ada_ring = const("ada_ring", [4, PIECE])
        ada_lo = at("ada_lo", [4, PIECE], off_ring, F32R)
        ada_hi = at("ada_hi", [2, PIECE], off_w + 4096, F32R)
        ada_e_hi = at("ada_e_hi", [2, 2 * PIECE], off_ring, F32R)
        early_hi = lambda u: ada_e_hi[:, u % 4, :] if u % 4 < 2 else (w_hi if u % 4 == 2 else w_lo)[:, 1, :]
        r5 = const("r5", [JB, R512])
        r10 = const("r10", [KD, R1024])
        bada = const("bada", [N_ADA])
        silu2 = const("silu2", [KD, 2 * NC], F32R)
        sel = const("sel", [NC])
        tails = const("tails", [JB, TAILS])
        bn = const("bn", [NT, 6])
        mv = const("mv", [NT, 2])
        v_std = const("v_std", [NT])
        ssq = const("ssq", [NT])
        std = const("std", [NT])
        rstd = const("rstd", [NT])
        ones = const("ones", [1])
        eps = const("eps", [1])
        lam = at("lam", [8, JB], tmp(4))
        decays = const("decays", [2, JB])
        decay, decay_n = decays[:, 0, :], decays[:, 1, :]
        assert pos[0] <= nc.sbuf_usable_end, (pos[0], nc.sbuf_usable_end)
        pieces = at("pieces", [PIECE], off_w64)
        PB, PE_ROWS = 64, 64 + 2 * NC
        tmp1 = at("tmp1", [2, 384], off_ws)
        smp1 = at("smp1", [KD, T_SAMPLE], off_w64)
        smp_acc = at("smp_acc", [KD, T_SAMPLE], off_bs)
        g_fin = at("g_fin", [D], off_gate)
        smp_t = at("smp_t", [T_SAMPLE], off_ws + 3072)
        tails_out = at("tails_out", [D_RG], off_w64)

        full = [sem(f"bank{b}_full") for b in range(8)]
        free = [sem(f"bank{b}_free") for b in range(8)]
        raw_in = [sem(f"raw_in{s}") for s in range(2)]
        hi_done = [sem(f"hi_done{s}") for s in range(2)]
        lo_done = [sem(f"lo_done{s}") for s in range(2)]
        ada_in = [sem(f"ada_in{s}") for s in range(4)]
        ada_hi_done = sem("ada_hi_done")
        ada_lo_pool = sem("ada_lo_pool")
        ada_lo_dve = sem("ada_lo_dve")
        ada_hi_read = sem("ada_hi_read")
        ada_lo_read = sem("ada_lo_read")
        x_in = [sem(f"x_in{t}") for t in range(NT)]
        ada_w_in = [sem(f"ada_w_in{u}") for u in range(E_UNITS)]
        rows1024_in = sem("rows1024_in")
        rows512_in = sem("rows512_in")
        ws_in = sem("ws_in")
        bs_in = sem("bs_in")
        gates_in = sem("gates_in")
        gfin_in = sem("gfin_in")
        stored = sem("stored")
        tails_stored = sem("tails_stored")
        vrows_out = sem("vrows_out")
        pool_set = sem("pool_set")
        x_sq = sem("x_sq")
        hm_mod = sem("hm_mod")
        hm_hi = sem("hm_hi")
        hm_ready = sem("hm_ready")
        hms_step = sem("hms_step")
        hms_hi = sem("hms_hi")
        hms_ready = sem("hms_ready")
        norm_tmp = sem("norm_tmp")
        norm_hi = sem("norm_hi")
        act_ready = sem("act_ready")
        smp_step = sem("smp_step")
        eye_ready = sem("eye_ready")
        silu_step = sem("silu_step")
        silu_ready = sem("silu_ready")
        piece_turned = sem("piece_turned")
        lam_exp = sem("lam_exp")
        lam_step = sem("lam_step")
        ada_ready = sem("ada_ready")
        mixb_ready = sem("mixb_ready")
        std_done = sem("std_done")
        rstd_done = sem("rstd_done")
        halo_done = sem("halo_done")
        tap_done = sem("tap_done")
        row_read = sem("row_read")
        ix_done = sem("ix_done")
        decay_done = sem("decay_done")
        act_chain = sem("act_chain")
        q_done = sem("q_done")
        root_done = sem("root_done")
        term_done = sem("term_done")
        scan_done = sem("scan_done")
        rg_done = sem("rg_done")
        h_tail = sem("h_tail")
        v_stat = sem("v_stat")
        v_std_done = sem("v_std_done")
        v_norm = sem("v_norm")
        mix_done = sem("mix_done")
        rgsq = sem("rgsq")
        rgsum = sem("rgsum")
        sgsq = sem("sgsq")
        sgsum = sem("sgsum")
        rg_norm = sem("rg_norm")
        mrg_hi = sem("mrg_hi")
        mrg_ready = sem("mrg_ready")
        sg_norm = sem("sg_norm")
        msg_hi = sem("msg_hi")
        msg_ready = sem("msg_ready")
        x1_smp = sem("x1_smp")
        x1sq = sem("x1sq")
        x1sum = sem("x1sum")
        relu_done = sem("relu_done")
        hhi_done = sem("hhi_done")
        h_ready = sem("h_ready")
        smp_zero = sem("smp_zero")
        y_smp = sem("y_smp")
        ysq = sem("ysq")
        ysum = sem("ysum")

        def cols(t, g):
            c, n = GROUPS[g]
            return t[:, c:c + n] if len(t.shape) == 2 else t[:, :, c:c + n]

        def blk(t, k, g, n=None):
            c, m = GROUPS[g]
            return t[:, k, c:c + (m if n is None else n)]

        def smp(t, start, n):
            at0 = min(start, seg0)
            return t[:, at0:at0 + NB * SEG].rearrange("p (b x) -> p b x", x=SEG)[:, :, start - at0:start - at0 + n]

        def by_sample(t):
            return t.rearrange("p (b t) -> p b t", t=TB)

        f32 = lambda view: view.bitcast(F32)
        row_tok = HALO
        seg0 = HALO + T_PROMPT
        tile_rows = lambda t: min(P, T - t * P)

        def claim(pe, name):
            bank, turn = USE[name]
            if turn > 0:
                pe.wait_ge(free[bank], turn)
            return psum[bank]

        def when_full(eng, name):
            bank, turn = USE[name]
            eng.wait_ge(full[bank], turn + 1)
            return psum[bank]

        def when_read(eng, name):
            bank, turn = USE[name]
            eng.wait_ge(free[bank], turn + 1)

        raw_slot = lambda n: n % 2 if n < 2 or n >= U_OUT_A else 0

        def wait_lo(eng, n):
            eng.wait_ge(lo_done[n % 2], n // 2 + 1)

        def wait_ada_lo_read(eng, m):
            if m % KD == KD - 1:
                when_full(eng, ("ap", m // KD))
            else:
                eng.wait_ge(ada_lo_read, m + 1 - m // KD)

        def slot_units(i):
            if i not in PIECE_OF:
                return []
            n = 2 * UNIT_SLOTS.index(i)
            return [n, n + 1]

        full_of = lambda name: full[USE[name][0]]
        free_of = lambda name: free[USE[name][0]]

        x_p = a["x_prompt"].rearrange("a t d -> (a t) d")
        x_s = a["x_sample"].rearrange("b t d -> (b t) d")
        w_in_v = a["w_in"][0].rearrange("(k p) n -> p k n", p=P)
        w_out_v = a["w_out"][0].rearrange("(k p) n -> p k n", p=P)
        w_ff1_v = a["w_ff1"][0].rearrange("(k p) n -> p k n", p=P)
        w_ff2_v = a["w_ff2"][0].rearrange("(k p) n -> p k n", p=P)
        w_ada_v = a["w_ada"][0].rearrange("(k p) n -> p k n", p=P)

        unit_cols = [2 * D_RG + D_SG + P * j for j in range(JB)]
        for j in range(JB):
            unit_cols += [P * j, D_RG + P * j]
        unit_cols += [2 * D_RG + P * j for j in range(JB)]

        block = ctx.enter_context(nc.Block())

        @block.sync
        def _(sp):
            for t in range(NT):
                src = x_p[P * t:P * t + P] if t < NT - 1 else x_s
                sp.dma_start(xin[0:tile_rows(t), t, :], src).then_inc(x_in[t], 16)

            def unit(s, half, src, shape_k):
                if not (isinstance(half, int) and half == 0):
                    sp.wait_ge(lo_done[s], half)
                sp.dma_start(w_raw[:, s, :].rearrange("p (k n) -> p k n", k=shape_k), src).then_inc(raw_in[s], 16)

            def in_unit(n):
                if n == 2:
                    wait_lo(sp, 0)
                elif n > 2:
                    wait_lo(sp, n - 1)
                sp.dma_start(w_raw[:, raw_slot(n), :].rearrange("p (k n) -> p k n", k=KD),
                             w_in_v[:, :, unit_cols[n]:unit_cols[n] + P]).then_inc(raw_in[n % 2], 16)

            def late_unit(m):
                if m < 4:
                    when_full(sp, "ada1")
                else:
                    wait_ada_lo_read(sp, m - 4)
                c = ADA_EARLY * P + PIECE * (m // KD)
                sp.dma_start(ada_ring[:, m % 4, :], w_ada_v[:, m % KD, c:c + PIECE]).then_inc(ada_in[m % 4], 16)

            for u in range(E_UNITS):
                if u == E_UNITS - 2:
                    in_unit(0)
                k, c = u % (KD // 2) * 2, u // (KD // 2) * PIECE
                sp.dma_start(ada_w[:, u, :].rearrange("p (k n) -> p k n", k=2), w_ada_v[:, k:k + 2, c:c + PIECE]
                             ).then_inc(ada_w_in[u], 16)
            in_unit(1)
            order = [(3 * (n - 2) + 0.5, 0, in_unit, n) for n in range(2, U_OUT_A)]
            order += [(UNIT_SLOTS[(m - 4) // 2] + 0.9 if m >= 4 else 0, 1, late_unit, m) for m in range(L_UNITS)]
            for _, _, load, n in sorted(order, key=lambda e: (e[0], e[1], e[3])):
                load(n)
            when_read(sp, ("gi", JB - 1, 2))
            sp.dma_start(g_fin[:], a["g_final"].partition_broadcast(P)).then_inc(gfin_in, 16)
            for n in range(U_OUT_A, U_FF):
                o = (n - U_OUT_A) % KD
                if n == U_OUT_A:
                    wait_lo(sp, n - 1)
                if n == U_OUT_A + 1:
                    when_full(sp, ("ap", L_PIECES - 1))
                unit(n % 2, n // 2, w_out_v[:, :, P * o:P * o + P], KD)

            def ff1_units(b):
                for c in range(2):
                    unit(c, ff1_half(b), w_ff1_v[:, :, bass.ds(256 * b + P * c, P)], KD)

            def ff2_units(b):
                for h in range(2):
                    unit(h, ff2_half(b), w_ff2_v[:, bass.ds(2 * b, 2), 512 * h:512 * h + 512], 2)

            ff1_units(0)
            with sp.Fori(0, FF_BLOCKS - 1) as b:
                ff1_units(b + 1)
                ff2_units(b)
            ff2_units(FF_BLOCKS - 1)
            yp, ys = out[0].rearrange("a t d -> (a t) d"), out[1].rearrange("b t d -> (b t) d")
            for t in range(NT):
                when_read(sp, ("y", t, 1))
                dst = yp[P * t:P * t + P] if t < NT - 1 else ys
                sp.dma_start(dst, yout[0:tile_rows(t), t, :]).then_inc(stored, 16)
            sp.wait_ge(stored, 16 * NT)
            sp.wait_ge(tails_stored, 64)

        @block.gpsimd
        def _(pool):
            g = nc.gpsimd
            g.memset(gate_w[:], 0.0).then_inc(pool_set, 1)
            g.memset(ident[:], 0.0).then_inc(pool_set, 1)
            g.memset(ones[:], 1.0).then_inc(pool_set, 1)
            g.memset(ones64[:], 1.0).then_inc(pool_set, 1)
            g.memset(eps[:], EPS).then_inc(pool_set, 1)
            g.memset(own[0:64], 1.0).then_inc(pool_set, 1)
            pool.wait_ge(pool_set, 6)
            g.affine_select(out=ident[:], in_=ident[:], compare_op=ALU.not_equal, fill=1.0, base=0,
                            pattern=[[-1, P]], channel_multiplier=1).then_inc(pool_set, 1)
            g.affine_select(out=own[0:64], in_=own[0:64], compare_op=ALU.is_ge, fill=0.0, base=0,
                            pattern=[[-TB, NB]], channel_multiplier=1).then_inc(pool_set, 1)
            pool.wait_ge(pool_set, 8)
            g.affine_select(out=own[0:64], in_=own[0:64], compare_op=ALU.is_ge, fill=0.0, base=TB - 1,
                            pattern=[[TB, NB]], channel_multiplier=-1).then_inc(pool_set, 1)
            loads = [
                (R_STATE, NB * HALO, a["state_conv"][0].rearrange("b t d -> (b t) d")),
                (R_H0, NB, a["state_rglru"][0]), (R_CW, CONV_W, a["conv_w"][0]), (R_CB, 1, a["conv_b"]),
                (R_BRA, 1, a["b_ra"].rearrange("l h d -> l (h d)")),
                (R_BRI, 1, a["b_ri"].rearrange("l h d -> l (h d)")),
                (R_LRU, 1, a["lru_l"]), (R_LNG, 1, a["ln_v_g"]), (R_LNB, 1, a["ln_v_b"]),
                (R_GRG, 1, a["g_rg"]), (R_GSG, 1, a["g_sg"]),
            ]
            assert len(loads) == N_ROW_LOADS
            pool.dma_start(ws_raw[:], a["w_s"][0].rearrange("h t s -> t h s")).then_inc(ws_in, 16)
            for r, n, src in loads:
                pool.dma_start(rows512[r:r + n, :], src).then_inc(rows512_in, 16)
            for e in range(2):
                pool.dma_start(mix_b[HD * e:HD * e + HD, :, :],
                               a["b_s"][0].rearrange("(j e) t -> e j t", e=2)[e].partition_broadcast(HD)
                               ).then_inc(bs_in, 16)
            for i, name in enumerate(("w_ra", "w_ri")):
                for e in range(2):
                    pool.dma_start(gate_w[HD * e:HD * e + HD, i, :, HD * e:HD * e + HD],
                                   a[name][0].rearrange("(j e) i o -> e i j o", e=2)[e]).then_inc(gates_in, 16)
            pool.wait_ge(ws_in, 16)
            g.affine_select(out=ws_raw[:], in_=ws_raw[:], compare_op=ALU.is_ge, fill=0.0, base=0,
                            pattern=[[0, HEADS], [-1, CHUNK]], channel_multiplier=1).then_inc(pool_set, 1)

            for u in range(0, E_UNITS, 2):
                pool.wait_ge(ada_hi_done, u + 1)
                g.tensor_tensor(ada_w_lo[:, u, :], ada_w[:, u, :], f32(early_hi(u)), ALU.subtract
                                ).then_inc(ada_lo_pool, 1)
            pool.wait_ge(hi_done[0], 1)
            g.tensor_tensor(w_lo[:, 0, :], w_raw[:, 0, :], f32(w_hi[:, 0, :]), ALU.subtract).then_inc(lo_done[0], 1)

            def late_lo(i):
                for m in slot_units(i):
                    pool.wait_ge(ada_hi_done, E_UNITS + m + 1)
                    g.tensor_tensor(ada_lo[:, m % 4, :], ada_ring[:, m % 4, :], f32(ada_hi[:, m % 2, :]),
                                    ALU.subtract).then_inc(ada_lo_pool, 1)

            pool.wait_ge(ada_ready, 1)
            for gi in range(3):
                when_read(pool, ("bcx", gi))
            view = xn[:, :, T_PROMPT:T].rearrange("p k (b t) -> p k b t", t=TB)
            for q, (m, op) in enumerate(((gain_m, ALU.mult), (ada_e[:, 0:KD], ALU.add))):
                if q > 0:
                    pool.wait_ge(hms_step, q)
                g.tensor_tensor(view, view, m[:, :, 1:NC].unsqueeze(3).to_broadcast([P, KD, NB, TB]), op
                                ).then_inc(hms_step, 1)
            pool.wait_ge(hms_hi, 1)
            g.tensor_tensor(act_lo[:, :, T_PROMPT:T], xn[:, :, T_PROMPT:T], f32(act_hi[:, :, T_PROMPT:T]),
                            ALU.subtract).then_inc(hms_ready, 1)

            for i in range(13):
                late_lo(i)
            for j in range(JB):
                if j == 0:
                    when_read(pool, "rows512")
                    when_read(pool, "rowsum")
                else:
                    pool.wait_ge(term_done, j)
                if j == 0:
                    for i in range(13, 15):
                        late_lo(i)
                g.memset(row[:, 0:HALO], 0.0).then_inc(halo_done, 1)
                g.tensor_copy(smp(row, seg0, HALO),
                              r5[:, j, R_STATE:R_STATE + NB * HALO].rearrange("p (b x) -> p b x", x=HALO)
                              ).then_inc(halo_done, 1)
                when_read(pool, ("xr", j, 2))
                g.tensor_copy(tails[:, j, 0:HALO], row[:, T_PROMPT:T_PROMPT + HALO])
                g.tensor_copy(tails[:, j, HALO:HALO + NB * HALO].rearrange("p (b x) -> p b x", x=HALO),
                              smp(row, seg0 + TB, HALO)).then_inc(row_read, 1)
                for i in range(15 + 6 * j, 21 + 6 * j) if j < JB - 1 else range(33, 39):
                    late_lo(i)
                when_read(pool, ("gi", j, 2))
                g.tensor_tensor(ig[:, 0:SCAN_W], ig[:, 0:SCAN_W], xc[:, 0:SCAN_W], ALU.mult).then_inc(ix_done, 1)
                if j == 2:
                    when_read(pool, ("vt", NT - 1))
                    pool.dma_start(out[4][0, 0].rearrange("t (j d) -> t j d", j=JB), V[:, :, P * 7:P * 8]).then_inc(vrows_out, 16)
                    pool.dma_start(out[7][0].rearrange("b t (j d) -> (b t) j d", j=JB), V[0:64, :, P * 8:P * 9]
                                   ).then_inc(vrows_out, 16)
                pool.wait_ge(scan_done, 3 * j + 3)
                c = HALO + NB * HALO
                g.tensor_copy(tails[:, j, c:c + 1], rr[:, T_PROMPT - 1:T_PROMPT])
                g.tensor_copy(tails[:, j, c + 1:c + 1 + NB],
                              smp(rr, seg0 + TB - 1, 1).rearrange("p b x -> p (b x)")).then_inc(h_tail, 1)
            pool.wait_ge(vrows_out, 32)
            when_read(pool, ("mix", JB - 1, 2))
            g.memset(smp_acc[:], 0.0).then_inc(smp_zero, 1)
            pool.wait_ge(h_tail, JB)
            for j in range(1, JB):
                pool.wait_ge(rgsq, j + 1)
                if j > 1:
                    pool.wait_ge(rgsum, j - 1)
                g.tensor_tensor(ss_rg[:], sq_rg[:, 0, 0:T] if j == 1 else ss_rg[:],
                                sq_rg[:, j % 2, 0:T], ALU.add).then_inc(rgsum, 1)
                late_lo(38 + j)
            for i in range(42, LAST_TURN):
                late_lo(i)
            for gi in range(3):
                for j in range(JB):
                    pool.wait_ge(mrg_hi, JB * gi + j + 1)
                    g.tensor_tensor(blk(act_lo, j, gi), blk(RG, j, gi), f32(blk(act_hi, j, gi)),
                                    ALU.subtract).then_inc(mrg_ready, 1)
            when_read(pool, "tails")
            n1, n2 = HALO, HALO + NB * HALO
            pool.dma_start(out[2][0, 0], tails_out[0:n1, :]).then_inc(tails_stored, 16)
            pool.dma_start(out[5][0].rearrange("b t d -> (b t) d"), tails_out[n1:n2, :]).then_inc(tails_stored, 16)
            pool.dma_start(out[3][0], tails_out[n2:n2 + 1, :]).then_inc(tails_stored, 16)
            pool.dma_start(out[6][0], tails_out[n2 + 1:n2 + 1 + NB, :]).then_inc(tails_stored, 16)

            def hidden_lo(b, pair):
                for c in range(2):
                    for gi in range(3):
                        item = 3 * c + gi
                        n = GROUPS[gi][1]
                        bank = 3 * c + gi
                        pool.wait_ge(free[bank], ff1_turn(b) + 1)
                        pool.wait_ge(hhi_done, 6 * b + item + 1)
                        s = 2 * pair + c
                        g.tensor_tensor(blk(h_lo, s, gi), sqr[:, item % 2, 0:n], f32(blk(h_hi, s, gi)),
                                        ALU.subtract).then_inc(h_ready, 1)

            hidden_lo(0, 0)
            with pool.Fori(0, (FF_BLOCKS - 2) // 2) as m:
                hidden_lo(2 * m + 1, 1)
                hidden_lo(2 * m + 2, 0)
            hidden_lo(FF_BLOCKS - 1, 1)

        SCALE_NO = {"x": 1, "rg": 2, ("sg", 0): 3, ("sg", 1): 4, ("sg", 2): 5,
                    ("x1", 0): 6, ("x1", 1): 7, ("x1", 2): 8, ("y", 0): 9, ("y", 1): 10, ("y", 2): 11}

        def by_rows(tiles):
            whole = [t for t in tiles if tile_rows(t) == P]
            parts = [(P, whole[0], whole[-1] + 1)]
            if NT - 1 in tiles:
                parts.append((tile_rows(NT - 1), NT - 1, NT))
            return parts

        @block.tensor
        def _(pe):
            mm = nc.tensor.matmul

            def turn(dst, src, rows=P):
                return nc.tensor.transpose(dst, src, ident[0:rows, 0:rows])

            def early_rows():
                pe.wait_ge(rows1024_in, 16 * N_EARLY_LOADS)
                bank = claim(pe, "rows1024")
                for k in range(KD):
                    turn(bank[:, R1024 * k:R1024 * k + R1024], rows1024[0:R1024, P * k:P * k + P], R1024)
                turn(bank[:, P:P + N_ADA], bada_rows[0:N_ADA, :], N_ADA).then_inc(full_of("rows1024"), 1)

            pe.wait_ge(pool_set, 7)
            for t in range(NT):
                if t == 3:
                    early_rows()
                pe.wait_ge(x_in[t], 16)
                r = tile_rows(t)
                for h in range(2):
                    bank = claim(pe, ("x", t, h))
                    for i in range(4):
                        k = 4 * h + i
                        last = turn(bank[:, r * i:r * i + r], xin[0:r, t, P * k:P * k + P], r)
                    last.then_inc(full_of(("x", t, h)), 1)

            def spread_scale(name, scale, tiles):
                pe.wait_ge(rstd_done, SCALE_NO[scale])
                bank = claim(pe, name)
                for i, t in enumerate(tiles):
                    r = tile_rows(t)
                    last = turn(bank[:, P * i:P * i + r], rstd[0:r, t:t + 1].to_broadcast([r, P]), r)
                last.then_inc(full_of(name), 1)

            def sum_squares(name, squares, tiles):
                bank = claim(pe, name)
                for t in tiles:
                    r = tile_rows(t)
                    last = mm(bank[0:r, t:t + 1], squares[:, P * t:P * t + r], ones[:, :], start=True, stop=True)
                last.then_inc(full_of(name), 1)

            def small_rows():
                pe.wait_ge(rows512_in, 16 * N_ROW_LOADS)
                bank = claim(pe, "rows512")
                for j in range(JB):
                    last = turn(bank[:, R512 * j:R512 * j + R512], rows512[0:R512, P * j:P * j + P], R512)
                last.then_inc(full_of("rows512"), 1)

            def mixing_weights(half):
                pe.wait_ge(pool_set, 10)
                bank = claim(pe, f"ws{half}")
                for h in range(4):
                    last = turn(bank[:, CHUNK * h:CHUNK * h + CHUNK], ws_raw[:, 4 * half + h, :])
                last.then_inc(full_of(f"ws{half}"), 1)

            def mixing_corner():
                when_read(pe, "ws0")
                when_read(pe, "ws1")
                pe.wait_ge(eye_ready, 2)
                bank = claim(pe, "wsmall")
                mm(bank[0:64, 0:64], eye8[0:TB].rearrange("p b s -> p (b s)"), wsT[0:TB, :, 0:TB],
                   start=True, stop=True).then_inc(full_of("wsmall"), 1)

            def mixing_row_sums():
                bank = claim(pe, "rowsum")
                for h in range(HEADS):
                    e = h % 2
                    last = mm(bank[HD * e:HD * e + HD, CHUNK * (h // 2):CHUNK * (h // 2) + CHUNK], ones64[:, :],
                              wsT[:, h, :], start=True, stop=True)
                last.then_inc(full_of("rowsum"), 1)

            def turn_piece(bank, c0):
                for i in range(PIECE // P):
                    last = mm(bank[:, NC * (c0 + i):NC * (c0 + i) + NC], pieces[PB:PE_ROWS, P * i:P * i + P],
                              sel[PB:PE_ROWS, :], start=True, stop=True)
                return last

            for g in range(3):
                spread_scale(("bcx", g), "x", TILES_OF[g])

            pe.wait_ge(silu_ready, 1)
            pe.wait_ge(eye_ready, 2)
            ada1_bank = claim(pe, "ada1")
            for u in range(E_UNITS):
                p, q = u // (KD // 2), u % (KD // 2)
                if q == 0:
                    bank = claim(pe, ("ap_early", p))
                pe.wait_ge(ada_lo_dve if u % 2 else ada_lo_pool, u // 2 + 1)
                for part in range(2):
                    src = early_hi(u) if part == 0 else ada_w_lo[:, u, :]
                    for k in range(2):
                        last = mm(bank[0:2 * NC, 0:PIECE], silu2[:, 2 * q + k, :], src[:, PIECE * k:PIECE * k + PIECE],
                                  start=(q == 0 and part == 0 and k == 0), stop=(q == KD // 2 - 1 and part == 1 and k == 1))
                    if part == 0:
                        last.then_inc(ada_hi_read, 1)
                if q == KD // 2 - 1:
                    last.then_inc(full_of(("ap_early", p)), 1)
                if q == 0 and p > 0:
                    when_read(pe, ("ap_early", p - 1))
                    turn_piece(ada1_bank, PIECE // P * (p - 1)).then_inc(piece_turned, 1)
            when_read(pe, ("ap_early", E_PIECES - 1))
            turn_piece(ada1_bank, PIECE // P * (E_PIECES - 1)).then_inc(full_of("ada1"), 1)

            def split_product(bank, n, w, rhs, k, first, final):
                mm(bank[:, 0:n], w(w_hi), rhs(act_hi if rhs_act[0] else h_hi), start=first, stop=False)
                mm(bank[:, 0:n], w(w_hi), rhs(act_lo if rhs_act[0] else h_lo), start=False, stop=False)
                return mm(bank[:, 0:n], w(w_lo), rhs(act_hi if rhs_act[0] else h_hi), start=False, stop=final)

            rhs_act = [True]

            def project(bank, s, g, wait_k=None):
                c, n = GROUPS[g]
                for k in range(KD):
                    if wait_k:
                        wait_k(k)
                    last = split_product(bank, n, lambda t: t[:, s, P * k:P * k + P],
                                         lambda t: t[:, k, c:c + n], k, k == 0, k == KD - 1)
                return last

            slots = [0]

            def slot():
                i = slots[0]
                slots[0] += 1
                if i in FIRST_SLOT and i > FIRST_SLOT[0] or i == LAST_TURN:
                    p = FIRST_SLOT.index(i) - 1 if i in FIRST_SLOT else L_PIECES - 1
                    when_read(pe, ("ap", p))
                    turn_piece(claim(pe, ("turned", p)), 0).then_inc(full_of(("turned", p)), 1)
                if i in FIRST_SLOT:
                    claim(pe, ("ap", PIECE_OF[i]))
                for m in slot_units(i):
                    p, k = m // KD, m % KD
                    bank = psum[USE["ap", p][0]]
                    pe.wait_ge(ada_lo_pool, E_UNITS // 2 + m + 1)
                    mm(bank[0:2 * NC, 0:PIECE], silu2[:, k, :], ada_hi[:, m % 2, :], start=(k == 0), stop=False
                       ).then_inc(ada_hi_read, 1)
                    mm(bank[0:2 * NC, 0:PIECE], silu2[:, k, :], ada_lo[:, m % 4, :], start=False, stop=(k == KD - 1)
                       ).then_inc(full_of(("ap", p)) if k == KD - 1 else ada_lo_read, 1)
                if i == ROWS_SLOT:
                    small_rows()
                if i in WS_SLOTS:
                    mixing_weights(WS_SLOTS.index(i))
                if i == SMALL_SLOT:
                    mixing_corner()
                if i == ROWSUM_SLOT:
                    mixing_row_sums()

            def v_by_token(t):
                bank = claim(pe, ("vt", t))
                r = tile_rows(t)
                for j in range(JB):
                    last = turn(bank[0:r, P * j:P * j + P], V[:, j, P * t:P * t + r])
                last.then_inc(full_of(("vt", t)), 1)

            def in_tile(name, j, n, after=()):
                pe.wait_ge(lo_done[n % 2], n // 2 + 1)
                for g in range(3):
                    bank = claim(pe, (name, j, g))
                    project(bank, n % 2, g).then_inc(full_of((name, j, g)), 1)
                    for f in after[g:g + 1]:
                        f()

            for g in range(3):
                for j in range(2):
                    wait_k = None
                    if j == 0:
                        wait_k = lambda k: pe.wait_ge(hm_ready, KD * g + k + 1)
                    if j == 0 and g == 2:
                        pe.wait_ge(hms_ready, 1)
                    if g == 0:
                        pe.wait_ge(lo_done[j], 1)
                    project(claim(pe, ("v", j, g)), j, g, wait_k).then_inc(full_of(("v", j, g)), 1)
                    slot()
            for j in range(2, JB):
                in_tile("v", j, U_V + j, [slot] * 3)
            for j in range(JB):
                def after_group(g, yg, j=j):
                    slot()
                    if j < 3 and not yg and g == 2:
                        v_by_token(3 * j)
                    if j < 3 and yg and g > 0:
                        v_by_token(3 * j + g)
                if j == 0:
                    for jj in range(2, JB):
                        for g in range(3):
                            when_read(pe, ("v", jj, g))
                in_tile("xr", j, U_RG + 2 * j, [lambda g=g: after_group(g, False) for g in range(3)])
                in_tile("yg", j, U_RG + 2 * j + 1, [lambda g=g: after_group(g, True) for g in range(3)])
                if j == JB - 1:
                    pe.wait_ge(v_norm, NT + 2)
                    for jj in range(JB):
                        for g in range(2):
                            bank = claim(pe, ("mix", jj, g))
                            for c in range(4):
                                for e in range(2):
                                    col = P * (4 * g + c) + HD * e
                                    last = mm(bank[HD * e:HD * e + HD, P * c:P * c + P], V[:, jj, col:col + HD],
                                              wsT[:, 2 * jj + e, :], start=True, stop=True)
                            last.then_inc(full_of(("mix", jj, g)), 1)
                        bank = claim(pe, ("mix", jj, 2))
                        for e in range(2):
                            col = P * (NT - 1) + HD * e
                            last = mm(bank[HD * e:HD * e + HD, 0:T_SAMPLE], V[0:T_SAMPLE, jj, col:col + HD],
                                      ws64[0:T_SAMPLE, 2 * jj + e].rearrange("p b t -> p (b t)"),
                                      start=True, stop=True)
                        last.then_inc(full_of(("mix", jj, 2)), 1)
                if j == 0:
                    pe.wait_ge(gates_in, 64)
                pe.wait_ge(tap_done, 4 * j + 4)
                for i, name in enumerate(("gr", "gi")):
                    for g, (c, n) in enumerate(SCAN_GROUPS):
                        bank = claim(pe, (name, j, g))
                        mm(bank[:, 0:n], gate_w[:, i, j, :], xc[:, c:c + n],
                           start=True, stop=True).then_inc(full_of((name, j, g)), 1)

            for j in range(JB - 1):
                in_tile("u", j, U_U + j, [slot] * 3)
            pe.wait_ge(rgsum, JB - 1)
            sum_squares("ss_rg", ss_rg, range(NT))

            def sum_sg(g):
                pe.wait_ge(sgsum, 3 * (JB - 2) + g + 1)
                sum_squares(("ss_sg", g), ss_sg, TILES_OF[g])

            def after_u0():
                spread_scale(("bcrg", 0), "rg", TILES_OF[0])
                spread_scale(("bcrg", 1), "rg", TILES_OF[1])

            def after_u1():
                sum_sg(0)
                spread_scale(("bcrg", 2), "rg", TILES_OF[2])

            in_tile("u", JB - 1, U_U + JB - 1, [after_u0, after_u1])
            spread_scale(("bcsg", 0), ("sg", 0), TILES_OF[0])
            sum_sg(1)

            def out_group(n, o, g):
                def wait_k(k):
                    if k < JB:
                        pe.wait_ge(mrg_ready, JB * g + k + 1)
                    else:
                        pe.wait_ge(msg_ready, JB * g + k - JB + 1)
                pe.wait_ge(lo_done[n % 2], n // 2 + 1)
                bank = claim(pe, ("out", o, g))
                project(bank, n % 2, g, wait_k if o == 0 else None).then_inc(full_of(("out", o, g)), 1)

            for o in range(KD):
                out_group(U_OUT_A + o, o, 0)
                if o == 0:
                    spread_scale(("bcsg", 1), ("sg", 1), TILES_OF[1])
                    sum_sg(2)
                out_group(U_OUT_A + o, o, 1)
                if o == 0:
                    spread_scale(("bcsg", 2), ("sg", 2), TILES_OF[2])
                    pe.wait_ge(h_tail, JB)
                    bank = claim(pe, "tails")
                    for j in range(JB):
                        last = turn(bank[0:TAILS, P * j:P * j + P], tails[:, j, :])
                    last.then_inc(full_of("tails"), 1)
            for o in range(KD):
                out_group(U_OUT_B + o, o, 2)
                if o == 0:
                    pe.wait_ge(x1sum, 2 * (KD - 1))
                    sum_squares(("ss_x1", 0), ss_x, TILES_OF[0])
                if o == 1:
                    spread_scale(("bcx1", 0), ("x1", 0), TILES_OF[0])
                    sum_squares(("ss_x1", 1), ss_x, TILES_OF[1])
                if o == 4:
                    spread_scale(("bcx1", 1), ("x1", 1), TILES_OF[1])

            def hidden(b, first=False):
                rhs_act[0] = True
                for c in range(2):
                    pe.wait_ge(lo_done[c], ff1_half(b) + 1)
                    for g in range(3):
                        wait_k = None
                        if first and c == 0:
                            wait_k = lambda k: pe.wait_ge(act_ready, KD * g + k + 1 + (g == 2))
                        pe.wait_ge(free[3 * c + g], ff1_turn(b))
                        project(psum[3 * c + g], c, g, wait_k).then_inc(full[3 * c + g], 1)
                        if first and c == 0 and g == 0:
                            pe.wait_ge(x1sum, 3 * (KD - 1))
                            sum_squares(("ss_x1", 2), ss_x, TILES_OF[2])
                        if first and c == 0 and g == 1:
                            spread_scale(("bcx1", 2), ("x1", 2), TILES_OF[2])

            def back(b, pair):
                rhs_act[0] = False
                for h in range(2):
                    pe.wait_ge(lo_done[h], ff2_half(b) + 1)
                    for i in range(4):
                        o = 4 * h + i
                        for g, (c, n) in enumerate(GROUPS):
                            bank = 3 * (o % 2) + g
                            if o == 0:
                                pe.wait_ge(h_ready, 6 * b + 3 + g + 1)
                            pe.wait_ge(free[bank], ff2_turn(b) + o // 2)
                            for k in range(2):
                                last = split_product(psum[bank], n, lambda t: t[:, h, 512 * k + P * i:512 * k + P * i + P],
                                                     lambda t: t[:, 2 * pair + k, c:c + n], k, k == 0, k == 1)
                            last.then_inc(full[bank], 1)

            hidden(0, first=True)
            with pe.Fori(0, (FF_BLOCKS - 2) // 2) as m:
                hidden(2 * m + 1)
                back(2 * m, 0)
                hidden(2 * m + 2)
                back(2 * m + 1, 1)
            hidden(FF_BLOCKS - 1)
            back(FF_BLOCKS - 2, 0)
            back(FF_BLOCKS - 1, 1)

            for g in range(3):
                pe.wait_ge(ysum, 3 * (KD - 2) + g + 1)
                sum_squares(("ss_y", g), ss_x, TILES_OF[g])
            for t in range(NT):
                r = tile_rows(t)
                for h in range(2):
                    bank = claim(pe, ("y", t, h))
                    for i in range(4):
                        last = turn(bank[0:r, P * i:P * i + P], xT[:, 4 * h + i, P * t:P * t + r])
                    last.then_inc(full_of(("y", t, h)), 1)

        @block.scalar
        def _(act):
            s = nc.scalar

            loads = [
                (rows1024[R_C:R_C + 1, :], a["c_prompt"]), (rows1024[R_C + 1:R_C + NC, :], a["c_sample"]),
                (rows1024[R_GMIX:R_GMIX + 1, :], a["g_mix"]), (rows1024[R_GFFN:R_GFFN + 1, :], a["g_ffn"]),
                (bada_rows[0:N_ADA, :], a["b_ada"][0].rearrange("(m p) -> m p", p=P)),
            ]
            assert len(loads) == N_EARLY_LOADS
            for dst, src in loads:
                act.dma_start(dst, src).then_inc(rows1024_in, 16)

            for t in range(NT):
                r = tile_rows(t)
                act.wait_ge(x_in[t], 16)
                if t > 0:
                    act.wait_ge(x_sq, t)
                s.activation(w_lo[0:r, 1, :], xin[0:r, t, :], ACT.Square, accum_out=ssq[0:r, t:t + 1]).then_inc(x_sq, 1)
                bank = when_full(act, ("x", t, 1))
                s.activation(xT[:, 4:8, P * t:P * t + r], bank[:, 0:4 * r].rearrange("p (k c) -> p k c", k=4),
                             ACT.Copy).then_inc(free_of(("x", t, 1)), 1)
                if t == 4:
                    when_read(act, "rows1024")
                    s.activation(silu[:], r10[:, :, R_C:R_C + NC], ACT.Sigmoid).then_inc(silu_step, 1)
                if t == 7:
                    act.wait_ge(silu_step, 2)
                    s.activation(silu2[:, :, 0:NC], silu[:], ACT.Copy).then_inc(silu_step, 1)

            def root(name, scale, tiles, d):
                bank = when_full(act, name)
                if SCALE_NO[scale] > 1:
                    act.wait_ge(rstd_done, SCALE_NO[scale] - 1)
                parts = by_rows(tiles)
                for i, (r, t0, t1) in enumerate(parts):
                    ins = s.activation(std[0:r, t0:t1], bank[0:r, t0:t1], ACT.Sqrt, bias=eps[0:r, :], scale=1.0 / d)
                ins.then_inc(free_of(name), 1)

            def split_hi(slot, half, src_read, raw=None):
                act.wait_ge(raw_in[slot], 16 * (half + 1))
                if src_read is not None:
                    act.wait_ge(*src_read)
                s.activation(w_hi[:, slot, :], w_raw[:, slot if raw is None else raw, :], ACT.Copy
                             ).then_inc(hi_done[slot], 1)

            def full_at(name):
                bank, turn = USE[name]
                return full[bank], turn + 1

            act.wait_ge(x_sq, NT)
            act.wait_ge(pool_set, 5)
            for r, t0, t1 in by_rows(range(NT)):
                ins = s.activation(std[0:r, t0:t1], ssq[0:r, t0:t1], ACT.Sqrt, bias=eps[0:r, :], scale=1.0 / D)
            ins.then_inc(std_done, 1)

            def piece_out(name, read):
                bank = when_full(act, name)
                if read is not None:
                    act.wait_ge(*read)
                s.activation(pieces[PB:PE_ROWS, :], bank[0:2 * NC, 0:PIECE], ACT.Copy).then_inc(free_of(name), 1)

            for u in range(E_UNITS):
                if u == E_UNITS - 2:
                    split_hi(0, 0, None)
                act.wait_ge(ada_w_in[u], 16)
                if u >= 4:
                    act.wait_ge(ada_hi_read, u - 3)
                s.activation(early_hi(u), ada_w[:, u, :], ACT.Copy).then_inc(ada_hi_done, 1)
                if u % 4 == 1 and u > 4:
                    p = u // 4 - 1
                    piece_out(("ap_early", p), (piece_turned, p) if p > 0 else None)
            piece_out(("ap_early", E_PIECES - 1), (piece_turned, E_PIECES - 1))

            def late_hi(m):
                act.wait_ge(ada_in[m % 4], 16 * (m // 4 + 1))
                if m < 2:
                    wait_lo(act, 1)
                else:
                    act.wait_ge(ada_hi_read, E_UNITS + m - 1)
                s.activation(ada_hi[:, m % 2, :], ada_ring[:, m % 4, :], ACT.Copy).then_inc(ada_hi_done, 1)

            slots = [0]

            def slot():
                i = slots[0]
                slots[0] += 1
                if i in FIRST_SLOT and i > FIRST_SLOT[0] or i == LAST_TURN:
                    p = FIRST_SLOT.index(i) - 1 if i in FIRST_SLOT else L_PIECES - 1
                    bank = when_full(act, ("turned", p))
                    c = PIECE // P
                    s.activation(ada_late[:, c * p:c * p + c, :], bank[:, 0:c * NC].rearrange("p (m c) -> p m c", c=NC),
                                 ACT.Copy).then_inc(free_of(("turned", p)), 1)
                for m in slot_units(i):
                    if m + 2 < L_UNITS:
                        late_hi(m + 2)
                if i in LAST_SLOT:
                    p = LAST_SLOT.index(i)
                    piece_out(("ap", p), full_at(("turned", p - 1)) if p > 0 else None)

            for i in range(HM_ITEMS):
                g, k = i // KD, i % KD
                if i == 2:
                    split_hi(1, 0, full_at("ada1"))
                if i == KD:
                    act.wait_ge(hms_step, 2)
                    s.activation(act_hi[:, :, T_PROMPT:T], xn[:, :, T_PROMPT:T], ACT.Copy).then_inc(hms_hi, 1)
                act.wait_ge(hm_mod, i + 1)
                n = GROUPS[g][1] if g < 2 else PROMPT_G2
                s.activation(blk(act_hi, k, g, n), blk(xn, k, g, n), ACT.Copy).then_inc(hm_hi, 1)

            def norm_hi_items(n0, n1, shift, smp_buf, tmp_buf):
                for i in range(n0, n1):
                    act.wait_ge(norm_tmp, i + 1)
                    if i == 2 * KD:
                        s.activation(act_hi[:, :, T_PROMPT:T], smp_buf[:, :, :], ACT.Copy).then_inc(norm_hi, 1)
                        continue
                    g, k = (i // KD, i % KD) if i < 2 * KD else (2, i - 2 * KD - 1)
                    n = GROUPS[g][1] if g < 2 else PROMPT_G2
                    s.activation(blk(act_hi, k, g, n), tmp_buf[:, i % 2, 0:n], ACT.Identity,
                                 bias=shift[:, k, 0:1]).then_inc(norm_hi, 1)

            late_hi(0)
            late_hi(1)

            act.wait_ge(hm_ready, HM_ITEMS)
            act.wait_ge(hms_ready, 1)

            def v_out(j, g):
                bank = when_full(act, ("v", j, g))
                s.activation(blk(V, j, g), bank[:, 0:GROUPS[g][1]], ACT.Copy).then_inc(free_of(("v", j, g)), 1)
                slot()

            def split_in(n, src):
                split_hi(n % 2, n // 2, full_at(src), raw_slot(n))

            for g in range(3):
                for j in range(2):
                    v_out(j, g)
                    if g == 2:
                        split_in(j + 2, ("v", j, 2))
            for j in range(2, JB):
                for g in range(3):
                    v_out(j, g)
                split_in(j + 2, ("v", j, 2))
            act.wait_ge(lam_step, 1)
            s.activation(lam[:, 1, :], lam[:, 0, :], ACT.Exp, scale=-1.0).then_inc(lam_exp, 1)

            def v_copy(t):
                bank = when_full(act, ("vt", t))
                r = tile_rows(t)
                s.activation(V[0:r, :, P * t:P * t + P], bank[0:r, :].rearrange("p (j d) -> p j d", j=JB),
                             ACT.Copy).then_inc(free_of(("vt", t)), 1)

            for j in range(JB):
                if j > 0:
                    act.wait_ge(term_done, j)
                for g in range(2):
                    bank = when_full(act, ("xr", j, g))
                    c, n = GROUPS[g]
                    s.activation(row[:, row_tok + c:row_tok + c + n], bank[:, 0:n], ACT.Copy
                                 ).then_inc(free_of(("xr", j, g)), 1)
                    slot()
                bank = when_full(act, ("xr", j, 2))
                c = row_tok + GROUPS[2][0]
                s.activation(row[:, c:c + PROMPT_G2], bank[:, 0:PROMPT_G2], ACT.Copy)
                s.activation(smp(row, seg0 + HALO, TB), by_sample(bank[:, PROMPT_G2:PROMPT_G2 + T_SAMPLE]), ACT.Copy
                             ).then_inc(free_of(("xr", j, 2)), 1)
                slot()
                split_in(U_RG + 2 * j + 2, ("xr", j, 2))
                when_read(act, ("xr", j, 2))
                act.wait_ge(halo_done, 2 * j + 2)
                if j > 0:
                    act.wait_ge(ix_done, j)
                s.activation(xc[:, 0:SCAN_W], row[:, 0:SCAN_W], ACT.Identity, bias=r5[:, j, R_CB:R_CB + 1],
                             scale=r5[:, j, R_CW:R_CW + 1]).then_inc(tap_done, 1)
                if j < 3:
                    v_copy(3 * j)
                for g in range(3):
                    bank = when_full(act, ("yg", j, g))
                    s.activation(blk(RG, j, g), bank[:, 0:GROUPS[g][1]], ACT.Gelu_apprx_tanh
                                 ).then_inc(free_of(("yg", j, g)), 1)
                    slot()
                    if j < 3 and g > 0:
                        v_copy(3 * j + g)
                split_in(U_RG + 2 * j + 3, ("yg", j, 2))
                if j > 0:
                    act.wait_ge(rg_done, j)
                    act.wait_ge(h_tail, j)
                for name, dst, bias in (("gr", rr, R_BRA), ("gi", ig, R_BRI)):
                    for g, (c, n) in enumerate(SCAN_GROUPS):
                        bank = when_full(act, (name, j, g))
                        s.activation(dst[:, c:c + n], bank[:, 0:n], ACT.Sigmoid, bias=r5[:, j, bias:bias + 1]
                                     ).then_inc(free_of((name, j, g)), 1)
                when_read(act, ("gr", j, 2))
                act.wait_ge(lam_step, LAM_STEPS)
                s.activation(aa[:, 0:SCAN_W], rr[:, 0:SCAN_W], ACT.Exp, scale=decay[:, j:j + 1]).then_inc(decay_done, 1)
                act.wait_ge(decay_done, j + 1)
                s.activation(rr[:, 0:SCAN_W], rr[:, 0:SCAN_W], ACT.Tanh, scale=decay_n[:, j:j + 1]).then_inc(act_chain, 1)
                act.wait_ge(row_read, j + 1)
                act.wait_ge(tap_done, 4 * j + 4)
                s.activation(row[:, 0:SCAN_W], aa[:, 0:SCAN_W], ACT.Square).then_inc(act_chain, 1)
                act.wait_ge(q_done, j + 1)
                s.activation(row[:, 0:SCAN_W], row[:, 0:SCAN_W], ACT.Sqrt).then_inc(root_done, 1)
                if j == 2:
                    act.wait_ge(v_stat, 2 * NT)
                    for r, t0, t1 in by_rows(range(NT)):
                        s.activation(v_std[0:r, t0:t1], mv[0:r, t0:t1, 1], ACT.Sqrt, bias=eps[0:r, :]
                                     ).then_inc(v_std_done, 1)

            def rg_square(j):
                if j >= 2:
                    act.wait_ge(rgsum, 1)
                s.activation(sq_rg[:, j % 2, 0:T], RG[:, j, :], ACT.Square).then_inc(rgsq, 1)

            def sg_square(j, g):
                i = 3 * j + g
                when_read(act, ("u", j, g))
                if i >= 5:
                    act.wait_ge(sgsum, i - 4)
                n = GROUPS[g][1]
                s.activation(cols(ss_sg, g) if j == 0 else sq_g[:, i % 2, 0:n], blk(V, j, g), ACT.Square
                             ).then_inc(sgsq, 1)

            def branch_hi(g):
                act.wait_ge(*full_at(("u", JB - 1, g)))
                for j in range(JB):
                    act.wait_ge(rg_norm, JB * g + j + 1)
                    s.activation(blk(act_hi, j, g), blk(RG, j, g), ACT.Copy).then_inc(mrg_hi, 1)

            def gate_hi(g):
                for j in range(JB):
                    act.wait_ge(sg_norm, JB * g + j + 1)
                    s.activation(blk(act_hi, JB + j, g), blk(V, j, g), ACT.Copy).then_inc(msg_hi, 1)

            act.wait_ge(rg_done, JB)
            act.wait_ge(h_tail, JB)
            rg_square(0)
            rg_square(1)
            for j in range(JB - 1):
                for g in range(3):
                    sg_square(j, g)
                    slot()
                if j == 0:
                    rg_square(2)
                    rg_square(3)
                split_in(U_U + j + 2, ("u", j, 2))
            root("ss_rg", "rg", range(NT), D_RG)
            sg_square(3, 0)
            branch_hi(0)
            sg_square(3, 1)
            root(("ss_sg", 0), ("sg", 0), TILES_OF[0], D_SG)
            branch_hi(1)
            sg_square(3, 2)
            branch_hi(2)
            n = U_OUT_A + 1
            split_hi(n % 2, n // 2, full_at(("u", 3, 2)))
            gate_hi(0)
            root(("ss_sg", 1), ("sg", 1), TILES_OF[1], D_SG)
            gate_hi(1)
            root(("ss_sg", 2), ("sg", 2), TILES_OF[2], D_SG)
            gate_hi(2)
            bank = when_full(act, "tails")
            s.activation(tails_out[0:TAILS, :], bank[0:TAILS, :], ACT.Copy).then_inc(free_of("tails"), 1)

            def x1_square(o, g):
                i = 2 * o + g
                if g < 2:
                    when_read(act, ("out", o, g))
                    if i >= 4:
                        act.wait_ge(x1sum, i - 3)
                    slot = i % 2
                else:
                    act.wait_ge(x1_smp, o + 1)
                    act.wait_ge(x1sum, max(2 * (KD - 1), 2 * (KD - 1) + o - 2))
                    slot = o % 2
                n = GROUPS[g][1]
                s.activation(cols(ss_x, g) if o == 0 else sq_g[:, slot, 0:n], blk(xT, o, g), ACT.Square
                             ).then_inc(x1sq, 1)

            hf = lambda n0, n1: norm_hi_items(n0, n1, ada_late[:, KD:2 * KD], smp1, tmp1)
            for o in range(KD):
                x1_square(o, 0)
                x1_square(o, 1)
                n = U_OUT_A + o + 2
                split_hi(n % 2, n // 2, full_at(("out", o, 1)))
            for o in range(KD):
                x1_square(o, 2)
                n = U_OUT_B + o + 2
                split_hi(n % 2, n // 2, full_at(("out", o, 2)))
                if o == 0:
                    root(("ss_x1", 0), ("x1", 0), TILES_OF[0], D)
                if o == 1:
                    root(("ss_x1", 1), ("x1", 1), TILES_OF[1], D)
                hf(HF_AT[o], HF_AT[o + 1])
            root(("ss_x1", 2), ("x1", 2), TILES_OF[2], D)
            hf(2 * KD, NORM_ITEMS)

            def hidden_hi(b, pair, next_unit=None, first=False):
                for c in range(2):
                    for g in range(3):
                        i = 3 * c + g
                        n = GROUPS[g][1]
                        bank = 3 * c + g
                        act.wait_ge(full[bank], ff1_turn(b) + 1)
                        if not (first and i < 2):
                            act.wait_ge(h_ready, 6 * b + i - 1)
                        s.activation(relu[:, i % 2, 0:n], psum[bank][:, 0:n], ACT.Relu).then_inc(relu_done, 1)
                        act.wait_ge(relu_done, 6 * b + i + 1)
                        s.activation(blk(h_hi, 2 * pair + c, g), relu[:, i % 2, 0:n], ACT.Square).then_inc(hhi_done, 1)
                    if next_unit is not None:
                        split_hi(c, next_unit, (full[3 * c + 2], ff1_turn(b) + 1))

            def back_hi(b, next_unit):
                for h in range(2):
                    if next_unit is not None:
                        split_hi(h, next_unit, (full[5], ff2_turn(b) + 2 * h + 2))

            hidden_hi(0, 0, ff1_half(1), first=True)
            with act.Fori(0, (FF_BLOCKS - 2) // 2) as m:
                hidden_hi(2 * m + 1, 1, ff2_half(2 * m))
                back_hi(2 * m, ff1_half(2 * m + 2))
                hidden_hi(2 * m + 2, 0, ff2_half(2 * m + 1))
                back_hi(2 * m + 1, ff1_half(2 * m + 3))
            hidden_hi(FF_BLOCKS - 1, 1, ff2_half(FF_BLOCKS - 2))
            back_hi(FF_BLOCKS - 2, ff2_half(FF_BLOCKS - 1))

            for o in range(KD):
                for g in range(3):
                    i = 3 * o + g
                    if g < 2:
                        act.wait_ge(free[3 * (o % 2) + g], ff2_turn(FF_BLOCKS - 1) + o // 2 + 1)
                    else:
                        act.wait_ge(y_smp, 2 * o + 2)
                    if i >= 5:
                        act.wait_ge(ysum, i - 4)
                    n = GROUPS[g][1]
                    s.activation(cols(ss_x, g) if o == 0 else sq_g[:, i % 2, 0:n], blk(xT, o, g), ACT.Square
                                 ).then_inc(ysq, 1)
            for g in range(3):
                root(("ss_y", g), ("y", g), TILES_OF[g], D)

        @block.vector
        def _(dve):
            v = nc.vector

            for t in range(NT):
                if t == 3:
                    bank = when_full(dve, "rows1024")
                    v.tensor_copy(bada[:], bank[:, P:P + N_ADA])
                    v.tensor_copy(r10[:], bank[:, 0:KD * R1024].rearrange("p (k r) -> p k r", k=KD)
                                  ).then_inc(free_of("rows1024"), 1)
                if t == 4:
                    dve.wait_ge(pool_set, 9)
                    v.tensor_copy(eye8[0:TB], ident[0:TB, 0:TB].unsqueeze(1).to_broadcast([TB, NB, TB])
                                  ).then_inc(eye_ready, 1)
                    v.tensor_tensor(sel[PB:PE_ROWS, :], ident[PB:PE_ROWS, PB:PB + NC], ident[PB:PE_ROWS, PB + NC:PB + 2 * NC],
                                    ALU.add).then_inc(eye_ready, 1)
                r = tile_rows(t)
                bank = when_full(dve, ("x", t, 0))
                v.tensor_copy(xT[:, 0:4, P * t:P * t + r], bank[:, 0:4 * r].rearrange("p (k c) -> p k c", k=4)
                              ).then_inc(free_of(("x", t, 0)), 1)
                if t == 6:
                    dve.wait_ge(silu_step, 1)
                    v.tensor_tensor(silu[:], silu[:], r10[:, :, R_C:R_C + NC], ALU.mult).then_inc(silu_step, 1)
            dve.wait_ge(silu_step, 3)
            v.tensor_tensor(silu2[:, :, NC:2 * NC], silu[:], f32(silu2[:, :, 0:NC]), ALU.subtract
                            ).then_inc(silu_ready, 1)

            def inverse(scale, tiles):
                for i, (r, t0, t1) in enumerate(by_rows(tiles)):
                    ins = v.reciprocal(rstd[0:r, t0:t1], std[0:r, t0:t1])
                ins.then_inc(rstd_done, 1)

            dve.wait_ge(std_done, 1)
            inverse("x", range(NT))

            when_read(dve, ("x", NT - 1, 0))
            when_read(dve, ("x", NT - 1, 1))
            early_los = iter(range(1, E_UNITS, 2))
            for g in range(3):
                bank = when_full(dve, ("bcx", g))
                for k in range(KD):
                    ins = v.tensor_tensor(blk(xn, k, g), blk(xT, k, g), bank[:, 0:GROUPS[g][1]], ALU.mult)
                    if k == KD - 1:
                        ins.then_inc(free_of(("bcx", g)), 1)
                    if (KD * g + k) % 3 == 2:
                        u = next(early_los)
                        dve.wait_ge(ada_hi_done, u + 1)
                        v.tensor_tensor(ada_w_lo[:, u, :], ada_w[:, u, :], f32(early_hi(u)), ALU.subtract
                                        ).then_inc(ada_lo_dve, 1)

            def split_lo(slot, half, raw=None):
                dve.wait_ge(hi_done[slot], half + 1)
                v.tensor_tensor(w_lo[:, slot, :], w_raw[:, slot if raw is None else raw, :], f32(w_hi[:, slot, :]),
                                ALU.subtract).then_inc(lo_done[slot], 1)

            def split_in(n):
                split_lo(n % 2, n // 2, raw_slot(n))

            bank = when_full(dve, "ada1")
            v.tensor_tensor(ada_e[:], bank[:, 0:ADA_EARLY * NC].rearrange("p (m c) -> p m c", c=NC),
                            bada[:, 0:ADA_EARLY].unsqueeze(2).to_broadcast([P, ADA_EARLY, NC]), ALU.add
                            ).then_inc(free_of("ada1"), 1)
            when_read(dve, "ada1")
            v.scalar_tensor_tensor(gain_m[:], ada_e[:, KD:2 * KD], 1.0,
                                   r10[:, :, R_GMIX:R_GMIX + 1].to_broadcast([P, KD, NC]), ALU.add, ALU.mult
                                   ).then_inc(ada_ready, 1)
            dve.wait_ge(ada_ready, 1)

            def release(name, done, count):
                dve.wait_ge(done, count)
                dve.sem_inc(free_of(name), 1)

            pending = [None]

            def norm_items(n0, n1, spread, gain, shift, smp_buf, tmp_buf):
                def lower(i):
                    dve.wait_ge(norm_hi, i + 1)
                    if i == 2 * KD:
                        v.tensor_tensor(act_lo[:, :, T_PROMPT:T], smp_buf[:, :, :], f32(act_hi[:, :, T_PROMPT:T]),
                                        ALU.subtract).then_inc(act_ready, 1)
                        return
                    g, k = (i // KD, i % KD) if i < 2 * KD else (2, i - 2 * KD - 1)
                    n = GROUPS[g][1] if g < 2 else PROMPT_G2
                    v.scalar_tensor_tensor(blk(act_lo, k, g, n), tmp_buf[:, i % 2, 0:n], shift[:, k, 0:1],
                                           f32(blk(act_hi, k, g, n)), ALU.add, ALU.subtract).then_inc(act_ready, 1)

                for i in range(n0, n1):
                    if i in (0, KD, 2 * KD):
                        when_read(dve, ("ss_x1", i // KD))
                        inverse(("x1", i // KD), TILES_OF[i // KD])
                    if i == 2 * KD:
                        bank = when_full(dve, (spread, 2))
                        dve.wait_ge(tails_stored, 64)
                        sc = bank[:, PROMPT_G2:PROMPT_G2 + T_SAMPLE]
                        v.tensor_tensor(smp_buf[:], xT[:, :, T_PROMPT:T],
                                        sc.unsqueeze(1).to_broadcast([P, KD, T_SAMPLE]), ALU.mult
                                        ).then_inc(smp_step, 1)
                        for q, (m, op) in enumerate(((gain, ALU.mult), (shift, ALU.add))):
                            dve.wait_ge(smp_step, q + 1)
                            view = smp_buf[:].rearrange("p k (b t) -> p k b t", t=TB)
                            ins = v.tensor_tensor(view, view, m[:, :, 1:NC].unsqueeze(3).to_broadcast([P, KD, NB, TB]), op)
                            ins.then_inc(smp_step if q == 0 else norm_tmp, 1)
                    else:
                        g, k = (i // KD, i % KD) if i < 2 * KD else (2, i - 2 * KD - 1)
                        n = GROUPS[g][1] if g < 2 else PROMPT_G2
                        bank = when_full(dve, (spread, g))
                        if i >= 2:
                            dve.wait_ge(act_ready, i - 1)
                        v.scalar_tensor_tensor(tmp_buf[:, i % 2, 0:n], blk(xT, k, g, n), gain[:, k, 0:1],
                                               bank[:, 0:n], ALU.mult, ALU.mult).then_inc(norm_tmp, 1)
                    if pending[0] is not None:
                        lower(pending[0])
                    pending[0] = i
                    if i in (KD - 1, 2 * KD - 1, NORM_ITEMS - 1):
                        lower(i)
                        pending[0] = None
                        g = {KD - 1: 0, 2 * KD - 1: 1, NORM_ITEMS - 1: 2}[i]
                        release((spread, g), act_ready, i + 1)
                if pending[0] is not None:
                    lower(pending[0])
                    pending[0] = None

            def lower_hm(i):
                g, k = i // KD, i % KD
                n = GROUPS[g][1] if g < 2 else PROMPT_G2
                dve.wait_ge(hm_hi, i + 1)
                v.tensor_tensor(blk(act_lo, k, g, n), blk(xn, k, g, n), f32(blk(act_hi, k, g, n)), ALU.subtract
                                ).then_inc(hm_ready, 1)

            for g in range(3):
                when_read(dve, ("bcx", g))
            for i in range(HM_ITEMS):
                g, k = i // KD, i % KD
                n = GROUPS[g][1] if g < 2 else PROMPT_G2
                v.tensor_scalar(blk(xn, k, g, n), blk(xn, k, g, n), gain_m[:, k, 0:1], ada_e[:, k, 0:1],
                                ALU.mult, ALU.add).then_inc(hm_mod, 1)
                if i > 0:
                    lower_hm(i - 1)
                if i == 3:
                    split_lo(1, 0)
            lower_hm(HM_ITEMS - 1)
            split_in(2)
            split_in(3)

            bank = when_full(dve, "rows512")
            v.tensor_copy(r5[:], bank[:, 0:JB * R512].rearrange("p (j r) -> p j r", j=JB)
                          ).then_inc(free_of("rows512"), 1)
            when_read(dve, "rows512")
            raw_l = r5[:, :, R_LRU]
            v.scalar_tensor_tensor(lam[:, 0, :], raw_l, -1.0, raw_l, ALU.mult, ALU.max).then_inc(lam_step, 1)
            for half in range(2):
                bank = when_full(dve, f"ws{half}")
                v.tensor_copy(wsT[:, 4 * half:4 * half + 4], bank[:].rearrange("p (h t) -> p h t", h=4)
                              ).then_inc(free_of(f"ws{half}"), 1)
            split_in(4)
            bank = when_full(dve, "wsmall")
            small = bank[0:64, 0:64].rearrange("p (h t) -> p h t", h=HEADS).unsqueeze(2).to_broadcast([64, HEADS, NB, TB])
            mask = own[0:64].unsqueeze(1).unsqueeze(3).to_broadcast([64, HEADS, NB, TB])
            v.tensor_tensor(ws64[0:64], small, mask, ALU.mult).then_inc(free_of("wsmall"), 1)
            bank = when_full(dve, "rowsum")
            dve.wait_ge(bs_in, 32)
            for j in range(JB):
                ins = v.scalar_tensor_tensor(mix_b[:, j, :], bank[:, CHUNK * j:CHUNK * j + CHUNK],
                                             r5[:, j, R_LNB:R_LNB + 1], mix_b[:, j, :], ALU.mult, ALU.add)
            ins.then_inc(free_of("rowsum"), 1)
            split_in(5)

            steps = [1]

            def step(ins):
                steps[0] += 1
                ins.then_inc(lam_step, 1)
                dve.wait_ge(lam_step, steps[0])

            u, num, s1, s2, ser, low = (lam[:, i, :] for i in (1, 2, 3, 4, 5, 6))
            dve.wait_ge(lam_exp, 1)
            step(v.tensor_scalar(num, u, 2.0, None, ALU.add))
            step(v.reciprocal(num, num))
            step(v.tensor_tensor(s1, u, num, ALU.mult))
            step(v.tensor_tensor(s2, s1, s1, ALU.mult))
            step(v.tensor_scalar(ser, s2, 1.0 / 17.0, None, ALU.mult))
            for d in (15, 13, 11, 9, 7, 5, 3):
                step(v.scalar_tensor_tensor(ser, ser, 1.0 / d, s2, ALU.add, ALU.mult))
            step(v.scalar_tensor_tensor(ser, ser, 1.0, s1, ALU.add, ALU.mult))
            step(v.tensor_scalar(low, raw_l, 0.0, None, ALU.min))
            step(v.scalar_tensor_tensor(low, ser, -2.0, low, ALU.mult, ALU.add))
            step(v.tensor_scalar(decay[:], low, LRU_C, None, ALU.mult))
            step(v.tensor_scalar(decay_n[:], low, -LRU_C, None, ALU.mult))
            assert steps[0] == LAM_STEPS


            def v_stats(t):
                when_read(dve, ("vt", t))
                r = tile_rows(t)
                v.bn_stats(bn[0:r, t, :], V[0:r, :, P * t:P * t + P]).then_inc(v_stat, 1)
                dve.wait_ge(v_stat, 2 * t + 1)
                v.bn_aggr(mv[0:r, t, :], bn[0:r, t, :]).then_inc(v_stat, 1)

            for j in range(JB):
                split_in(U_RG + 2 * j + 2)
                for k in range(1, CONV_W):
                    dve.wait_ge(tap_done, 4 * j + k)
                    v.scalar_tensor_tensor(xc[:, 0:SCAN_W], row[:, k:k + SCAN_W], r5[:, j, R_CW + k:R_CW + k + 1],
                                           xc[:, 0:SCAN_W], ALU.mult, ALU.add).then_inc(tap_done, 1)
                if j < 3:
                    for i in range(3):
                        v_stats(3 * j + i)
                else:
                    dve.wait_ge(v_std_done, 2)
                    for r, t0, t1 in by_rows(range(NT)):
                        v.reciprocal(v_std[0:r, t0:t1], v_std[0:r, t0:t1]).then_inc(v_norm, 1)
                    dve.wait_ge(v_norm, 2)
                    dve.wait_ge(vrows_out, 32)
                    for t in range(NT):
                        r = tile_rows(t)
                        v.tensor_scalar(V[0:r, :, P * t:P * t + P], V[0:r, :, P * t:P * t + P], mv[0:r, t, 0:1],
                                        v_std[0:r, t:t + 1], ALU.subtract, ALU.mult).then_inc(v_norm, 1)
                split_in(U_RG + 2 * j + 3)
                if j == JB - 1:
                    for jj in range(JB):
                        gain = r5[:, jj, R_LNG:R_LNG + 1]
                        for g in range(2):
                            bank = when_full(dve, ("mix", jj, g))
                            v.scalar_tensor_tensor(
                                V[:, jj, 512 * g:512 * g + 512].rearrange("p (c t) -> p c t", t=CHUNK),
                                bank[:].rearrange("p (c t) -> p c t", t=CHUNK), gain,
                                mix_b[:, jj, :].unsqueeze(1).to_broadcast([P, 4, CHUNK]), ALU.mult, ALU.add
                            ).then_inc(free_of(("mix", jj, g)), 1)
                        bank = when_full(dve, ("mix", jj, 2))
                        v.scalar_tensor_tensor(
                            by_sample(V[:, jj, T_PROMPT:T]), by_sample(bank[:, 0:T_SAMPLE]), gain,
                            mix_b[:, jj, 0:TB].unsqueeze(1).to_broadcast([P, NB, TB]), ALU.mult, ALU.add
                        ).then_inc(free_of(("mix", jj, 2)), 1)
                dve.wait_ge(act_chain, 2 * j + 2)
                v.scalar_tensor_tensor(row[:, 0:SCAN_W], row[:, 0:SCAN_W], 1.0, rr[:, 0:SCAN_W],
                                       ALU.add, ALU.mult).then_inc(q_done, 1)
                dve.wait_ge(root_done, j + 1)
                dve.wait_ge(ix_done, j + 1)
                v.tensor_tensor(ig[:, 1:SCAN_W], row[:, 1:SCAN_W], ig[:, 1:SCAN_W], ALU.mult).then_inc(term_done, 1)
                v.memset(smp(aa, seg0 - 1, 1), 0.0).then_inc(scan_done, 1)
                dve.wait_ge(term_done, j + 1)
                v.tensor_copy(smp(ig, seg0 - 1, 1), r5[:, j, R_H0:R_H0 + NB].unsqueeze(2)).then_inc(scan_done, 1)
                dve.wait_ge(scan_done, 3 * j + 2)
                v.tensor_tensor_scan(rr[:, 0:SCAN_W], aa[:, 0:SCAN_W], ig[:, 0:SCAN_W], 0.0, ALU.mult, ALU.add
                                     ).then_inc(scan_done, 1)
                dve.wait_ge(scan_done, 3 * j + 3)
                when_read(dve, ("yg", j, 2))
                v.tensor_tensor(RG[:, j, 0:T_PROMPT], RG[:, j, 0:T_PROMPT], rr[:, 0:T_PROMPT], ALU.mult)
                v.tensor_tensor(by_sample(RG[:, j, T_PROMPT:T]), by_sample(RG[:, j, T_PROMPT:T]), smp(rr, seg0, TB),
                                ALU.mult).then_inc(rg_done, 1)

            def gate(j, g):
                bank = when_full(dve, ("u", j, g))
                v.tensor_tensor(blk(V, j, g), bank[:, 0:GROUPS[g][1]], blk(V, j, g), ALU.mult
                                ).then_inc(free_of(("u", j, g)), 1)

            def add_sg(i):
                g = i % 3
                dve.wait_ge(sgsq, i + 1)
                if i < 3:
                    return
                if i >= 6:
                    dve.wait_ge(sgsum, i - 5)
                v.tensor_tensor(cols(ss_sg, g), cols(ss_sg, g), sq_g[:, i % 2, 0:GROUPS[g][1]], ALU.add
                                ).then_inc(sgsum, 1)

            for j in range(JB - 1):
                for g in range(3):
                    gate(j, g)
                    if 3 * j + g > 0:
                        add_sg(3 * j + g - 1)
                split_in(U_U + j + 2)
            add_sg(3 * (JB - 1) - 1)
            when_read(dve, ("turned", L_PIECES - 1))
            v.tensor_tensor(ada_late[:], ada_late[:], bada[:, ADA_EARLY:N_ADA].unsqueeze(2)
                            .to_broadcast([P, N_ADA - ADA_EARLY, NC]), ALU.add).then_inc(ada_ready, 1)
            dve.wait_ge(ada_ready, 2)
            v.scalar_tensor_tensor(gain_f[:], ada_late[:, 2 * KD:3 * KD], 1.0,
                                   r10[:, :, R_GFFN:R_GFFN + 1].to_broadcast([P, KD, NC]), ALU.add, ALU.mult
                                   ).then_inc(ada_ready, 1)
            when_read(dve, "ss_rg")
            inverse("rg", range(NT))

            def norm_rg(g):
                bank = when_full(dve, ("bcrg", g))
                for j in range(JB):
                    v.scalar_tensor_tensor(blk(RG, j, g), blk(RG, j, g), r5[:, j, R_GRG:R_GRG + 1],
                                           bank[:, 0:GROUPS[g][1]], ALU.mult, ALU.mult).then_inc(rg_norm, 1)
                release(("bcrg", g), rg_norm, JB * (g + 1))

            def norm_sg(g):
                when_read(dve, ("ss_sg", g))

                def lower(j):
                    dve.wait_ge(msg_hi, JB * g + j + 1)
                    v.tensor_tensor(blk(act_lo, JB + j, g), blk(V, j, g), f32(blk(act_hi, JB + j, g)), ALU.subtract
                                    ).then_inc(msg_ready, 1)

                bank = when_full(dve, ("bcsg", g))
                for j in range(JB):
                    v.scalar_tensor_tensor(blk(V, j, g), blk(V, j, g), r5[:, j, R_GSG:R_GSG + 1],
                                           bank[:, 0:GROUPS[g][1]], ALU.mult, ALU.mult).then_inc(sg_norm, 1)
                    if j > 0:
                        lower(j - 1)
                lower(JB - 1)
                release(("bcsg", g), sg_norm, JB * (g + 1))

            for g in range(3):
                gate(JB - 1, g)
                add_sg(3 * (JB - 1) + g)
                norm_rg(g)
                if g == 1:
                    when_read(dve, ("ss_sg", 0))
                    inverse(("sg", 0), TILES_OF[0])
            n = U_OUT_A + 1
            split_lo(n % 2, n // 2)
            for g in range(3):
                if g > 0:
                    when_read(dve, ("ss_sg", g))
                    inverse(("sg", g), TILES_OF[g])
                norm_sg(g)

            def add_out(o, g):
                gt = ada_late[:, o, :]
                bank = when_full(dve, ("out", o, g))
                n = GROUPS[g][1] if g < 2 else PROMPT_G2
                ins = v.scalar_tensor_tensor(blk(xT, o, g, n), bank[:, 0:n], gt[:, 0:1], blk(xT, o, g, n),
                                             ALU.mult, ALU.add)
                if g < 2:
                    ins.then_inc(free_of(("out", o, g)), 1)
                    return
                if o > 0:
                    dve.wait_ge(x1_smp, o)
                v.tensor_tensor(by_sample(smp_t[:]), by_sample(bank[:, PROMPT_G2:PROMPT_G2 + T_SAMPLE]),
                                gt[:, 1:NC].unsqueeze(2).to_broadcast([P, NB, TB]), ALU.mult
                                ).then_inc(free_of(("out", o, 2)), 1)
                when_read(dve, ("out", o, 2))
                v.tensor_tensor(xT[:, o, T_PROMPT:T], xT[:, o, T_PROMPT:T], smp_t[:], ALU.add).then_inc(x1_smp, 1)

            def add_x1(o, g):
                if o == 0:
                    return
                if g < 2:
                    i = 2 * o + g
                    dve.wait_ge(x1sq, i + 1)
                    if o >= 2:
                        dve.wait_ge(x1sum, i - 3)
                    slot = i % 2
                else:
                    dve.wait_ge(x1sq, 2 * KD + o + 1)
                    if o >= 2:
                        dve.wait_ge(x1sum, 2 * (KD - 1) + o - 1)
                    slot = o % 2
                v.tensor_tensor(cols(ss_x, g), cols(ss_x, g), sq_g[:, slot, 0:GROUPS[g][1]], ALU.add).then_inc(x1sum, 1)

            hf = lambda n0, n1: norm_items(n0, n1, "bcx1", gain_f[:], ada_late[:, KD:2 * KD], smp1, tmp1)
            for o in range(KD):
                add_out(o, 0)
                if o > 0:
                    add_x1(o - 1, 1)
                add_out(o, 1)
                add_x1(o, 0)
                n = U_OUT_A + o + 2
                split_lo(n % 2, n // 2)
            add_x1(KD - 1, 1)
            for o in range(KD):
                add_out(o, 2)
                n = U_OUT_B + o + 2
                split_lo(n % 2, n // 2)
                add_x1(o, 2)
                hf(HF_AT[o], HF_AT[o + 1])
            hf(2 * KD, NORM_ITEMS)

            def hidden_square(b, next_unit=None, first=False):
                for c in range(2):
                    for g in range(3):
                        i = 3 * c + g
                        n = GROUPS[g][1]
                        bank = 3 * c + g
                        dve.wait_ge(relu_done, 6 * b + i + 1)
                        if not (first and i < 2):
                            dve.wait_ge(h_ready, 6 * b + i - 1)
                        v.scalar_tensor_tensor(sqr[:, i % 2, 0:n], psum[bank][:, 0:n], 0.0, relu[:, i % 2, 0:n],
                                               ALU.max, ALU.mult).then_inc(free[bank], 1)
                    if next_unit is not None:
                        split_lo(c, next_unit)

            def add_back(b, o, g):
                bank = 3 * (o % 2) + g
                dve.wait_ge(full[bank], ff2_turn(b) + o // 2 + 1)
                n = GROUPS[g][1] if g < 2 else PROMPT_G2
                ins = v.scalar_tensor_tensor(blk(xT, o, g, n), psum[bank][:, 0:n], ada_late[:, 3 * KD + o, 0:1],
                                             blk(xT, o, g, n), ALU.mult, ALU.add)
                if g == 2:
                    ins = v.tensor_tensor(smp_acc[:, o, :], smp_acc[:, o, :],
                                          psum[bank][:, PROMPT_G2:PROMPT_G2 + T_SAMPLE], ALU.add)
                ins.then_inc(free[bank], 1)

            def back_add(b, next_unit):
                for h in range(2):
                    for i in range(4):
                        for g in range(3):
                            add_back(b, 4 * h + i, g)
                    split_lo(h, next_unit)

            dve.wait_ge(smp_zero, 1)
            hidden_square(0, ff1_half(1), first=True)
            with dve.Fori(0, (FF_BLOCKS - 2) // 2) as m:
                hidden_square(2 * m + 1, ff2_half(2 * m))
                back_add(2 * m, ff1_half(2 * m + 2))
                hidden_square(2 * m + 2, ff2_half(2 * m + 1))
                back_add(2 * m + 1, ff1_half(2 * m + 3))
            hidden_square(FF_BLOCKS - 1, ff2_half(FF_BLOCKS - 2))
            back_add(FF_BLOCKS - 2, ff2_half(FF_BLOCKS - 1))

            def add_y(i):
                g = i % 3
                dve.wait_ge(ysq, i + 1)
                if i < 3:
                    return
                if i >= 6:
                    dve.wait_ge(ysum, i - 5)
                v.tensor_tensor(cols(ss_x, g), cols(ss_x, g), sq_g[:, i % 2, 0:GROUPS[g][1]], ALU.add
                                ).then_inc(ysum, 1)

            last_b = FF_BLOCKS - 1
            for o in range(KD):
                for g in range(3):
                    add_back(last_b, o, g)
                    if g == 2:
                        dve.wait_ge(free[3 * (o % 2) + 2], ff2_turn(last_b) + o // 2 + 1)
                        if o > 0:
                            dve.wait_ge(y_smp, 2 * o)
                        v.tensor_tensor(by_sample(smp_t[:]), by_sample(smp_acc[:, o, :]),
                                        ada_late[:, 3 * KD + o, 1:NC].unsqueeze(2).to_broadcast([P, NB, TB]),
                                        ALU.mult).then_inc(y_smp, 1)
                        dve.wait_ge(y_smp, 2 * o + 1)
                        v.tensor_tensor(xT[:, o, T_PROMPT:T], xT[:, o, T_PROMPT:T], smp_t[:], ALU.add
                                        ).then_inc(y_smp, 1)
                    if 3 * o + g > 0:
                        add_y(3 * o + g - 1)
            add_y(3 * KD - 1)
            for g in range(3):
                when_read(dve, ("ss_y", g))
                inverse(("y", g), TILES_OF[g])
            dve.wait_ge(rstd_done, SCALE_NO["y", 2])
            dve.wait_ge(gfin_in, 16)
            for t in range(NT):
                r = tile_rows(t)
                for h in range(2):
                    bank = when_full(dve, ("y", t, h))
                    v.scalar_tensor_tensor(yout[0:r, t, 512 * h:512 * h + 512], bank[0:r, :], rstd[0:r, t:t + 1],
                                           g_fin[0:r, 512 * h:512 * h + 512], ALU.mult, ALU.mult
                                           ).then_inc(free_of(("y", t, h)), 1)


_INS = ['x_prompt', 'x_sample', 'c_prompt', 'c_sample', 'state_conv', 'state_rglru', 'w_ada', 'b_ada', 'g_mix',
        'g_ffn', 'w_in', 'conv_w', 'conv_b', 'w_ra', 'b_ra', 'w_ri', 'b_ri', 'lru_l', 'ln_v_g', 'ln_v_b', 'w_s',
        'b_s', 'g_rg', 'g_sg', 'w_out', 'w_ff1', 'w_ff2', 'g_final']
_OUTS = [(1, T_PROMPT, D), (NB, TB, D), (1, 1, HALO, D_RG), (1, 1, D_RG), (1, 1, CHUNK, D_SG),
         (1, NB, HALO, D_RG), (1, NB, D_RG), (1, NB, TB, D_SG)]


def kernel(**inputs):
    import numpy as _np
    import concourse.bacc as _bacc
    from concourse import mybir as _mybir
    from concourse.bass_utils import run_bass_kernel_spmd as _run

    nc = _bacc.Bacc("TRN2", target_bir_lowering=False, num_devices=1)
    arrays, args = {}, {}
    for name in _INS:
        x = _np.ascontiguousarray(inputs[name])
        arrays[f"in_{name}"] = x
        args[name] = nc.dram_tensor(f"in_{name}", x.shape, _mybir.dt.from_np(x.dtype), kind="ExternalInput").ap()
    outs = [nc.dram_tensor(f"out_{i}", shape, _mybir.dt.float32, kind="ExternalOutput").ap()
            for i, shape in enumerate(_OUTS)]
    build(nc, args, outs)
    r = _run(nc, [arrays], core_ids=[0])
    return tuple(r.results[0][f"out_{i}"] for i in range(len(_OUTS)))
```

```python
from contextlib import ExitStack

import concourse.bass as bass
from concourse import mybir

F32 = mybir.dt.float32
F32R = mybir.dt.float32r
ALU = mybir.AluOpType
ACT = mybir.ActivationFunctionType

P = 128
D = 1024
T_PROMPT = 1024
NB, TB = 8, 8
T_SAMPLE = NB * TB
T = T_PROMPT + T_SAMPLE
KD = D // P
D_RG = D_SG = D // 2
JB = D_RG // P
D_FF = 4 * D
D_IN = 2 * D_RG + 2 * D_SG
CONV_W = 4
HALO = CONV_W - 1
HEADS, HD = 8, 64
CHUNK = 128
EPS = 1e-6
LRU_C = 8.0
NT = (T + P - 1) // P
NC = 1 + NB
N_ADA = 6 * KD
ADA_EARLY = 2 * KD

GROUPS = [(0, 384), (384, 384), (768, 320)]
TILES_OF = [[0, 1, 2], [3, 4, 5], [6, 7, 8]]
PROMPT_G2 = T_PROMPT - GROUPS[2][0]

SEG = HALO + TB
ROW_W = HALO + T_PROMPT + NB * SEG
SCAN_W = ROW_W - HALO
WIDE = 1120
SCAN_GROUPS = [(0, 384), (384, 384), (768, SCAN_W - 768)]

R_STATE, R_H0, R_CW, R_CB, R_BRA, R_BRI, R_LRU, R_LNG, R_LNB, R_GRG, R_GSG, R512 = 0, 24, 32, 36, 37, 38, 39, 40, 41, 42, 43, 44
V_GMIX, V_GFFN, V_GFIN, N_VECS = N_ADA, N_ADA + KD, N_ADA + 2 * KD, N_ADA + 3 * KD
TAILS = HALO + NB * HALO + 1 + NB

PIECE = 512
E_PIECES, L_PIECES = ADA_EARLY * P // PIECE, (N_ADA - ADA_EARLY) * P // PIECE
E_UNITS, L_UNITS = E_PIECES * KD // 2, L_PIECES * KD
UNIT_SLOTS = [*range(4, 18), *range(20, 24), *range(26, 30), *range(32, 36), *range(38, 44)]
LAST_TURN = UNIT_SLOTS[-1] + 1
assert len(UNIT_SLOTS) * 2 == L_UNITS
DVE_UNITS = [*range(1, E_UNITS - 2, 2), E_UNITS - 2, E_UNITS - 1]
POOL_UNITS = [u for u in range(E_UNITS) if u not in DVE_UNITS]
PIECE_OF = {UNIT_SLOTS[i]: i * 2 // KD for i in range(len(UNIT_SLOTS))}
FIRST_SLOT = [UNIT_SLOTS[KD // 2 * p] for p in range(L_PIECES)]
LAST_SLOT = [UNIT_SLOTS[KD // 2 * (p + 1) - 1] for p in range(L_PIECES)]
ROWS_SLOT, WS_SLOTS, SMALL_SLOT, ROWSUM_SLOT = 6, (7, 8), 9, 10

U_V, U_RG, U_U, U_OUT = 0, 4, 12, 16
U_FF = U_OUT + 3 * KD
FF_BLOCKS = D_FF // 256

N_VEC_LOADS = 4
N_ROW_LOADS = 11
LAM_STEPS = 18
SG_ORDER = [(j, g) for j in range(JB - 2) for g in range(3)] + [(j, g) for g in range(3) for j in (JB - 2, JB - 1)]
HF_AT = [0] * (KD + 4) + list(range(1, 14))
MERGE_AT = {(0, 1): ("rg", 1, 0, 2), (0, 2): ("rg", 1, 2, 4), (0, 3): ("sg", 1, 0, 2), (0, 4): ("sg", 1, 2, 4),
            (0, 6): ("rg", 2, 0, 2), (0, 7): ("rg", 2, 2, 4), (1, 0): ("sg", 2, 0, 2), (1, 1): ("sg", 2, 2, 4)}
FIRST_ORDER = [(0, 0), (0, 1), (1, 0), (1, 1), (0, 2), (1, 2)]
HIDDEN_ORDER = [(c, g) for c in range(2) for g in range(3)]
LAST_GROUPS = (2, 0, 1)
LAST_ORDER = [(g, o) for g in LAST_GROUPS for o in range(KD)]
Y_HALVES = [(t, h) for g in LAST_GROUPS for t in TILES_OF[g] for h in range(2)]
Y_SUM_AT = [KD + 5, 2 * KD + 5]
Y_ROOT_AT = [KD + 3, 2 * KD + 4]
ACT_Y_OUT_AT = {KD + 6: 1, KD + 8: 3, KD + 10: 5, 2 * KD + 7: 7}
Y_TURN_AT = {KD + 7 + q: q for q in range(6)} | {2 * KD + 6 + q: 6 + q for q in range(2)}
NORM_ITEMS = 3 * KD


def plan_banks():
    turns, use = [0] * 8, {}

    def take(name, bank):
        use[name] = (bank, turns[bank])
        turns[bank] += 1

    take("cond", 6)
    for t in range(NT):
        for h in range(2):
            take(("x", t, h), (2 * t + h) % 6)
    for g, b in enumerate((7, 0, 1)):
        take(("bcx", g), b)
    for p in range(E_PIECES):
        take(("ap_early", p), 2 + p)
    take("vecs", 6)
    take("ada1", 6)
    take("ada1_end", 7)

    def slot(i):
        if i in FIRST_SLOT:
            p = FIRST_SLOT.index(i)
            if p > 0:
                take(("turned", p - 1), 7)
            take(("ap", p), 6)
        if i == LAST_TURN:
            take(("turned", L_PIECES - 1), 7)
        if i == ROWS_SLOT:
            take("rows512", 7)
        if i in WS_SLOTS:
            take(f"ws{WS_SLOTS.index(i)}", 7)
        if i == SMALL_SLOT:
            take("wsmall", 7)
        if i == ROWSUM_SLOT:
            take("rowsum", 7)

    n_slot = 0
    for j in range(JB):
        for g in range(3):
            take(("v", j, g), 3 * (j % 2) + g)
            slot(n_slot)
            n_slot += 1
    for j in range(JB):
        for name, s in (("xr", 0), ("yg", 1)):
            for g in range(3):
                take((name, j, g), 3 * s + g)
                slot(n_slot)
                n_slot += 1
                if j < 3 and (g > 0 if name == "yg" else g == 2):
                    take(("vt", 3 * j + (g if name == "yg" else 0)), 7)
        if j == JB - 1:
            for jj in range(JB):
                for g in range(3):
                    take(("mix", jj, g), 3 * (jj % 2) + g)
        for name, s in (("gr", 0), ("gi", 1)):
            for g in range(3):
                take((name, j, g), 3 * s + g)
    for i in range(n_slot, LAST_TURN):
        slot(i)
    for j in range(JB):
        for g in range(3):
            take(("u", j, g), 3 * (j % 2) + g)
    take("ss_rg", 7)
    slot(LAST_TURN)
    take(("bcrg", 0), 6)
    take(("ss_sg", 0), 7)
    take(("bcsg", 0), 6)
    take(("bcrg", 1), 6)
    take(("ss_sg", 1), 7)
    take(("bcsg", 1), 7)
    take(("bcrg", 2), 6)
    take(("ss_sg", 2), 7)
    take(("bcsg", 2), 7)
    take(("ss_x1", 0), 6)
    take(("bcx1", 0), 6)
    take("tails", 7)
    take(("ss_x1", 1), 7)
    take(("bcx1", 1), 7)
    take(("ss_x1", 2), 6)
    take(("bcx1", 2), 6)
    for g in range(3):
        for o in range(KD):
            take(("out", o, g), (KD * g + o) % 6)
    assert len(set(turns[:6])) == 1
    ff = turns[0]
    for b in range(6):
        turns[b] += 5 * FF_BLOCKS
    take(("ss_y", 2), 7)
    for q in range(6):
        take(("y", *Y_HALVES[q]), 6 + q % 2)
    take(("ss_y", 0), 6)
    for q, bank in zip(range(6, 18), (7, 6, 0, 1, 2, 3, 4, 5, 6, 0, 1, 2)):
        take(("y", *Y_HALVES[q]), bank)
        if q == 9:
            take(("ss_y", 1), 7)
    return use, ff


USE, FF_TURN = plan_banks()


def ff1_turn(b):
    return FF_TURN if isinstance(b, int) and b == 0 else 5 * b + (FF_TURN - 4)


def ff2_turn(b):
    last = isinstance(b, int) and b == FF_BLOCKS - 1
    return 5 * b + (FF_TURN + 1 if last else FF_TURN + 2)


def ff1_half(b):
    return U_FF // 2 if isinstance(b, int) and b == 0 else 2 * b + (U_FF // 2 - 1)


def ff2_half(b):
    last = isinstance(b, int) and b == FF_BLOCKS - 1
    return 2 * b + (U_FF // 2 + 1 if last else U_FF // 2 + 2)


def build(nc, a, out):
    with ExitStack() as ctx:
        sem = lambda name: ctx.enter_context(nc.semaphore(name))
        psum = [ctx.enter_context(nc.psum_tensor(f"bank{b}", [P, 512], F32)) for b in range(8)]

        base = (nc.sbuf_base + 31) // 32 * 32

        def at(name, shape, offset, dt=F32):
            return nc.alloc_sbuf_tensor_at(name, [P, *shape], dt, offset=offset)

        off_x = base
        off_act = off_x + KD * T * 4
        off_w = off_act + 2 * KD * T * 4
        off_v = off_w + 6 * 4096
        off_rg = off_v + JB * NT * P * 4
        off_t = off_rg + JB * T * 4
        off_c = off_t + 5 * WIDE * 4
        tmp = lambda n: off_t + n * WIDE * 4

        xT = at("xT", [KD, T], off_x)
        act_hi = at("act_hi", [KD, T], off_act, F32R)
        act_lo = at("act_lo", [KD, T], off_act + KD * T * 4, F32R)
        w_raw = at("w_raw", [2, 1024], off_w)
        w_hi = at("w_hi", [2, 1024], off_w + 2 * 4096, F32R)
        w_lo = at("w_lo", [2, 1024], off_w + 4 * 4096, F32R)
        V = at("V", [JB, NT * P], off_v)
        RG = at("RG", [JB, T], off_rg)
        row = at("row", [WIDE], tmp(0))
        xc = at("xc", [WIDE], tmp(1))
        rr = at("rr", [WIDE], tmp(2))
        ig = at("ig", [WIDE], tmp(3))
        aa = at("aa", [WIDE], tmp(4))
        sq_rg = at("sq_rg", [2, WIDE], tmp(0))
        ss_rg = at("ss_rg", [T], tmp(2))
        ss_sg = at("ss_sg", [T], tmp(3))
        sq_g = at("sq_g", [2, 384], tmp(4))
        xin = at("xin", [NT, D], off_v)
        ada_w = at("ada_w", [E_UNITS, 2 * PIECE], off_act)
        ada_w_lo = at("ada_w_lo", [E_UNITS, 2 * PIECE], off_act, F32R)
        xn = at("xn", [KD, T], off_v)
        ws_raw = at("ws_raw", [HEADS, CHUNK], tmp(1))
        own = at("own", [NB], tmp(1) + 4096)
        cond_rows = at("cond_rows", [D], tmp(2))
        eye8 = at("eye8", [NB, TB], tmp(2) + 4096)
        rows512 = at("rows512", [D_RG], tmp(3))
        vec_rows = at("vec_rows", [P], tmp(3) + 2048)
        ada_e = at("ada_e", [ADA_EARLY, NC], tmp(3) + 2560)
        gain_m = at("gain_m", [KD, NC], tmp(3) + 3136)
        ones64 = at("ones64", [HD], tmp(3) + 3424)
        h_hi = at("h_hi", [4, T], off_v, F32R)
        h_lo = at("h_lo", [4, T], off_v + 4 * T * 4, F32R)
        relu = at("relu", [2, 384], tmp(0))
        sqr = at("sqr", [2, 384], tmp(1))
        ss_x = at("ss_x", [T], tmp(2))
        yout = at("yout", [NT, D], off_act)
        xg = at("xg", [KD, T], off_act + NT * D * 4)

        pos = [off_c]

        def const(name, shape, dt=F32):
            n = 4
            for s in shape:
                n *= s
            t = at(name, shape, pos[0], dt)
            pos[0] += (n + 31) // 32 * 32
            return t

        off_ws = pos[0]
        wsT = const("wsT", [HEADS, CHUNK])
        off_w64 = pos[0]
        ws64 = const("ws64", [HEADS, NB, TB])
        off_bs = pos[0]
        mix_b = const("mix_b", [JB, CHUNK])
        off_gate = pos[0]
        gate_w = const("gate_w", [2, JB, P])
        ident = const("ident", [P])
        ada_late = const("ada_late", [N_ADA - ADA_EARLY, NC])
        silu = at("silu", [KD, NC], pos[0] - (N_ADA - ADA_EARLY) * NC * 4)
        gain_f = const("gain_f", [KD, NC])
        off_ring = pos[0]
        ada_ring = const("ada_ring", [4, PIECE])
        ada_lo = at("ada_lo", [4, PIECE], off_ring, F32R)
        ada_hi = at("ada_hi", [2, PIECE], off_w + 4096, F32R)
        ada_e_hi = at("ada_e_hi", [2, 2 * PIECE], off_ring, F32R)
        early_hi = lambda u: ada_e_hi[:, u % 4, :] if u % 4 < 2 else (w_hi if u % 4 == 2 else w_lo)[:, 1, :]
        r5 = const("r5", [JB, R512])
        vecs = const("vecs", [N_VECS])
        bada = vecs[:, 0:N_ADA]
        silu2 = const("silu2", [KD, 2 * NC], F32R)
        sel = const("sel", [NC])
        tails = const("tails", [JB, TAILS])
        bn = const("bn", [NT, 6])
        mv = const("mv", [NT, 2])
        v_std = const("v_std", [NT])
        ssq = const("ssq", [NT])
        std = const("std", [NT])
        rstd = const("rstd", [NT])
        ones_eps = const("ones_eps", [2])
        ones, eps = ones_eps[:, 0:1], ones_eps[:, 1:2]
        lam = at("lam", [8, JB], tmp(4))
        decays = const("decays", [2, JB])
        decay, decay_n = decays[:, 0, :], decays[:, 1, :]
        assert pos[0] <= nc.sbuf_usable_end, (pos[0], nc.sbuf_usable_end)
        pieces = at("pieces", [PIECE], off_w64)
        PB, PE_ROWS = 64, 64 + 2 * NC
        tmp1 = at("tmp1", [2, 384], off_ws)
        smp1 = at("smp1", [KD, T_SAMPLE], off_w64)
        smp_acc = at("smp_acc", [KD, T_SAMPLE], off_bs)
        smp_t = at("smp_t", [T_SAMPLE], off_ws + 3072)
        tails_out = at("tails_out", [D_RG], off_w64)

        full = [sem(f"bank{b}_full") for b in range(8)]
        free = [sem(f"bank{b}_free") for b in range(8)]
        raw_in = [sem(f"raw_in{s}") for s in range(2)]
        hi_done = [sem(f"hi_done{s}") for s in range(2)]
        lo_done = [sem(f"lo_done{s}") for s in range(2)]
        ada_in = [sem(f"ada_in{s}") for s in range(4)]
        ada_hi_done = sem("ada_hi_done")
        ada_lo_pool = sem("ada_lo_pool")
        ada_lo_dve = sem("ada_lo_dve")
        ada_hi_read = sem("ada_hi_read")
        ada_lo_read = sem("ada_lo_read")
        x_in = [sem(f"x_in{t}") for t in range(NT)]
        ada_w_in = [sem(f"ada_w_in{u}") for u in range(E_UNITS)]
        cond_in = sem("cond_in")
        vecs_in = sem("vecs_in")
        rows512_in = sem("rows512_in")
        ws_in = sem("ws_in")
        bs_in = sem("bs_in")
        gates_in = sem("gates_in")
        stored = sem("stored")
        tails_stored = sem("tails_stored")
        vrows_out = sem("vrows_out")
        pool_set = sem("pool_set")
        x_sq = sem("x_sq")
        hm_mod = sem("hm_mod")
        hm_hi = sem("hm_hi")
        hm_ready = sem("hm_ready")
        hms_step = sem("hms_step")
        hms_hi = sem("hms_hi")
        hms_ready = sem("hms_ready")
        hfs_step = sem("hfs_step")
        hfs_hi = sem("hfs_hi")
        hfs_ready = sem("hfs_ready")
        norm_tmp = sem("norm_tmp")
        norm_hi = sem("norm_hi")
        act_ready = sem("act_ready")
        eye_ready = sem("eye_ready")
        silu_step = sem("silu_step")
        silu_ready = sem("silu_ready")
        piece_turned = sem("piece_turned")
        lam_exp = sem("lam_exp")
        lam_step = sem("lam_step")
        ada_ready = sem("ada_ready")
        mixb_ready = sem("mixb_ready")
        std_done = sem("std_done")
        rstd_done = sem("rstd_done")
        halo_done = sem("halo_done")
        tap_done = sem("tap_done")
        row_read = sem("row_read")
        ix_done = sem("ix_done")
        decay_done = sem("decay_done")
        act_chain = sem("act_chain")
        q_done = sem("q_done")
        root_done = sem("root_done")
        term_done = sem("term_done")
        scan_done = sem("scan_done")
        rg_done = sem("rg_done")
        h_tail = sem("h_tail")
        v_stat = sem("v_stat")
        v_std_done = sem("v_std_done")
        v_norm = sem("v_norm")
        mix_done = sem("mix_done")
        rgsq = sem("rgsq")
        rgsum = sem("rgsum")
        sgsq = sem("sgsq")
        sgsum = sem("sgsum")
        rg_norm = sem("rg_norm")
        mrg_hi = sem("mrg_hi")
        mrg_ready = sem("mrg_ready")
        sg_norm = sem("sg_norm")
        msg_hi = sem("msg_hi")
        msg0_ready = sem("msg0_ready")
        msg_ready = sem("msg_ready")
        x1_smp = sem("x1_smp")
        x1sq = sem("x1sq")
        x1sum = sem("x1sum")
        relu_done = sem("relu_done")
        hhi_done = sem("hhi_done")
        h_ready = sem("h_ready")
        smp_zero = sem("smp_zero")
        y_smp = sem("y_smp")
        ysq = sem("ysq")
        ysum = sem("ysum")
        xg_done = sem("xg_done")

        def cols(t, g):
            c, n = GROUPS[g]
            return t[:, c:c + n] if len(t.shape) == 2 else t[:, :, c:c + n]

        def blk(t, k, g, n=None):
            c, m = GROUPS[g]
            return t[:, k, c:c + (m if n is None else n)]

        def smp(t, start, n):
            at0 = min(start, seg0)
            return t[:, at0:at0 + NB * SEG].rearrange("p (b x) -> p b x", x=SEG)[:, :, start - at0:start - at0 + n]

        def by_sample(t):
            return t.rearrange("p (b t) -> p b t", t=TB)

        f32 = lambda view: view.bitcast(F32)
        row_tok = HALO
        seg0 = HALO + T_PROMPT
        tile_rows = lambda t: min(P, T - t * P)

        def claim(pe, name):
            bank, turn = USE[name]
            if turn > 0:
                pe.wait_ge(free[bank], turn)
            return psum[bank]

        def when_full(eng, name):
            bank, turn = USE[name]
            eng.wait_ge(full[bank], turn + 1)
            return psum[bank]

        def when_read(eng, name):
            bank, turn = USE[name]
            eng.wait_ge(free[bank], turn + 1)

        raw_slot = lambda n: n % 2 if n < 2 or n >= U_OUT else 0

        def wait_lo(eng, n):
            eng.wait_ge(lo_done[n % 2], n // 2 + 1)

        def wait_ada_lo_read(eng, m):
            if m % KD == KD - 1:
                when_full(eng, ("ap", m // KD))
            else:
                eng.wait_ge(ada_lo_read, m + 1 - m // KD)

        def slot_units(i):
            if i not in PIECE_OF:
                return []
            n = 2 * UNIT_SLOTS.index(i)
            return [n, n + 1]

        full_of = lambda name: full[USE[name][0]]
        free_of = lambda name: free[USE[name][0]]

        x_p = a["x_prompt"].rearrange("a t d -> (a t) d")
        x_s = a["x_sample"].rearrange("b t d -> (b t) d")
        w_in_v = a["w_in"][0].rearrange("(k p) n -> p k n", p=P)
        w_out_v = a["w_out"][0].rearrange("(k p) n -> p k n", p=P)
        w_ff1_v = a["w_ff1"][0].rearrange("(k p) n -> p k n", p=P)
        w_ff2_v = a["w_ff2"][0].rearrange("(k p) n -> p k n", p=P)
        w_ada_v = a["w_ada"][0].rearrange("(k p) n -> p k n", p=P)

        unit_cols = [2 * D_RG + D_SG + P * j for j in range(JB)]
        for j in range(JB):
            unit_cols += [P * j, D_RG + P * j]
        unit_cols += [2 * D_RG + P * j for j in range(JB)]

        def sum_x1_squares(eng, e, i):
            g, o = i // KD, i % KD
            if o == 0:
                return
            eng.wait_ge(x1sq, i + 1)
            if o >= 2:
                eng.wait_ge(x1sum, (KD - 1) * g + o - 1)
            e.tensor_tensor(cols(ss_x, g), cols(ss_x, g), sq_g[:, i % 2, 0:GROUPS[g][1]], ALU.add).then_inc(x1sum, 1)

        def last_tile(n):
            return n % 6, ff2_turn(FF_BLOCKS - 1) + n // 6

        def y_adds(n):
            return (KD - 1) * (n // KD) + n % KD

        def add_y(eng, e, n):
            g, o = LAST_ORDER[n]
            if o == 0:
                return
            eng.wait_ge(ysq, n + 1)
            if y_adds(n) > 1:
                eng.wait_ge(ysum, y_adds(n) - 1)
            e.tensor_tensor(cols(ss_x, g), cols(ss_x, g), sq_g[:, n % 2, 0:GROUPS[g][1]], ALU.add).then_inc(ysum, 1)

        block = ctx.enter_context(nc.Block())

        @block.sync
        def _(sp):
            for t in range(NT):
                src = x_p[P * t:P * t + P] if t < NT - 1 else x_s
                sp.dma_start(xin[0:tile_rows(t), t, :], src).then_inc(x_in[t], 16)

            def unit(s, half, src, shape_k):
                if not (isinstance(half, int) and half == 0):
                    sp.wait_ge(lo_done[s], half)
                sp.dma_start(w_raw[:, s, :].rearrange("p (k n) -> p k n", k=shape_k), src).then_inc(raw_in[s], 16)

            def in_unit(n):
                if n == 2:
                    wait_lo(sp, 0)
                elif n > 2:
                    wait_lo(sp, n - 1)
                sp.dma_start(w_raw[:, raw_slot(n), :].rearrange("p (k n) -> p k n", k=KD),
                             w_in_v[:, :, unit_cols[n]:unit_cols[n] + P]).then_inc(raw_in[n % 2], 16)

            def late_unit(m):
                if m < 4:
                    when_full(sp, "ada1_end")
                else:
                    wait_ada_lo_read(sp, m - 4)
                c = ADA_EARLY * P + PIECE * (m // KD)
                sp.dma_start(ada_ring[:, m % 4, :], w_ada_v[:, m % KD, c:c + PIECE]).then_inc(ada_in[m % 4], 16)

            for u in range(E_UNITS):
                if u == E_UNITS - 2:
                    in_unit(0)
                k, c = u % (KD // 2) * 2, u // (KD // 2) * PIECE
                sp.dma_start(ada_w[:, u, :].rearrange("p (k n) -> p k n", k=2), w_ada_v[:, k:k + 2, c:c + PIECE]
                             ).then_inc(ada_w_in[u], 16)
            in_unit(1)
            order = [(3 * (n - 2) + 0.5, 0, in_unit, n) for n in range(2, U_OUT)]
            order += [(UNIT_SLOTS[(m - 4) // 2] + 0.9 if m >= 4 else 0, 1, late_unit, m) for m in range(L_UNITS)]
            for _, _, load, n in sorted(order, key=lambda e: (e[0], e[1], e[3])):
                load(n)
            for n in range(U_OUT, U_FF):
                o = (n - U_OUT) % KD
                if n == U_OUT:
                    wait_lo(sp, n - 1)
                if n == U_OUT + 1:
                    when_full(sp, ("ap", L_PIECES - 1))
                unit(n % 2, n // 2, w_out_v[:, :, P * o:P * o + P], KD)

            def ff1_units(b):
                for c in range(2):
                    unit(c, ff1_half(b), w_ff1_v[:, :, bass.ds(256 * b + P * c, P)], KD)

            def ff2_units(b):
                for h in range(2):
                    unit(h, ff2_half(b), w_ff2_v[:, bass.ds(2 * b, 2), 512 * h:512 * h + 512], 2)

            ff1_units(0)
            with sp.Fori(0, FF_BLOCKS - 1) as b:
                ff1_units(b + 1)
                ff2_units(b)
            ff2_units(FF_BLOCKS - 1)
            yp, ys = out[0].rearrange("a t d -> (a t) d"), out[1].rearrange("b t d -> (b t) d")
            for t in [t for g in LAST_GROUPS for t in TILES_OF[g]]:
                when_read(sp, ("y", t, 0))
                when_read(sp, ("y", t, 1))
                dst = yp[P * t:P * t + P] if t < NT - 1 else ys
                sp.dma_start(dst, yout[0:tile_rows(t), t, :]).then_inc(stored, 16)
            sp.wait_ge(stored, 16 * NT)
            sp.wait_ge(tails_stored, 64)

        @block.gpsimd
        def _(pool):
            g = nc.gpsimd
            g.memset(gate_w[:], 0.0).then_inc(pool_set, 1)
            g.memset(ident[:], 0.0).then_inc(pool_set, 1)
            g.memset(ones[:], 1.0).then_inc(pool_set, 1)
            g.memset(ones64[:], 1.0).then_inc(pool_set, 1)
            g.memset(eps[:], EPS).then_inc(pool_set, 1)
            g.memset(own[0:64], 1.0).then_inc(pool_set, 1)
            pool.wait_ge(pool_set, 6)
            g.affine_select(out=ident[:], in_=ident[:], compare_op=ALU.not_equal, fill=1.0, base=0,
                            pattern=[[-1, P]], channel_multiplier=1).then_inc(pool_set, 1)
            g.affine_select(out=own[0:64], in_=own[0:64], compare_op=ALU.is_ge, fill=0.0, base=0,
                            pattern=[[-TB, NB]], channel_multiplier=1).then_inc(pool_set, 1)
            pool.wait_ge(pool_set, 8)
            g.affine_select(out=own[0:64], in_=own[0:64], compare_op=ALU.is_ge, fill=0.0, base=TB - 1,
                            pattern=[[TB, NB]], channel_multiplier=-1).then_inc(pool_set, 1)
            loads = [
                (R_STATE, NB * HALO, a["state_conv"][0].rearrange("b t d -> (b t) d")),
                (R_H0, NB, a["state_rglru"][0]), (R_CW, CONV_W, a["conv_w"][0]), (R_CB, 1, a["conv_b"]),
                (R_BRA, 1, a["b_ra"].rearrange("l h d -> l (h d)")),
                (R_BRI, 1, a["b_ri"].rearrange("l h d -> l (h d)")),
                (R_LRU, 1, a["lru_l"]), (R_LNG, 1, a["ln_v_g"]), (R_LNB, 1, a["ln_v_b"]),
                (R_GRG, 1, a["g_rg"]), (R_GSG, 1, a["g_sg"]),
            ]
            assert len(loads) == N_ROW_LOADS
            pool.dma_start(ws_raw[:], a["w_s"][0].rearrange("h t s -> t h s")).then_inc(ws_in, 16)
            for r, n, src in loads:
                pool.dma_start(rows512[r:r + n, :], src).then_inc(rows512_in, 16)
            for e in range(2):
                pool.dma_start(mix_b[HD * e:HD * e + HD, :, :],
                               a["b_s"][0].rearrange("(j e) t -> e j t", e=2)[e].partition_broadcast(HD)
                               ).then_inc(bs_in, 16)
            for i, name in enumerate(("w_ra", "w_ri")):
                for e in range(2):
                    pool.dma_start(gate_w[HD * e:HD * e + HD, i, :, HD * e:HD * e + HD],
                                   a[name][0].rearrange("(j e) i o -> e i j o", e=2)[e]).then_inc(gates_in, 16)
            pool.wait_ge(ws_in, 16)
            g.affine_select(out=ws_raw[:], in_=ws_raw[:], compare_op=ALU.is_ge, fill=0.0, base=0,
                            pattern=[[0, HEADS], [-1, CHUNK]], channel_multiplier=1).then_inc(pool_set, 1)

            for u in POOL_UNITS:
                pool.wait_ge(ada_hi_done, u + 1)
                g.tensor_tensor(ada_w_lo[:, u, :], ada_w[:, u, :], f32(early_hi(u)), ALU.subtract
                                ).then_inc(ada_lo_pool, 1)
            pool.wait_ge(hi_done[0], 1)
            g.tensor_tensor(w_lo[:, 0, :], w_raw[:, 0, :], f32(w_hi[:, 0, :]), ALU.subtract).then_inc(lo_done[0], 1)

            def late_lo(i):
                for m in slot_units(i):
                    pool.wait_ge(ada_hi_done, E_UNITS + m + 1)
                    g.tensor_tensor(ada_lo[:, m % 4, :], ada_ring[:, m % 4, :], f32(ada_hi[:, m % 2, :]),
                                    ALU.subtract).then_inc(ada_lo_pool, 1)

            pool.wait_ge(ada_ready, 2)
            for gi in range(3):
                when_read(pool, ("bcx", gi))
            view = xn[:, :, T_PROMPT:T].rearrange("p k (b t) -> p k b t", t=TB)
            for q, (m, op) in enumerate(((gain_m, ALU.mult), (ada_e[:, 0:KD], ALU.add))):
                if q > 0:
                    pool.wait_ge(hms_step, q)
                g.tensor_tensor(view, view, m[:, :, 1:NC].unsqueeze(3).to_broadcast([P, KD, NB, TB]), op
                                ).then_inc(hms_step, 1)
            pool.wait_ge(hms_hi, 1)
            g.tensor_tensor(act_lo[:, :, T_PROMPT:T], xn[:, :, T_PROMPT:T], f32(act_hi[:, :, T_PROMPT:T]),
                            ALU.subtract).then_inc(hms_ready, 1)

            for i in range(13):
                late_lo(i)
            for j in range(JB):
                if j == 0:
                    when_read(pool, "rows512")
                    when_read(pool, "rowsum")
                else:
                    pool.wait_ge(term_done, j)
                if j == 0:
                    for i in range(13, 15):
                        late_lo(i)
                g.memset(row[:, 0:HALO], 0.0).then_inc(halo_done, 1)
                g.tensor_copy(smp(row, seg0, HALO),
                              r5[:, j, R_STATE:R_STATE + NB * HALO].rearrange("p (b x) -> p b x", x=HALO)
                              ).then_inc(halo_done, 1)
                when_read(pool, ("xr", j, 2))
                g.tensor_copy(tails[:, j, 0:HALO], row[:, T_PROMPT:T_PROMPT + HALO])
                g.tensor_copy(tails[:, j, HALO:HALO + NB * HALO].rearrange("p (b x) -> p b x", x=HALO),
                              smp(row, seg0 + TB, HALO)).then_inc(row_read, 1)
                for i in range(15 + 6 * j, 21 + 6 * j) if j < JB - 1 else range(33, 39):
                    late_lo(i)
                when_read(pool, ("gi", j, 2))
                g.tensor_tensor(ig[:, 0:SCAN_W], ig[:, 0:SCAN_W], xc[:, 0:SCAN_W], ALU.mult).then_inc(ix_done, 1)
                if j == 2:
                    when_read(pool, ("vt", NT - 1))
                    pool.dma_start(out[4][0, 0].rearrange("t (j d) -> t j d", j=JB), V[:, :, P * 7:P * 8]).then_inc(vrows_out, 16)
                    pool.dma_start(out[7][0].rearrange("b t (j d) -> (b t) j d", j=JB), V[0:64, :, P * 8:P * 9]
                                   ).then_inc(vrows_out, 16)
                pool.wait_ge(scan_done, 3 * j + 3)
                c = HALO + NB * HALO
                g.tensor_copy(tails[:, j, c:c + 1], rr[:, T_PROMPT - 1:T_PROMPT])
                g.tensor_copy(tails[:, j, c + 1:c + 1 + NB],
                              smp(rr, seg0 + TB - 1, 1).rearrange("p b x -> p (b x)")).then_inc(h_tail, 1)
            pool.wait_ge(vrows_out, 32)
            when_read(pool, ("mix", JB - 1, 2))
            g.memset(smp_acc[:], 0.0).then_inc(smp_zero, 1)
            for i in range(39, LAST_TURN):
                late_lo(i)
            for gi in range(3):
                for j in range(JB):
                    pool.wait_ge(mrg_hi, JB * gi + j + 1)
                    g.tensor_tensor(blk(act_lo, j, gi), blk(RG, j, gi), f32(blk(act_hi, j, gi)),
                                    ALU.subtract).then_inc(mrg_ready, 1)
                if gi > 0:
                    for j in range(JB):
                        pool.wait_ge(msg_hi, JB * gi + j + 1)
                        g.tensor_tensor(blk(act_lo, JB + j, gi), blk(V, j, gi), f32(blk(act_hi, JB + j, gi)),
                                        ALU.subtract).then_inc(msg_ready, 1)
            for i in range(KD, 3 * KD):
                sum_x1_squares(pool, g, i)
                if i == KD + 5:
                    when_read(pool, "tails")
                    n1, n2 = HALO, HALO + NB * HALO
                    pool.dma_start(out[2][0, 0], tails_out[0:n1, :]).then_inc(tails_stored, 16)
                    pool.dma_start(out[5][0].rearrange("b t d -> (b t) d"), tails_out[n1:n2, :]).then_inc(tails_stored, 16)
                    pool.dma_start(out[3][0], tails_out[n2:n2 + 1, :]).then_inc(tails_stored, 16)
                    pool.dma_start(out[6][0], tails_out[n2 + 1:n2 + 1 + NB, :]).then_inc(tails_stored, 16)

            pool.wait_ge(ada_ready, 4)
            view = smp1[:].rearrange("p k (b t) -> p k b t", t=TB)
            for q, (m, op) in enumerate(((gain_f, ALU.mult), (ada_late[:, KD:2 * KD], ALU.add))):
                pool.wait_ge(hfs_step, q + 1)
                g.tensor_tensor(view, view, m[:, :, 1:NC].unsqueeze(3).to_broadcast([P, KD, NB, TB]), op
                                ).then_inc(hfs_step, 1)
            pool.wait_ge(hfs_hi, 1)
            g.tensor_tensor(act_lo[:, :, T_PROMPT:T], smp1[:], f32(act_hi[:, :, T_PROMPT:T]), ALU.subtract
                            ).then_inc(hfs_ready, 1)

            def hidden_lo(b, pair, order=HIDDEN_ORDER):
                for item, (c, gi) in enumerate(order):
                    n = GROUPS[gi][1]
                    pool.wait_ge(free[3 * c + gi], ff1_turn(b) + 1)
                    pool.wait_ge(hhi_done, 6 * b + item + 1)
                    s = 2 * pair + c
                    g.tensor_tensor(blk(h_lo, s, gi), sqr[:, item % 2, 0:n], f32(blk(h_hi, s, gi)),
                                    ALU.subtract).then_inc(h_ready, 1)

            hidden_lo(0, 0, FIRST_ORDER)
            with pool.Fori(0, (FF_BLOCKS - 2) // 2) as m:
                hidden_lo(2 * m + 1, 1)
                hidden_lo(2 * m + 2, 0)
            hidden_lo(FF_BLOCKS - 1, 1)
            for n in range(2 * KD):
                add_y(pool, g, n)

        SCALE_NO = {"x": 1, "rg": 2, ("sg", 0): 3, ("sg", 1): 4, ("sg", 2): 5,
                    ("x1", 0): 6, ("x1", 1): 7, ("x1", 2): 8, ("y", 2): 9, ("y", 0): 10, ("y", 1): 11}

        def by_rows(tiles):
            whole = [t for t in tiles if tile_rows(t) == P]
            parts = [(P, whole[0], whole[-1] + 1)]
            if NT - 1 in tiles:
                parts.append((tile_rows(NT - 1), NT - 1, NT))
            return parts

        @block.tensor
        def _(pe):
            mm = nc.tensor.matmul

            def turn(dst, src, rows=P):
                return nc.tensor.transpose(dst, src, ident[0:rows, 0:rows])

            def turn_cond():
                pe.wait_ge(cond_in, 32)
                bank = claim(pe, "cond")
                for k in range(KD):
                    last = turn(bank[:, NC * k:NC * k + NC], cond_rows[0:NC, P * k:P * k + P], NC)
                last.then_inc(full_of("cond"), 1)

            pe.wait_ge(pool_set, 7)
            for t in range(NT):
                if t == 3:
                    turn_cond()
                pe.wait_ge(x_in[t], 16)
                r = tile_rows(t)
                for h in range(2):
                    bank = claim(pe, ("x", t, h))
                    for i in range(4):
                        k = 4 * h + i
                        last = turn(bank[:, r * i:r * i + r], xin[0:r, t, P * k:P * k + P], r)
                    last.then_inc(full_of(("x", t, h)), 1)

            def spread_scale(name, scale, tiles):
                pe.wait_ge(rstd_done, SCALE_NO[scale])
                bank = claim(pe, name)
                for i, t in enumerate(tiles):
                    r = tile_rows(t)
                    last = turn(bank[:, P * i:P * i + r], rstd[0:r, t:t + 1].to_broadcast([r, P]), r)
                last.then_inc(full_of(name), 1)

            def sum_squares(name, squares, tiles):
                bank = claim(pe, name)
                for t in tiles:
                    r = tile_rows(t)
                    last = mm(bank[0:r, t:t + 1], squares[:, P * t:P * t + r], ones[:, :], start=True, stop=True)
                last.then_inc(full_of(name), 1)

            def small_rows():
                pe.wait_ge(rows512_in, 16 * N_ROW_LOADS)
                bank = claim(pe, "rows512")
                for j in range(JB):
                    last = turn(bank[:, R512 * j:R512 * j + R512], rows512[0:R512, P * j:P * j + P], R512)
                last.then_inc(full_of("rows512"), 1)

            def mixing_weights(half):
                pe.wait_ge(pool_set, 10)
                bank = claim(pe, f"ws{half}")
                for h in range(4):
                    last = turn(bank[:, CHUNK * h:CHUNK * h + CHUNK], ws_raw[:, 4 * half + h, :])
                last.then_inc(full_of(f"ws{half}"), 1)

            def mixing_corner():
                when_read(pe, "ws0")
                when_read(pe, "ws1")
                pe.wait_ge(eye_ready, 2)
                bank = claim(pe, "wsmall")
                mm(bank[0:64, 0:64], eye8[0:TB].rearrange("p b s -> p (b s)"), wsT[0:TB, :, 0:TB],
                   start=True, stop=True).then_inc(full_of("wsmall"), 1)

            def mixing_row_sums():
                bank = claim(pe, "rowsum")
                for h in range(HEADS):
                    e = h % 2
                    last = mm(bank[HD * e:HD * e + HD, CHUNK * (h // 2):CHUNK * (h // 2) + CHUNK], ones64[:, :],
                              wsT[:, h, :], start=True, stop=True)
                last.then_inc(full_of("rowsum"), 1)

            def turn_piece(bank, c0):
                for i in range(PIECE // P):
                    last = mm(bank[:, NC * (c0 + i):NC * (c0 + i) + NC], pieces[PB:PE_ROWS, P * i:P * i + P],
                              sel[PB:PE_ROWS, :], start=True, stop=True)
                return last

            for g in range(3):
                spread_scale(("bcx", g), "x", TILES_OF[g])

            pe.wait_ge(vecs_in, 16 * N_VEC_LOADS)
            turn(claim(pe, "vecs")[:, 0:N_VECS], vec_rows[0:N_VECS, :], N_VECS).then_inc(full_of("vecs"), 1)

            pe.wait_ge(silu_ready, 1)
            pe.wait_ge(eye_ready, 2)
            for u in range(E_UNITS):
                p, q = u // (KD // 2), u % (KD // 2)
                if q == 0:
                    bank = claim(pe, ("ap_early", p))
                pe.wait_ge(ada_lo_dve if u in DVE_UNITS else ada_lo_pool,
                           DVE_UNITS.index(u) + 1 if u in DVE_UNITS else POOL_UNITS.index(u) + 1)
                for part in range(2):
                    src = early_hi(u) if part == 0 else ada_w_lo[:, u, :]
                    for k in range(2):
                        last = mm(bank[0:2 * NC, 0:PIECE], silu2[:, 2 * q + k, :], src[:, PIECE * k:PIECE * k + PIECE],
                                  start=(q == 0 and part == 0 and k == 0), stop=(q == KD // 2 - 1 and part == 1 and k == 1))
                    if part == 0:
                        last.then_inc(ada_hi_read, 1)
                if q == KD // 2 - 1:
                    last.then_inc(full_of(("ap_early", p)), 1)
                if q == KD // 2 - 2 and p > 0:
                    when_read(pe, ("ap_early", p - 1))
                    if p == 1:
                        ada1_bank = claim(pe, "ada1")
                    ins = turn_piece(ada1_bank, PIECE // P * (p - 1))
                    if p < E_PIECES - 1:
                        ins.then_inc(piece_turned, 1)
                    else:
                        ins.then_inc(full_of("ada1"), 1)
            when_read(pe, ("ap_early", E_PIECES - 1))
            turn_piece(claim(pe, "ada1_end"), 0).then_inc(full_of("ada1_end"), 1)

            def split_product(bank, n, w, rhs, k, first, final):
                mm(bank[:, 0:n], w(w_hi), rhs(act_hi if rhs_act[0] else h_hi), start=first, stop=False)
                mm(bank[:, 0:n], w(w_hi), rhs(act_lo if rhs_act[0] else h_lo), start=False, stop=False)
                return mm(bank[:, 0:n], w(w_lo), rhs(act_hi if rhs_act[0] else h_hi), start=False, stop=final)

            rhs_act = [True]

            def project(bank, s, g, wait_k=None):
                c, n = GROUPS[g]
                for k in range(KD):
                    if wait_k:
                        wait_k(k)
                    last = split_product(bank, n, lambda t: t[:, s, P * k:P * k + P],
                                         lambda t: t[:, k, c:c + n], k, k == 0, k == KD - 1)
                return last

            slots = [0]

            def slot():
                i = slots[0]
                slots[0] += 1
                if i in FIRST_SLOT and i > FIRST_SLOT[0] or i == LAST_TURN:
                    p = FIRST_SLOT.index(i) - 1 if i in FIRST_SLOT else L_PIECES - 1
                    when_read(pe, ("ap", p))
                    turn_piece(claim(pe, ("turned", p)), 0).then_inc(full_of(("turned", p)), 1)
                if i in FIRST_SLOT:
                    claim(pe, ("ap", PIECE_OF[i]))
                for m in slot_units(i):
                    p, k = m // KD, m % KD
                    bank = psum[USE["ap", p][0]]
                    pe.wait_ge(ada_lo_pool, len(POOL_UNITS) + m + 1)
                    mm(bank[0:2 * NC, 0:PIECE], silu2[:, k, :], ada_hi[:, m % 2, :], start=(k == 0), stop=False
                       ).then_inc(ada_hi_read, 1)
                    mm(bank[0:2 * NC, 0:PIECE], silu2[:, k, :], ada_lo[:, m % 4, :], start=False, stop=(k == KD - 1)
                       ).then_inc(full_of(("ap", p)) if k == KD - 1 else ada_lo_read, 1)
                if i == ROWS_SLOT:
                    small_rows()
                if i in WS_SLOTS:
                    mixing_weights(WS_SLOTS.index(i))
                if i == SMALL_SLOT:
                    mixing_corner()
                if i == ROWSUM_SLOT:
                    mixing_row_sums()

            def v_by_token(t):
                bank = claim(pe, ("vt", t))
                r = tile_rows(t)
                for j in range(JB):
                    last = turn(bank[0:r, P * j:P * j + P], V[:, j, P * t:P * t + r])
                last.then_inc(full_of(("vt", t)), 1)

            def in_tile(name, j, n, after=()):
                pe.wait_ge(lo_done[n % 2], n // 2 + 1)
                for g in range(3):
                    bank = claim(pe, (name, j, g))
                    project(bank, n % 2, g).then_inc(full_of((name, j, g)), 1)
                    for f in after[g:g + 1]:
                        f()

            for g in range(3):
                for j in range(2):
                    wait_k = None
                    if j == 0:
                        wait_k = lambda k: pe.wait_ge(hm_ready, KD * g + k + 1)
                    if j == 0 and g == 2:
                        pe.wait_ge(hms_ready, 1)
                    if g == 0:
                        pe.wait_ge(lo_done[j], 1)
                    project(claim(pe, ("v", j, g)), j, g, wait_k).then_inc(full_of(("v", j, g)), 1)
                    slot()
            for j in range(2, JB):
                in_tile("v", j, U_V + j, [slot] * 3)
            for j in range(JB):
                def after_group(g, yg, j=j):
                    slot()
                    if j < 3 and not yg and g == 2:
                        v_by_token(3 * j)
                    if j < 3 and yg and g > 0:
                        v_by_token(3 * j + g)
                if j == 0:
                    for jj in range(2, JB):
                        for g in range(3):
                            when_read(pe, ("v", jj, g))
                in_tile("xr", j, U_RG + 2 * j, [lambda g=g: after_group(g, False) for g in range(3)])
                in_tile("yg", j, U_RG + 2 * j + 1, [lambda g=g: after_group(g, True) for g in range(3)])
                if j == JB - 1:
                    pe.wait_ge(v_norm, NT + 2)
                    for jj in range(JB):
                        for g in range(2):
                            bank = claim(pe, ("mix", jj, g))
                            for c in range(4):
                                for e in range(2):
                                    col = P * (4 * g + c) + HD * e
                                    last = mm(bank[HD * e:HD * e + HD, P * c:P * c + P], V[:, jj, col:col + HD],
                                              wsT[:, 2 * jj + e, :], start=True, stop=True)
                            last.then_inc(full_of(("mix", jj, g)), 1)
                        bank = claim(pe, ("mix", jj, 2))
                        for e in range(2):
                            col = P * (NT - 1) + HD * e
                            last = mm(bank[HD * e:HD * e + HD, 0:T_SAMPLE], V[0:T_SAMPLE, jj, col:col + HD],
                                      ws64[0:T_SAMPLE, 2 * jj + e].rearrange("p b t -> p (b t)"),
                                      start=True, stop=True)
                        last.then_inc(full_of(("mix", jj, 2)), 1)
                if j == 0:
                    pe.wait_ge(gates_in, 64)
                pe.wait_ge(tap_done, 4 * j + 4)
                for i, name in enumerate(("gr", "gi")):
                    for g, (c, n) in enumerate(SCAN_GROUPS):
                        bank = claim(pe, (name, j, g))
                        mm(bank[:, 0:n], gate_w[:, i, j, :], xc[:, c:c + n],
                           start=True, stop=True).then_inc(full_of((name, j, g)), 1)

            for j in range(JB - 2):
                in_tile("u", j, U_U + j, [slot] * 3)
            pe.wait_ge(rgsum, JB - 1)
            sum_squares("ss_rg", ss_rg, range(NT))

            def sum_sg(g):
                pe.wait_ge(sgsum, SG_ORDER.index((JB - 1, g)) - 2)
                sum_squares(("ss_sg", g), ss_sg, TILES_OF[g])

            for j, g in SG_ORDER[3 * (JB - 2):]:
                if g == 0:
                    wait_lo(pe, U_U + j)
                project(claim(pe, ("u", j, g)), (U_U + j) % 2, g).then_inc(full_of(("u", j, g)), 1)
                slot()
                if (j, g) == (JB - 2, 1):
                    spread_scale(("bcrg", 0), "rg", TILES_OF[0])
                    sum_sg(0)
                if (j, g) == (JB - 2, 2):
                    spread_scale(("bcsg", 0), ("sg", 0), TILES_OF[0])

            def out_group(n, o, g):
                def wait_k(k):
                    if k < JB:
                        pe.wait_ge(mrg_ready, JB * g + k + 1)
                    elif g == 0:
                        pe.wait_ge(msg0_ready, k - JB + 1)
                    else:
                        pe.wait_ge(msg_ready, JB * (g - 1) + k - JB + 1)
                pe.wait_ge(lo_done[n % 2], n // 2 + 1)
                bank = claim(pe, ("out", o, g))
                project(bank, n % 2, g, wait_k if o == 0 else None).then_inc(full_of(("out", o, g)), 1)

            def turn_tails():
                pe.wait_ge(h_tail, JB)
                bank = claim(pe, "tails")
                for j in range(JB):
                    last = turn(bank[0:TAILS, P * j:P * j + P], tails[:, j, :])
                last.then_inc(full_of("tails"), 1)

            def sum_x1(g):
                pe.wait_ge(x1sum, (KD - 1) * (g + 1))
                sum_squares(("ss_x1", g), ss_x, TILES_OF[g])

            behind = {
                (0, 0): lambda: (spread_scale(("bcrg", 1), "rg", TILES_OF[1]), sum_sg(1)),
                (0, 2): lambda: spread_scale(("bcsg", 1), ("sg", 1), TILES_OF[1]),
                (0, 3): lambda: spread_scale(("bcrg", 2), "rg", TILES_OF[2]),
                (0, 5): lambda: sum_sg(2),
                (0, 7): lambda: spread_scale(("bcsg", 2), ("sg", 2), TILES_OF[2]),
                (1, 1): lambda: sum_x1(0),
                (1, 2): lambda: spread_scale(("bcx1", 0), ("x1", 0), TILES_OF[0]),
                (1, 4): turn_tails,
                (2, 1): lambda: sum_x1(1),
                (2, 2): lambda: spread_scale(("bcx1", 1), ("x1", 1), TILES_OF[1]),
            }
            for g in range(3):
                for o in range(KD):
                    out_group(U_OUT + KD * g + o, o, g)
                    if (g, o) in behind:
                        behind[g, o]()

            def hidden(b, first=False):
                rhs_act[0] = True
                for c, g in FIRST_ORDER if first else HIDDEN_ORDER:
                    if g == 0:
                        pe.wait_ge(lo_done[c], ff1_half(b) + 1)
                    wait_k = None
                    if first and c == 0:
                        wait_k = lambda k: pe.wait_ge(act_ready, KD * g + k + 1)
                    if first and (c, g) == (0, 2):
                        pe.wait_ge(hfs_ready, 1)
                    pe.wait_ge(free[3 * c + g], ff1_turn(b))
                    project(psum[3 * c + g], c, g, wait_k).then_inc(full[3 * c + g], 1)
                    if first and (c, g) == (0, 0):
                        sum_x1(2)
                    if first and (c, g) == (0, 1):
                        spread_scale(("bcx1", 2), ("x1", 2), TILES_OF[2])

            def back(b, pair):
                rhs_act[0] = False
                for h in range(2):
                    pe.wait_ge(lo_done[h], ff2_half(b) + 1)
                    for i in range(4):
                        o = 4 * h + i
                        for g, (c, n) in enumerate(GROUPS):
                            bank = 3 * (o % 2) + g
                            if o == 0:
                                pe.wait_ge(h_ready, 6 * b + 3 + g + 1)
                            pe.wait_ge(free[bank], ff2_turn(b) + o // 2)
                            for k in range(2):
                                last = split_product(psum[bank], n, lambda t: t[:, h, 512 * k + P * i:512 * k + P * i + P],
                                                     lambda t: t[:, 2 * pair + k, c:c + n], k, k == 0, k == 1)
                            last.then_inc(full[bank], 1)

            hidden(0, first=True)
            with pe.Fori(0, (FF_BLOCKS - 2) // 2) as m:
                hidden(2 * m + 1)
                back(2 * m, 0)
                hidden(2 * m + 2)
                back(2 * m + 1, 1)
            hidden(FF_BLOCKS - 1)
            back(FF_BLOCKS - 2, 0)

            def sum_y(g):
                pe.wait_ge(ysum, (KD - 1) * (LAST_GROUPS.index(g) + 1))
                sum_squares(("ss_y", g), ss_x, TILES_OF[g])

            def turn_y(q):
                t, h = Y_HALVES[q]
                r = tile_rows(t)
                bank = claim(pe, ("y", t, h))
                for i in range(4):
                    last = turn(bank[0:r, P * i:P * i + P], xg[:, 4 * h + i, P * t:P * t + r])
                last.then_inc(full_of(("y", t, h)), 1)

            last_b = FF_BLOCKS - 1
            rhs_act[0] = False
            for n, (g, o) in enumerate(LAST_ORDER):
                c, width = GROUPS[g]
                h, i = o // 4, o % 4
                if g == LAST_GROUPS[0] and i == 0:
                    pe.wait_ge(lo_done[h], ff2_half(last_b) + 1)
                if o == 0:
                    pe.wait_ge(h_ready, 6 * last_b + 3 + g + 1)
                bank, turns = last_tile(n)
                pe.wait_ge(free[bank], turns)
                for k in range(2):
                    last = split_product(psum[bank], width, lambda t: t[:, h, 512 * k + P * i:512 * k + P * i + P],
                                         lambda t: t[:, 2 + k, c:c + width], k, k == 0, k == 1)
                last.then_inc(full[bank], 1)
                if n in Y_SUM_AT:
                    sum_y(LAST_GROUPS[Y_SUM_AT.index(n)])
                if n in Y_TURN_AT:
                    if Y_TURN_AT[n] % 6 == 0:
                        pe.wait_ge(xg_done, KD * (Y_TURN_AT[n] // 6 + 1))
                    turn_y(Y_TURN_AT[n])
            for q in range(8, 12):
                turn_y(q)
                if q == 9:
                    sum_y(LAST_GROUPS[2])
            pe.wait_ge(xg_done, 3 * KD)
            for q in range(12, 18):
                turn_y(q)

        @block.scalar
        def _(act):
            s = nc.scalar

            act.dma_start(cond_rows[0:1, :], a["c_prompt"]).then_inc(cond_in, 16)
            act.dma_start(cond_rows[1:NC, :], a["c_sample"]).then_inc(cond_in, 16)
            loads = [(0, N_ADA, a["b_ada"][0]), (V_GMIX, KD, a["g_mix"][0]), (V_GFFN, KD, a["g_ffn"][0]),
                     (V_GFIN, KD, a["g_final"])]
            assert len(loads) == N_VEC_LOADS
            for r, n, src in loads:
                act.dma_start(vec_rows[r:r + n, :], src.rearrange("(m p) -> m p", p=P)).then_inc(vecs_in, 16)

            for t in range(NT):
                r = tile_rows(t)
                act.wait_ge(x_in[t], 16)
                if t > 0:
                    act.wait_ge(x_sq, t)
                s.activation(w_lo[0:r, 1, :], xin[0:r, t, :], ACT.Square, accum_out=ssq[0:r, t:t + 1]).then_inc(x_sq, 1)
                if t == 4:
                    bank = when_full(act, "cond")
                    s.activation(silu[:], bank[:, 0:KD * NC].rearrange("p (k c) -> p k c", k=KD), ACT.Sigmoid
                                 ).then_inc(silu_step, 1)
                if t == 6:
                    when_read(act, "cond")
                    s.activation(silu2[:, :, 0:NC], silu[:], ACT.Copy).then_inc(silu_step, 1)

            def root(name, scale, tiles, d):
                bank = when_full(act, name)
                if SCALE_NO[scale] > 1:
                    act.wait_ge(rstd_done, SCALE_NO[scale] - 1)
                parts = by_rows(tiles)
                for i, (r, t0, t1) in enumerate(parts):
                    ins = s.activation(std[0:r, t0:t1], bank[0:r, t0:t1], ACT.Sqrt, bias=eps[0:r, :], scale=1.0 / d)
                ins.then_inc(free_of(name), 1)

            def split_hi(slot, half, src_read, raw=None):
                act.wait_ge(raw_in[slot], 16 * (half + 1))
                if src_read is not None:
                    act.wait_ge(*src_read)
                s.activation(w_hi[:, slot, :], w_raw[:, slot if raw is None else raw, :], ACT.Copy
                             ).then_inc(hi_done[slot], 1)

            def full_at(name):
                bank, turn = USE[name]
                return full[bank], turn + 1

            act.wait_ge(x_sq, NT)
            act.wait_ge(pool_set, 5)
            for r, t0, t1 in by_rows(range(NT)):
                ins = s.activation(std[0:r, t0:t1], ssq[0:r, t0:t1], ACT.Sqrt, bias=eps[0:r, :], scale=1.0 / D)
            ins.then_inc(std_done, 1)

            def piece_out(name, read):
                bank = when_full(act, name)
                if read is not None:
                    act.wait_ge(*read)
                s.activation(pieces[PB:PE_ROWS, :], bank[0:2 * NC, 0:PIECE], ACT.Copy).then_inc(free_of(name), 1)

            for u in range(E_UNITS):
                if u == E_UNITS - 2:
                    split_hi(0, 0, None)
                act.wait_ge(ada_w_in[u], 16)
                if u >= 4:
                    act.wait_ge(ada_hi_read, u - 3)
                s.activation(early_hi(u), ada_w[:, u, :], ACT.Copy).then_inc(ada_hi_done, 1)
                if u % 4 == 2 and u > 4:
                    p = u // 4 - 1
                    piece_out(("ap_early", p), (piece_turned, p) if p > 0 else None)
            piece_out(("ap_early", E_PIECES - 1), full_at("ada1"))

            def late_hi(m):
                act.wait_ge(ada_in[m % 4], 16 * (m // 4 + 1))
                if m < 2:
                    wait_lo(act, 1)
                else:
                    act.wait_ge(ada_hi_read, E_UNITS + m - 1)
                s.activation(ada_hi[:, m % 2, :], ada_ring[:, m % 4, :], ACT.Copy).then_inc(ada_hi_done, 1)

            slots = [0]

            def slot():
                i = slots[0]
                slots[0] += 1
                if i in FIRST_SLOT and i > FIRST_SLOT[0] or i == LAST_TURN:
                    p = FIRST_SLOT.index(i) - 1 if i in FIRST_SLOT else L_PIECES - 1
                    bank = when_full(act, ("turned", p))
                    c = PIECE // P
                    s.activation(ada_late[:, c * p:c * p + c, :], bank[:, 0:c * NC].rearrange("p (m c) -> p m c", c=NC),
                                 ACT.Copy).then_inc(free_of(("turned", p)), 1)
                if i in LAST_SLOT:
                    p = LAST_SLOT.index(i)
                    piece_out(("ap", p), full_at(("turned", p - 1)) if p > 0 else None)
                for m in slot_units(i):
                    if m + 2 < L_UNITS:
                        late_hi(m + 2)

            for i in range(NORM_ITEMS):
                g, k = i // KD, i % KD
                if i == KD - 2:
                    split_hi(1, 0, full_at("ada1_end"))
                if i == KD:
                    act.wait_ge(hms_step, 2)
                    s.activation(act_hi[:, :, T_PROMPT:T], xn[:, :, T_PROMPT:T], ACT.Copy).then_inc(hms_hi, 1)
                act.wait_ge(hm_mod, i + 1)
                n = GROUPS[g][1] if g < 2 else PROMPT_G2
                s.activation(blk(act_hi, k, g, n), blk(xn, k, g, n), ACT.Copy).then_inc(hm_hi, 1)

            def norm_hi_items(n0, n1):
                for i in range(n0, n1):
                    if i == 2 * KD + 3:
                        act.wait_ge(hfs_step, 3)
                        s.activation(act_hi[:, :, T_PROMPT:T], smp1[:, :, :], ACT.Copy).then_inc(hfs_hi, 1)
                    act.wait_ge(norm_tmp, i + 1)
                    g, k = i // KD, i % KD
                    n = GROUPS[g][1] if g < 2 else PROMPT_G2
                    s.activation(blk(act_hi, k, g, n), tmp1[:, i % 2, 0:n], ACT.Identity,
                                 bias=ada_late[:, KD + k, 0:1]).then_inc(norm_hi, 1)

            late_hi(0)
            late_hi(1)

            act.wait_ge(hm_ready, NORM_ITEMS)
            act.wait_ge(hms_ready, 1)

            def v_out(j, g):
                bank = when_full(act, ("v", j, g))
                s.activation(blk(V, j, g), bank[:, 0:GROUPS[g][1]], ACT.Copy).then_inc(free_of(("v", j, g)), 1)
                slot()

            def split_in(n, src):
                split_hi(n % 2, n // 2, full_at(src), raw_slot(n))

            for g in range(3):
                for j in range(2):
                    v_out(j, g)
                    if g == 2:
                        split_in(j + 2, ("v", j, 2))
            for j in range(2, JB):
                for g in range(3):
                    v_out(j, g)
                split_in(j + 2, ("v", j, 2))
            act.wait_ge(lam_step, 1)
            s.activation(lam[:, 1, :], lam[:, 0, :], ACT.Exp, scale=-1.0).then_inc(lam_exp, 1)

            def v_copy(t):
                bank = when_full(act, ("vt", t))
                r = tile_rows(t)
                s.activation(V[0:r, :, P * t:P * t + P], bank[0:r, :].rearrange("p (j d) -> p j d", j=JB),
                             ACT.Copy).then_inc(free_of(("vt", t)), 1)

            for j in range(JB):
                if j > 0:
                    act.wait_ge(term_done, j)
                for g in range(2):
                    bank = when_full(act, ("xr", j, g))
                    c, n = GROUPS[g]
                    s.activation(row[:, row_tok + c:row_tok + c + n], bank[:, 0:n], ACT.Copy
                                 ).then_inc(free_of(("xr", j, g)), 1)
                    slot()
                bank = when_full(act, ("xr", j, 2))
                c = row_tok + GROUPS[2][0]
                s.activation(row[:, c:c + PROMPT_G2], bank[:, 0:PROMPT_G2], ACT.Copy)
                s.activation(smp(row, seg0 + HALO, TB), by_sample(bank[:, PROMPT_G2:PROMPT_G2 + T_SAMPLE]), ACT.Copy
                             ).then_inc(free_of(("xr", j, 2)), 1)
                slot()
                split_in(U_RG + 2 * j + 2, ("xr", j, 2))
                when_read(act, ("xr", j, 2))
                act.wait_ge(halo_done, 2 * j + 2)
                if j > 0:
                    act.wait_ge(ix_done, j)
                s.activation(xc[:, 0:SCAN_W], row[:, 0:SCAN_W], ACT.Identity, bias=r5[:, j, R_CB:R_CB + 1],
                             scale=r5[:, j, R_CW:R_CW + 1]).then_inc(tap_done, 1)
                if j < 3:
                    v_copy(3 * j)
                for g in range(3):
                    bank = when_full(act, ("yg", j, g))
                    s.activation(blk(RG, j, g), bank[:, 0:GROUPS[g][1]], ACT.Gelu_apprx_tanh
                                 ).then_inc(free_of(("yg", j, g)), 1)
                    slot()
                    if j < 3 and g > 0:
                        v_copy(3 * j + g)
                split_in(U_RG + 2 * j + 3, ("yg", j, 2))
                if j > 0:
                    act.wait_ge(rg_done, j)
                    act.wait_ge(h_tail, j)
                for name, dst, bias in (("gr", rr, R_BRA), ("gi", ig, R_BRI)):
                    for g, (c, n) in enumerate(SCAN_GROUPS):
                        bank = when_full(act, (name, j, g))
                        s.activation(dst[:, c:c + n], bank[:, 0:n], ACT.Sigmoid, bias=r5[:, j, bias:bias + 1]
                                     ).then_inc(free_of((name, j, g)), 1)
                when_read(act, ("gr", j, 2))
                act.wait_ge(lam_step, LAM_STEPS)
                s.activation(aa[:, 0:SCAN_W], rr[:, 0:SCAN_W], ACT.Exp, scale=decay[:, j:j + 1]).then_inc(decay_done, 1)
                act.wait_ge(decay_done, j + 1)
                s.activation(rr[:, 0:SCAN_W], rr[:, 0:SCAN_W], ACT.Tanh, scale=decay_n[:, j:j + 1]).then_inc(act_chain, 1)
                act.wait_ge(row_read, j + 1)
                act.wait_ge(tap_done, 4 * j + 4)
                s.activation(row[:, 0:SCAN_W], aa[:, 0:SCAN_W], ACT.Square).then_inc(act_chain, 1)
                act.wait_ge(q_done, j + 1)
                s.activation(row[:, 0:SCAN_W], row[:, 0:SCAN_W], ACT.Sqrt).then_inc(root_done, 1)
                if j == 2:
                    act.wait_ge(v_stat, 2 * NT)
                    for r, t0, t1 in by_rows(range(NT)):
                        s.activation(v_std[0:r, t0:t1], mv[0:r, t0:t1, 1], ACT.Sqrt, bias=eps[0:r, :]
                                     ).then_inc(v_std_done, 1)

            def rg_square(j):
                if j >= 2:
                    act.wait_ge(rgsum, 1)
                s.activation(sq_rg[:, j % 2, 0:T], RG[:, j, :], ACT.Square).then_inc(rgsq, 1)

            def sg_square(i):
                j, g = SG_ORDER[i]
                when_read(act, ("u", j, g))
                if i >= 5:
                    act.wait_ge(sgsum, i - 4)
                n = GROUPS[g][1]
                s.activation(cols(ss_sg, g) if j == 0 else sq_g[:, i % 2, 0:n], blk(V, j, g), ACT.Square
                             ).then_inc(sgsq, 1)

            def branch_hi(g, j0=0, j1=JB):
                act.wait_ge(*full_at(("u", JB - 1, g)))
                for j in range(j0, j1):
                    act.wait_ge(rg_norm, JB * g + j + 1)
                    s.activation(blk(act_hi, j, g), blk(RG, j, g), ACT.Copy).then_inc(mrg_hi, 1)

            def gate_hi(g, j0=0, j1=JB):
                for j in range(j0, j1):
                    act.wait_ge(sg_norm, JB * g + j + 1)
                    s.activation(blk(act_hi, JB + j, g), blk(V, j, g), ACT.Copy).then_inc(msg_hi, 1)

            for i in range(3):
                slot()
            act.wait_ge(rg_done, JB)
            act.wait_ge(h_tail, JB)
            rg_square(0)
            rg_square(1)
            for i, (j, g) in enumerate(SG_ORDER):
                if i >= 3:
                    slot()
                if i == len(SG_ORDER) - 1:
                    split_in(U_OUT + 1, ("u", JB - 1, 2))
                sg_square(i)
                if i == 1:
                    rg_square(2)
                    rg_square(3)
                if i in (2, 5):
                    split_in(U_U + j + 2, ("u", j, 2))
                if i == 6:
                    root("ss_rg", "rg", range(NT), D_RG)
                if (j, g) == (JB - 2, 1):
                    branch_hi(0)
                    root(("ss_sg", 0), ("sg", 0), TILES_OF[0], D_SG)
                if (j, g) == (JB - 2, 2):
                    split_in(U_OUT, ("u", JB - 2, 2))
                    gate_hi(0)

            def x1_square(g, o):
                i = KD * g + o
                if g < 2:
                    when_read(act, ("out", o, g))
                else:
                    act.wait_ge(x1_smp, o + 1)
                if i == 1:
                    act.wait_ge(sgsum, 3 * (JB - 1))
                if i >= 3:
                    act.wait_ge(x1sum, (KD - 1) * ((i - 2) // KD) + (i - 2) % KD)
                n = GROUPS[g][1]
                s.activation(cols(ss_x, g) if o == 0 else sq_g[:, i % 2, 0:n], blk(xT, o, g), ACT.Square
                             ).then_inc(x1sq, 1)

            def tails_copy():
                bank = when_full(act, "tails")
                s.activation(tails_out[0:TAILS, :], bank[0:TAILS, :], ACT.Copy).then_inc(free_of("tails"), 1)

            hf = norm_hi_items
            behind = {
                (0, 0): lambda: root(("ss_sg", 1), ("sg", 1), TILES_OF[1], D_SG),
                (0, 5): lambda: root(("ss_sg", 2), ("sg", 2), TILES_OF[2], D_SG),
                (1, 1): lambda: root(("ss_x1", 0), ("x1", 0), TILES_OF[0], D),
                (1, 4): tails_copy,
                (2, 1): lambda: root(("ss_x1", 1), ("x1", 1), TILES_OF[1], D),
            }
            for g in range(3):
                for o in range(KD):
                    i = KD * g + o
                    split_in(U_OUT + i + 2, ("out", o, g))
                    x1_square(g, o)
                    if (g, o) in behind:
                        behind[g, o]()
                    if (g, o) in MERGE_AT:
                        part, gm, j0, j1 = MERGE_AT[g, o]
                        (branch_hi if part == "rg" else gate_hi)(gm, j0, j1)
                    hf(HF_AT[i], HF_AT[i + 1])
            hf(HF_AT[3 * KD], 2 * KD)
            root(("ss_x1", 2), ("x1", 2), TILES_OF[2], D)
            hf(2 * KD, NORM_ITEMS)

            def hidden_hi(b, pair, next_unit=None, first=False):
                def next_hi(c):
                    split_hi(c, next_unit, (full[3 * c + 2], ff1_turn(b) + 1))

                for i, (c, g) in enumerate(FIRST_ORDER if first else HIDDEN_ORDER):
                    n = GROUPS[g][1]
                    bank = 3 * c + g
                    if first and g == 2:
                        next_hi(c)
                    act.wait_ge(full[bank], ff1_turn(b) + 1)
                    if not (first and i < 2):
                        act.wait_ge(h_ready, 6 * b + i - 1)
                    s.activation(relu[:, i % 2, 0:n], psum[bank][:, 0:n], ACT.Relu).then_inc(relu_done, 1)
                    act.wait_ge(relu_done, 6 * b + i + 1)
                    s.activation(blk(h_hi, 2 * pair + c, g), relu[:, i % 2, 0:n], ACT.Square).then_inc(hhi_done, 1)
                    if next_unit is not None and g == 2 and not first:
                        next_hi(c)

            def back_hi(b, next_unit):
                for h in range(2):
                    if next_unit is not None:
                        split_hi(h, next_unit, (full[5], ff2_turn(b) + 2 * h + 2))

            hidden_hi(0, 0, ff1_half(1), first=True)
            with act.Fori(0, (FF_BLOCKS - 2) // 2) as m:
                hidden_hi(2 * m + 1, 1, ff2_half(2 * m))
                back_hi(2 * m, ff1_half(2 * m + 2))
                hidden_hi(2 * m + 2, 0, ff2_half(2 * m + 1))
                back_hi(2 * m + 1, ff1_half(2 * m + 3))
            hidden_hi(FF_BLOCKS - 1, 1, ff2_half(FF_BLOCKS - 2))
            back_hi(FF_BLOCKS - 2, ff2_half(FF_BLOCKS - 1))

            def y_out(q):
                t, h = Y_HALVES[q]
                r = tile_rows(t)
                bank = when_full(act, ("y", t, h))
                act.wait_ge(rstd_done, SCALE_NO["y", LAST_GROUPS[q // 6]])
                s.activation(yout[0:r, t, 512 * h:512 * h + 512], bank[0:r, :], ACT.Copy, scale=rstd[0:r, t:t + 1]
                             ).then_inc(free_of(("y", t, h)), 1)

            for n, (g, o) in enumerate(LAST_ORDER):
                if g < 2:
                    bank, turns = last_tile(n)
                    act.wait_ge(free[bank], turns + 1)
                else:
                    act.wait_ge(y_smp, 2 * o + 2)
                if n >= 3:
                    act.wait_ge(ysum, y_adds(n - 2))
                width = GROUPS[g][1]
                s.activation(cols(ss_x, g) if o == 0 else sq_g[:, n % 2, 0:width], blk(xT, o, g), ACT.Square
                             ).then_inc(ysq, 1)
                s.activation(blk(xg, o, g), blk(xT, o, g), ACT.Copy, scale=vecs[:, V_GFIN + o:V_GFIN + o + 1]
                             ).then_inc(xg_done, 1)
                if n in Y_ROOT_AT:
                    gs = LAST_GROUPS[Y_ROOT_AT.index(n)]
                    root(("ss_y", gs), ("y", gs), TILES_OF[gs], D)
                if n in ACT_Y_OUT_AT:
                    y_out(ACT_Y_OUT_AT[n])
            y_out(9)
            root(("ss_y", 1), ("y", 1), TILES_OF[1], D)
            y_out(11)
            for q in (13, 15, 17):
                y_out(q)

        @block.vector
        def _(dve):
            v = nc.vector

            for t in range(NT):
                if t == 4:
                    dve.wait_ge(pool_set, 9)
                    v.tensor_copy(eye8[0:TB], ident[0:TB, 0:TB].unsqueeze(1).to_broadcast([TB, NB, TB])
                                  ).then_inc(eye_ready, 1)
                    v.tensor_tensor(sel[PB:PE_ROWS, :], ident[PB:PE_ROWS, PB:PB + NC], ident[PB:PE_ROWS, PB + NC:PB + 2 * NC],
                                    ALU.add).then_inc(eye_ready, 1)
                r = tile_rows(t)
                for h in range(2):
                    bank = when_full(dve, ("x", t, h))
                    v.tensor_copy(xT[:, 4 * h:4 * h + 4, P * t:P * t + r],
                                  bank[:, 0:4 * r].rearrange("p (k c) -> p k c", k=4)).then_inc(free_of(("x", t, h)), 1)
                if t == 5:
                    dve.wait_ge(silu_step, 1)
                    bank = when_full(dve, "cond")
                    v.tensor_tensor(silu[:], silu[:], bank[:, 0:KD * NC].rearrange("p (k c) -> p k c", k=KD), ALU.mult
                                    ).then_inc(free_of("cond"), 1)
                if t == 7:
                    dve.wait_ge(silu_step, 2)
                    v.tensor_tensor(silu2[:, :, NC:2 * NC], silu[:], f32(silu2[:, :, 0:NC]), ALU.subtract
                                    ).then_inc(silu_ready, 1)

            def inverse(scale, tiles):
                for i, (r, t0, t1) in enumerate(by_rows(tiles)):
                    ins = v.reciprocal(rstd[0:r, t0:t1], std[0:r, t0:t1])
                ins.then_inc(rstd_done, 1)

            dve.wait_ge(std_done, 1)
            inverse("x", range(NT))

            when_read(dve, ("x", NT - 1, 0))
            when_read(dve, ("x", NT - 1, 1))
            def early_lo(u):
                dve.wait_ge(ada_hi_done, u + 1)
                v.tensor_tensor(ada_w_lo[:, u, :], ada_w[:, u, :], f32(early_hi(u)), ALU.subtract
                                ).then_inc(ada_lo_dve, 1)

            early_units = iter(DVE_UNITS)
            for g in range(3):
                if g == 1:
                    bank = when_full(dve, "vecs")
                    v.tensor_copy(vecs[:], bank[:, 0:N_VECS]).then_inc(free_of("vecs"), 1)
                bank = when_full(dve, ("bcx", g))
                for k in range(KD):
                    ins = v.tensor_tensor(blk(xn, k, g), blk(xT, k, g), bank[:, 0:GROUPS[g][1]], ALU.mult)
                    if k == KD - 1:
                        ins.then_inc(free_of(("bcx", g)), 1)
                    if (KD * g + k) % 3 == 2:
                        early_lo(next(early_units))
            for u in early_units:
                early_lo(u)

            def split_lo(slot, half, raw=None):
                dve.wait_ge(hi_done[slot], half + 1)
                v.tensor_tensor(w_lo[:, slot, :], w_raw[:, slot if raw is None else raw, :], f32(w_hi[:, slot, :]),
                                ALU.subtract).then_inc(lo_done[slot], 1)

            def split_in(n):
                split_lo(n % 2, n // 2, raw_slot(n))

            def early_modulation(name, m0, m1):
                bank = when_full(dve, name)
                v.tensor_tensor(ada_e[:, m0:m1, :], bank[:, 0:NC * (m1 - m0)].rearrange("p (m c) -> p m c", c=NC),
                                bada[:, m0:m1].unsqueeze(2).to_broadcast([P, m1 - m0, NC]), ALU.add
                                ).then_inc(free_of(name), 1)
                when_read(dve, name)
                k0, k1 = max(0, m0 - KD), m1 - KD
                v.scalar_tensor_tensor(gain_m[:, k0:k1, :], ada_e[:, KD + k0:KD + k1], 1.0,
                                       vecs[:, V_GMIX + k0:V_GMIX + k1].unsqueeze(2).to_broadcast([P, k1 - k0, NC]),
                                       ALU.add, ALU.mult).then_inc(ada_ready, 1)

            first_k = KD - PIECE // P
            early_modulation("ada1", 0, ADA_EARLY - PIECE // P)
            dve.wait_ge(ada_ready, 1)

            def release(name, done, count):
                dve.wait_ge(done, count)
                dve.sem_inc(free_of(name), 1)

            pending = [None]

            def norm_items(n0, n1):
                def lower(i):
                    dve.wait_ge(norm_hi, i + 1)
                    g, k = i // KD, i % KD
                    n = GROUPS[g][1] if g < 2 else PROMPT_G2
                    v.scalar_tensor_tensor(blk(act_lo, k, g, n), tmp1[:, i % 2, 0:n], ada_late[:, KD + k, 0:1],
                                           f32(blk(act_hi, k, g, n)), ALU.add, ALU.subtract).then_inc(act_ready, 1)

                for i in range(n0, n1):
                    g, k = i // KD, i % KD
                    bank = when_full(dve, ("bcx1", g))
                    if i == 2 * KD:
                        dve.wait_ge(tails_stored, 64)
                        sc = bank[:, PROMPT_G2:PROMPT_G2 + T_SAMPLE]
                        v.tensor_tensor(smp1[:], xT[:, :, T_PROMPT:T],
                                        sc.unsqueeze(1).to_broadcast([P, KD, T_SAMPLE]), ALU.mult
                                        ).then_inc(hfs_step, 1)
                    n = GROUPS[g][1] if g < 2 else PROMPT_G2
                    if i >= 2:
                        dve.wait_ge(act_ready, i - 1)
                    v.scalar_tensor_tensor(tmp1[:, i % 2, 0:n], blk(xT, k, g, n), gain_f[:, k, 0:1],
                                           bank[:, 0:n], ALU.mult, ALU.mult).then_inc(norm_tmp, 1)
                    if pending[0] is not None:
                        lower(pending[0])
                    pending[0] = i
                    if k == KD - 1:
                        lower(i)
                        pending[0] = None
                        release(("bcx1", g), act_ready, i + 1)

            def lower_hm(i):
                g, k = i // KD, i % KD
                n = GROUPS[g][1] if g < 2 else PROMPT_G2
                dve.wait_ge(hm_hi, i + 1)
                v.tensor_tensor(blk(act_lo, k, g, n), blk(xn, k, g, n), f32(blk(act_hi, k, g, n)), ALU.subtract
                                ).then_inc(hm_ready, 1)

            for g in range(3):
                when_read(dve, ("bcx", g))
            for i in range(NORM_ITEMS):
                g, k = i // KD, i % KD
                n = GROUPS[g][1] if g < 2 else PROMPT_G2
                if i == first_k:
                    early_modulation("ada1_end", ADA_EARLY - PIECE // P, ADA_EARLY)
                    dve.wait_ge(ada_ready, 2)
                v.tensor_scalar(blk(xn, k, g, n), blk(xn, k, g, n), gain_m[:, k, 0:1], ada_e[:, k, 0:1],
                                ALU.mult, ALU.add).then_inc(hm_mod, 1)
                if i > 0:
                    lower_hm(i - 1)
                if i == KD:
                    split_lo(1, 0)
            lower_hm(NORM_ITEMS - 1)
            split_in(2)
            split_in(3)

            bank = when_full(dve, "rows512")
            v.tensor_copy(r5[:], bank[:, 0:JB * R512].rearrange("p (j r) -> p j r", j=JB)
                          ).then_inc(free_of("rows512"), 1)
            when_read(dve, "rows512")
            raw_l = r5[:, :, R_LRU]
            v.scalar_tensor_tensor(lam[:, 0, :], raw_l, -1.0, raw_l, ALU.mult, ALU.max).then_inc(lam_step, 1)
            for half in range(2):
                bank = when_full(dve, f"ws{half}")
                v.tensor_copy(wsT[:, 4 * half:4 * half + 4], bank[:].rearrange("p (h t) -> p h t", h=4)
                              ).then_inc(free_of(f"ws{half}"), 1)
            split_in(4)
            bank = when_full(dve, "wsmall")
            small = bank[0:64, 0:64].rearrange("p (h t) -> p h t", h=HEADS).unsqueeze(2).to_broadcast([64, HEADS, NB, TB])
            mask = own[0:64].unsqueeze(1).unsqueeze(3).to_broadcast([64, HEADS, NB, TB])
            v.tensor_tensor(ws64[0:64], small, mask, ALU.mult).then_inc(free_of("wsmall"), 1)
            bank = when_full(dve, "rowsum")
            dve.wait_ge(bs_in, 32)
            for j in range(JB):
                ins = v.scalar_tensor_tensor(mix_b[:, j, :], bank[:, CHUNK * j:CHUNK * j + CHUNK],
                                             r5[:, j, R_LNB:R_LNB + 1], mix_b[:, j, :], ALU.mult, ALU.add)
            ins.then_inc(free_of("rowsum"), 1)
            split_in(5)

            steps = [1]

            def step(ins):
                steps[0] += 1
                ins.then_inc(lam_step, 1)
                dve.wait_ge(lam_step, steps[0])

            u, num, s1, s2, ser, low = (lam[:, i, :] for i in (1, 2, 3, 4, 5, 6))
            dve.wait_ge(lam_exp, 1)
            step(v.tensor_scalar(num, u, 2.0, None, ALU.add))
            step(v.reciprocal(num, num))
            step(v.tensor_tensor(s1, u, num, ALU.mult))
            step(v.tensor_tensor(s2, s1, s1, ALU.mult))
            step(v.tensor_scalar(ser, s2, 1.0 / 17.0, None, ALU.mult))
            for d in (15, 13, 11, 9, 7, 5, 3):
                step(v.scalar_tensor_tensor(ser, ser, 1.0 / d, s2, ALU.add, ALU.mult))
            step(v.scalar_tensor_tensor(ser, ser, 1.0, s1, ALU.add, ALU.mult))
            step(v.tensor_scalar(low, raw_l, 0.0, None, ALU.min))
            step(v.scalar_tensor_tensor(low, ser, -2.0, low, ALU.mult, ALU.add))
            step(v.tensor_scalar(decay[:], low, LRU_C, None, ALU.mult))
            step(v.tensor_scalar(decay_n[:], low, -LRU_C, None, ALU.mult))
            assert steps[0] == LAM_STEPS


            def v_stats(t):
                when_read(dve, ("vt", t))
                r = tile_rows(t)
                v.bn_stats(bn[0:r, t, :], V[0:r, :, P * t:P * t + P]).then_inc(v_stat, 1)
                dve.wait_ge(v_stat, 2 * t + 1)
                v.bn_aggr(mv[0:r, t, :], bn[0:r, t, :]).then_inc(v_stat, 1)

            for j in range(JB):
                split_in(U_RG + 2 * j + 2)
                for k in range(1, CONV_W):
                    dve.wait_ge(tap_done, 4 * j + k)
                    v.scalar_tensor_tensor(xc[:, 0:SCAN_W], row[:, k:k + SCAN_W], r5[:, j, R_CW + k:R_CW + k + 1],
                                           xc[:, 0:SCAN_W], ALU.mult, ALU.add).then_inc(tap_done, 1)
                if j < 3:
                    for i in range(3):
                        v_stats(3 * j + i)
                else:
                    dve.wait_ge(v_std_done, 2)
                    for r, t0, t1 in by_rows(range(NT)):
                        v.reciprocal(v_std[0:r, t0:t1], v_std[0:r, t0:t1]).then_inc(v_norm, 1)
                    dve.wait_ge(v_norm, 2)
                    dve.wait_ge(vrows_out, 32)
                    for t in range(NT):
                        r = tile_rows(t)
                        v.tensor_scalar(V[0:r, :, P * t:P * t + P], V[0:r, :, P * t:P * t + P], mv[0:r, t, 0:1],
                                        v_std[0:r, t:t + 1], ALU.subtract, ALU.mult).then_inc(v_norm, 1)
                split_in(U_RG + 2 * j + 3)
                if j == JB - 1:
                    for jj in range(JB):
                        gain = r5[:, jj, R_LNG:R_LNG + 1]
                        for g in range(2):
                            bank = when_full(dve, ("mix", jj, g))
                            v.scalar_tensor_tensor(
                                V[:, jj, 512 * g:512 * g + 512].rearrange("p (c t) -> p c t", t=CHUNK),
                                bank[:].rearrange("p (c t) -> p c t", t=CHUNK), gain,
                                mix_b[:, jj, :].unsqueeze(1).to_broadcast([P, 4, CHUNK]), ALU.mult, ALU.add
                            ).then_inc(free_of(("mix", jj, g)), 1)
                        bank = when_full(dve, ("mix", jj, 2))
                        v.scalar_tensor_tensor(
                            by_sample(V[:, jj, T_PROMPT:T]), by_sample(bank[:, 0:T_SAMPLE]), gain,
                            mix_b[:, jj, 0:TB].unsqueeze(1).to_broadcast([P, NB, TB]), ALU.mult, ALU.add
                        ).then_inc(free_of(("mix", jj, 2)), 1)
                dve.wait_ge(act_chain, 2 * j + 2)
                v.scalar_tensor_tensor(row[:, 0:SCAN_W], row[:, 0:SCAN_W], 1.0, rr[:, 0:SCAN_W],
                                       ALU.add, ALU.mult).then_inc(q_done, 1)
                dve.wait_ge(root_done, j + 1)
                dve.wait_ge(ix_done, j + 1)
                v.tensor_tensor(ig[:, 1:SCAN_W], row[:, 1:SCAN_W], ig[:, 1:SCAN_W], ALU.mult).then_inc(term_done, 1)
                v.memset(smp(aa, seg0 - 1, 1), 0.0).then_inc(scan_done, 1)
                dve.wait_ge(term_done, j + 1)
                v.tensor_copy(smp(ig, seg0 - 1, 1), r5[:, j, R_H0:R_H0 + NB].unsqueeze(2)).then_inc(scan_done, 1)
                dve.wait_ge(scan_done, 3 * j + 2)
                v.tensor_tensor_scan(rr[:, 0:SCAN_W], aa[:, 0:SCAN_W], ig[:, 0:SCAN_W], 0.0, ALU.mult, ALU.add
                                     ).then_inc(scan_done, 1)
                dve.wait_ge(scan_done, 3 * j + 3)
                when_read(dve, ("yg", j, 2))
                v.tensor_tensor(RG[:, j, 0:T_PROMPT], RG[:, j, 0:T_PROMPT], rr[:, 0:T_PROMPT], ALU.mult)
                v.tensor_tensor(by_sample(RG[:, j, T_PROMPT:T]), by_sample(RG[:, j, T_PROMPT:T]), smp(rr, seg0, TB),
                                ALU.mult).then_inc(rg_done, 1)

            def gate(j, g):
                bank = when_full(dve, ("u", j, g))
                v.tensor_tensor(blk(V, j, g), bank[:, 0:GROUPS[g][1]], blk(V, j, g), ALU.mult
                                ).then_inc(free_of(("u", j, g)), 1)

            def add_sg(i):
                j, g = SG_ORDER[i]
                dve.wait_ge(sgsq, i + 1)
                if j == 0:
                    return
                if i >= 4:
                    dve.wait_ge(sgsum, i - 3)
                v.tensor_tensor(cols(ss_sg, g), cols(ss_sg, g), sq_g[:, i % 2, 0:GROUPS[g][1]], ALU.add
                                ).then_inc(sgsum, 1)

            def norm_rg(g, j0=0, j1=JB):
                bank = when_full(dve, ("bcrg", g))
                for j in range(j0, j1):
                    v.scalar_tensor_tensor(blk(RG, j, g), blk(RG, j, g), r5[:, j, R_GRG:R_GRG + 1],
                                           bank[:, 0:GROUPS[g][1]], ALU.mult, ALU.mult).then_inc(rg_norm, 1)
                if j1 == JB:
                    release(("bcrg", g), rg_norm, JB * (g + 1))

            def norm_sg(g, j0=0, j1=JB):
                def lower(j):
                    dve.wait_ge(msg_hi, j + 1)
                    v.tensor_tensor(blk(act_lo, JB + j, 0), blk(V, j, 0), f32(blk(act_hi, JB + j, 0)), ALU.subtract
                                    ).then_inc(msg0_ready, 1)

                bank = when_full(dve, ("bcsg", g))
                for j in range(j0, j1):
                    v.scalar_tensor_tensor(blk(V, j, g), blk(V, j, g), r5[:, j, R_GSG:R_GSG + 1],
                                           bank[:, 0:GROUPS[g][1]], ALU.mult, ALU.mult).then_inc(sg_norm, 1)
                    if g == 0 and j > 0:
                        lower(j - 1)
                if g == 0:
                    lower(JB - 1)
                if j1 == JB:
                    release(("bcsg", g), sg_norm, JB * (g + 1))

            def late_modulation():
                when_read(dve, ("turned", L_PIECES - 1))
                v.tensor_tensor(ada_late[:], ada_late[:], bada[:, ADA_EARLY:N_ADA].unsqueeze(2)
                                .to_broadcast([P, N_ADA - ADA_EARLY, NC]), ALU.add).then_inc(ada_ready, 1)
                dve.wait_ge(ada_ready, 3)
                v.scalar_tensor_tensor(gain_f[:], ada_late[:, 2 * KD:3 * KD], 1.0,
                                       vecs[:, V_GFFN:V_GFFN + KD].unsqueeze(2).to_broadcast([P, KD, NC]), ALU.add, ALU.mult
                                       ).then_inc(ada_ready, 1)

            def scale(name, scale_name, tiles):
                when_read(dve, name)
                inverse(scale_name, tiles)

            for i, (j, g) in enumerate(SG_ORDER):
                gate(j, g)
                if i > 0:
                    add_sg(i - 1)
                if i in (1, 3, 4):
                    jr = (1, 3, 4).index(i) + 1
                    dve.wait_ge(rgsq, jr + 1)
                    dve.wait_ge(h_tail, JB)
                    if jr > 1:
                        dve.wait_ge(rgsum, jr - 1)
                    v.tensor_tensor(ss_rg[:], sq_rg[:, 0, 0:T] if jr == 1 else ss_rg[:], sq_rg[:, jr % 2, 0:T], ALU.add
                                    ).then_inc(rgsum, 1)
                if i in (2, 5):
                    split_in(U_U + j + 2)
                if i == 6:
                    scale("ss_rg", "rg", range(NT))
                if (j, g) == (JB - 2, 1):
                    norm_rg(0)
                if (j, g) == (JB - 1, 1):
                    scale(("ss_sg", 0), ("sg", 0), TILES_OF[0])
                if (j, g) == (JB - 2, 2):
                    split_in(U_OUT)
                    norm_sg(0)
            split_in(U_OUT + 1)
            add_sg(len(SG_ORDER) - 1)
            late_modulation()

            def add_out(o, g):
                gt = ada_late[:, o, :]
                bank = when_full(dve, ("out", o, g))
                n = GROUPS[g][1] if g < 2 else PROMPT_G2
                ins = v.scalar_tensor_tensor(blk(xT, o, g, n), bank[:, 0:n], gt[:, 0:1], blk(xT, o, g, n),
                                             ALU.mult, ALU.add)
                if g < 2:
                    ins.then_inc(free_of(("out", o, g)), 1)
                    return
                if o > 0:
                    dve.wait_ge(x1_smp, o)
                v.tensor_tensor(by_sample(smp_t[:]), by_sample(bank[:, PROMPT_G2:PROMPT_G2 + T_SAMPLE]),
                                gt[:, 1:NC].unsqueeze(2).to_broadcast([P, NB, TB]), ALU.mult
                                ).then_inc(free_of(("out", o, 2)), 1)
                when_read(dve, ("out", o, 2))
                v.tensor_tensor(xT[:, o, T_PROMPT:T], xT[:, o, T_PROMPT:T], smp_t[:], ALU.add).then_inc(x1_smp, 1)

            def add_x1(i):
                sum_x1_squares(dve, v, i)

            hf = norm_items
            behind = {
                (0, 1): lambda: scale(("ss_sg", 1), ("sg", 1), TILES_OF[1]),
                (0, 6): lambda: scale(("ss_sg", 2), ("sg", 2), TILES_OF[2]),
                (1, 2): lambda: scale(("ss_x1", 0), ("x1", 0), TILES_OF[0]),
                (2, 2): lambda: scale(("ss_x1", 1), ("x1", 1), TILES_OF[1]),
            }
            for g in range(3):
                for o in range(KD):
                    i = KD * g + o
                    if (g, o) in behind:
                        behind[g, o]()
                    add_out(o, g)
                    if 0 < i <= KD:
                        add_x1(i - 1)
                    split_in(U_OUT + i + 2)
                    if (g, o) in MERGE_AT:
                        part, gm, j0, j1 = MERGE_AT[g, o]
                        (norm_rg if part == "rg" else norm_sg)(gm, j0, j1)
                    hf(HF_AT[i], HF_AT[i + 1])
            hf(HF_AT[3 * KD], 2 * KD)
            scale(("ss_x1", 2), ("x1", 2), TILES_OF[2])
            hf(2 * KD, NORM_ITEMS)

            def hidden_square(b, next_unit=None, first=False):
                for i, (c, g) in enumerate(FIRST_ORDER if first else HIDDEN_ORDER):
                    n = GROUPS[g][1]
                    bank = 3 * c + g
                    if first and g == 2:
                        split_lo(c, next_unit)
                    dve.wait_ge(relu_done, 6 * b + i + 1)
                    if not (first and i < 2):
                        dve.wait_ge(h_ready, 6 * b + i - 1)
                    v.scalar_tensor_tensor(sqr[:, i % 2, 0:n], psum[bank][:, 0:n], 0.0, relu[:, i % 2, 0:n],
                                           ALU.max, ALU.mult).then_inc(free[bank], 1)
                    if next_unit is not None and g == 2 and not first:
                        split_lo(c, next_unit)

            def add_back(b, o, g):
                bank = 3 * (o % 2) + g
                dve.wait_ge(full[bank], ff2_turn(b) + o // 2 + 1)
                n = GROUPS[g][1] if g < 2 else PROMPT_G2
                ins = v.scalar_tensor_tensor(blk(xT, o, g, n), psum[bank][:, 0:n], ada_late[:, 3 * KD + o, 0:1],
                                             blk(xT, o, g, n), ALU.mult, ALU.add)
                if g == 2:
                    ins = v.tensor_tensor(smp_acc[:, o, :], smp_acc[:, o, :],
                                          psum[bank][:, PROMPT_G2:PROMPT_G2 + T_SAMPLE], ALU.add)
                ins.then_inc(free[bank], 1)

            def back_add(b, next_unit):
                for h in range(2):
                    for i in range(4):
                        for g in range(3):
                            add_back(b, 4 * h + i, g)
                    split_lo(h, next_unit)

            dve.wait_ge(smp_zero, 1)
            hidden_square(0, ff1_half(1), first=True)
            with dve.Fori(0, (FF_BLOCKS - 2) // 2) as m:
                hidden_square(2 * m + 1, ff2_half(2 * m))
                back_add(2 * m, ff1_half(2 * m + 2))
                hidden_square(2 * m + 2, ff2_half(2 * m + 1))
                back_add(2 * m + 1, ff1_half(2 * m + 3))
            hidden_square(FF_BLOCKS - 1, ff2_half(FF_BLOCKS - 2))
            back_add(FF_BLOCKS - 2, ff2_half(FF_BLOCKS - 1))

            def y_out(q):
                t, h = Y_HALVES[q]
                r = tile_rows(t)
                bank = when_full(dve, ("y", t, h))
                dve.wait_ge(rstd_done, SCALE_NO["y", LAST_GROUPS[q // 6]])
                v.tensor_scalar(yout[0:r, t, 512 * h:512 * h + 512], bank[0:r, :], rstd[0:r, t:t + 1], None, ALU.mult
                                ).then_inc(free_of(("y", t, h)), 1)

            for m, (g, o) in enumerate(LAST_ORDER):
                if m - 1 in Y_SUM_AT:
                    gs = LAST_GROUPS[Y_SUM_AT.index(m - 1)]
                    scale(("ss_y", gs), ("y", gs), TILES_OF[gs])
                bank, turns = last_tile(m)
                dve.wait_ge(full[bank], turns + 1)
                n = GROUPS[g][1] if g < 2 else PROMPT_G2
                ins = v.scalar_tensor_tensor(blk(xT, o, g, n), psum[bank][:, 0:n], ada_late[:, 3 * KD + o, 0:1],
                                             blk(xT, o, g, n), ALU.mult, ALU.add)
                if g == 2:
                    ins = v.tensor_tensor(smp_acc[:, o, :], smp_acc[:, o, :],
                                          psum[bank][:, PROMPT_G2:PROMPT_G2 + T_SAMPLE], ALU.add)
                ins.then_inc(free[bank], 1)
                if g == 2:
                    dve.wait_ge(free[bank], turns + 1)
                    if o > 0:
                        dve.wait_ge(y_smp, 2 * o)
                    v.tensor_tensor(by_sample(smp_t[:]), by_sample(smp_acc[:, o, :]),
                                    ada_late[:, 3 * KD + o, 1:NC].unsqueeze(2).to_broadcast([P, NB, TB]),
                                    ALU.mult).then_inc(y_smp, 1)
                    dve.wait_ge(y_smp, 2 * o + 1)
                    v.tensor_tensor(xT[:, o, T_PROMPT:T], xT[:, o, T_PROMPT:T], smp_t[:], ALU.add).then_inc(y_smp, 1)
                if m > 2 * KD:
                    add_y(dve, v, m - 1)
                if m in Y_TURN_AT and Y_TURN_AT[m] % 2 == 0:
                    y_out(Y_TURN_AT[m])
            add_y(dve, v, 3 * KD - 1)
            y_out(8)
            scale(("ss_y", 1), ("y", 1), TILES_OF[1])
            y_out(10)
            for q in (12, 14, 16):
                y_out(q)


_INS = ['x_prompt', 'x_sample', 'c_prompt', 'c_sample', 'state_conv', 'state_rglru', 'w_ada', 'b_ada', 'g_mix',
        'g_ffn', 'w_in', 'conv_w', 'conv_b', 'w_ra', 'b_ra', 'w_ri', 'b_ri', 'lru_l', 'ln_v_g', 'ln_v_b', 'w_s',
        'b_s', 'g_rg', 'g_sg', 'w_out', 'w_ff1', 'w_ff2', 'g_final']
_OUTS = [(1, T_PROMPT, D), (NB, TB, D), (1, 1, HALO, D_RG), (1, 1, D_RG), (1, 1, CHUNK, D_SG),
         (1, NB, HALO, D_RG), (1, NB, D_RG), (1, NB, TB, D_SG)]


def kernel(**inputs):
    import numpy as _np
    import concourse.bacc as _bacc
    from concourse import mybir as _mybir
    from concourse.bass_utils import run_bass_kernel_spmd as _run

    nc = _bacc.Bacc("TRN2", target_bir_lowering=False, num_devices=1)
    arrays, args = {}, {}
    for name in _INS:
        x = _np.ascontiguousarray(inputs[name])
        arrays[f"in_{name}"] = x
        args[name] = nc.dram_tensor(f"in_{name}", x.shape, _mybir.dt.from_np(x.dtype), kind="ExternalInput").ap()
    outs = [nc.dram_tensor(f"out_{i}", shape, _mybir.dt.float32, kind="ExternalOutput").ap()
            for i, shape in enumerate(_OUTS)]
    build(nc, args, outs)
    r = _run(nc, [arrays], core_ids=[0])
    return tuple(r.results[0][f"out_{i}"] for i in range(len(_OUTS)))
```
